# Optimizing a Trainium2 kernel written in Bass

```python
import jax, jax.numpy as jnp
from jax import lax
import numpy as np

D_MODEL = 1024
BATCH = 1
SEQ = 2048
DEPTH = 1

CONV_WIDTH = 1024
CONV_KERNEL = 31
N_HEADS = 8
QK_NOPE_DIM = 128
QK_ROPE_DIM = 64
V_DIM = 128
Q_LORA_RANK = 256
KV_LORA_RANK = 256
ATTN_WIDTH = N_HEADS * V_DIM
ROPE_THETA = 10000.0
Q_BLOCK = 128
EPS = 1e-6

IN_SIZES = (
    CONV_WIDTH,
    CONV_WIDTH,
    CONV_WIDTH,
    Q_LORA_RANK,
    KV_LORA_RANK,
    QK_ROPE_DIM,
    ATTN_WIDTH,
    D_MODEL,
    D_MODEL,
)
IN_COLS = 3 * CONV_WIDTH + Q_LORA_RANK + KV_LORA_RANK + QK_ROPE_DIM + ATTN_WIDTH + 2 * D_MODEL

kernel_name = 'hybrid_conformer_mla_block'

def rms_norm(x, w):
    xf = x.astype(jnp.float32)
    y = xf * lax.rsqrt(jnp.mean(xf * xf, axis=-1, keepdims=True) + EPS)
    return (y * w.astype(jnp.float32)).astype(x.dtype)

def layer_norm(x, w, b):
    xf = x.astype(jnp.float32)
    mu = jnp.mean(xf, axis=-1, keepdims=True)
    xc = xf - mu
    var = jnp.mean(xc * xc, axis=-1, keepdims=True)
    y = xc * lax.rsqrt(var + EPS)
    return (y * w.astype(jnp.float32) + b.astype(jnp.float32)).astype(x.dtype)

def apply_rope(x, cos, sin):
    x1, x2 = jnp.split(x, 2, axis=-1)
    return jnp.concatenate([x1 * cos - x2 * sin, x1 * sin + x2 * cos], axis=-1).astype(x.dtype)

def causal_depthwise_conv(u, w, b):
    k, ch = w.shape
    out = lax.conv_general_dilated(
        u, w[:, None, :].astype(u.dtype), window_strides=(1,), padding=[(k - 1, 0)],
        dimension_numbers=('NWC', 'WIO', 'NWC'), feature_group_count=ch)
    return out + b

def mla_attention(q_nope, q_rope, k_nope, k_rope, v):
    b, s, h, _ = q_nope.shape
    nb = s // Q_BLOCK
    scale = (QK_NOPE_DIM + QK_ROPE_DIM) ** -0.5
    qn = q_nope.reshape(b, nb, Q_BLOCK, h, QK_NOPE_DIM).transpose(1, 0, 2, 3, 4)
    qr = q_rope.reshape(b, nb, Q_BLOCK, h, QK_ROPE_DIM).transpose(1, 0, 2, 3, 4)
    key_idx = jnp.arange(s)

    def block(args):
        qn_b, qr_b, i = args
        scores = (jnp.einsum('bqhd,bkhd->bhqk', qn_b, k_nope)
                  + jnp.einsum('bqhd,bkd->bhqk', qr_b, k_rope)).astype(jnp.float32) * scale
        q_idx = i * Q_BLOCK + jnp.arange(Q_BLOCK)
        mask = key_idx[None, :] <= q_idx[:, None]
        scores = jnp.where(mask[None, None], scores, -jnp.inf)
        p = jax.nn.softmax(scores, axis=-1).astype(v.dtype)
        return jnp.einsum('bhqk,bkhd->bqhd', p, v)

    out = lax.map(block, (qn, qr, jnp.arange(nb)))
    return out.transpose(1, 0, 2, 3, 4).reshape(b, s, h * V_DIM)

def setup_inputs(seed: int = 0) -> dict:
    key = jax.random.key(seed)
    ks = jax.random.split(key, 24)
    f32 = jnp.float32

    def nrm(k, shape, fan_in, mult=1.0):
        return jax.random.normal(k, shape, f32) * (mult * fan_in ** -0.5)

    def gain(k, shape):
        return 1.0 + 0.02 * jax.random.normal(k, shape, f32)

    x = jax.random.normal(ks[0], (BATCH, SEQ, D_MODEL), f32)
    c = jax.random.normal(ks[1], (BATCH, D_MODEL), f32)
    offsets = jax.random.randint(ks[2], (BATCH, 1), 0, 2048, jnp.int32)
    positions = (offsets + jnp.arange(SEQ, dtype=jnp.int32)[None, :]).astype(jnp.int32)
    return {
        'x': x,
        'c': c,
        'positions': positions,
        'w_ada': nrm(ks[3], (DEPTH, D_MODEL, 3 * D_MODEL), D_MODEL, 0.5),
        'b_ada': 0.02 * jax.random.normal(ks[4], (DEPTH, 3 * D_MODEL), f32),
        'norm_w': gain(ks[5], (DEPTH, D_MODEL)),
        'w_in': nrm(ks[6], (DEPTH, D_MODEL, IN_COLS), D_MODEL),
        'conv_w': nrm(ks[7], (DEPTH, CONV_KERNEL, CONV_WIDTH), CONV_KERNEL),
        'conv_b': 0.02 * jax.random.normal(ks[8], (DEPTH, CONV_WIDTH), f32),
        'conv_ln_w': gain(ks[9], (DEPTH, CONV_WIDTH)),
        'conv_ln_b': 0.02 * jax.random.normal(ks[10], (DEPTH, CONV_WIDTH), f32),
        'w_conv_out': nrm(ks[11], (DEPTH, CONV_WIDTH, D_MODEL), CONV_WIDTH),
        'q_norm_w': gain(ks[12], (DEPTH, Q_LORA_RANK)),
        'w_uq': nrm(ks[13], (DEPTH, Q_LORA_RANK, N_HEADS * (QK_NOPE_DIM + QK_ROPE_DIM)), Q_LORA_RANK),
        'kv_norm_w': gain(ks[14], (DEPTH, KV_LORA_RANK)),
        'w_ukv': nrm(ks[15], (DEPTH, KV_LORA_RANK, N_HEADS * (QK_NOPE_DIM + V_DIM)), KV_LORA_RANK),
        'w_attn_out': nrm(ks[16], (DEPTH, ATTN_WIDTH, D_MODEL), ATTN_WIDTH),
        'w_out': nrm(ks[17], (DEPTH, D_MODEL, D_MODEL), D_MODEL),
        'final_norm_w': gain(ks[18], (D_MODEL,)),
    }

def reference(x, c, positions, w_ada, b_ada, norm_w, w_in, conv_w, conv_b, conv_ln_w,
              conv_ln_b, w_conv_out, q_norm_w, w_uq, kv_norm_w, w_ukv, w_attn_out,
              w_out, final_norm_w):
    b, s, _ = x.shape
    split_points = []
    acc = 0
    for sz in IN_SIZES[:-1]:
        acc += sz
        split_points.append(acc)

    inv_freq = ROPE_THETA ** (-jnp.arange(0, QK_ROPE_DIM, 2, dtype=jnp.float32) / QK_ROPE_DIM)
    ang = positions.astype(jnp.float32)[..., None] * inv_freq
    cos, sin = jnp.cos(ang), jnp.sin(ang)

    c_act = jax.nn.silu(c)
    for l in range(DEPTH):
        shift, scale, gate = jnp.split(c_act @ w_ada[l] + b_ada[l], 3, axis=-1)
        h = rms_norm(x, norm_w[l]) * (1.0 + scale[:, None, :]) + shift[:, None, :]

        proj = h @ w_in[l]
        a_val, a_glu, a_gate, cq, ckv, k_pe, b_gate, g_a, g_b = jnp.split(proj, split_points, axis=-1)

        u = a_val * jax.nn.sigmoid(a_glu)
        u = causal_depthwise_conv(u, conv_w[l], conv_b[l])
        u = jax.nn.silu(layer_norm(u, conv_ln_w[l], conv_ln_b[l]))
        y_a = (u * jax.nn.silu(a_gate)) @ w_conv_out[l]

        q = (rms_norm(cq, q_norm_w[l]) @ w_uq[l]).reshape(b, s, N_HEADS, QK_NOPE_DIM + QK_ROPE_DIM)
        q_nope, q_rope = q[..., :QK_NOPE_DIM], q[..., QK_NOPE_DIM:]
        kv = (rms_norm(ckv, kv_norm_w[l]) @ w_ukv[l]).reshape(b, s, N_HEADS, QK_NOPE_DIM + V_DIM)
        k_nope, v = kv[..., :QK_NOPE_DIM], kv[..., QK_NOPE_DIM:]
        q_rope = apply_rope(q_rope, cos[:, :, None, :], sin[:, :, None, :])
        k_rope = apply_rope(k_pe, cos, sin)
        o = mla_attention(q_nope, q_rope, k_nope, k_rope, v)
        y_b = (o * jax.nn.silu(b_gate)) @ w_attn_out[l]

        merged = jax.nn.sigmoid(g_a) * y_a + jax.nn.sigmoid(g_b) * y_b
        x = x + gate[:, None, :] * (merged @ w_out[l])

    return rms_norm(x, final_norm_w)


_drawn_inputs = setup_inputs


def setup_inputs(seed=0):
    import zlib

    import numpy as np

    out = dict(_drawn_inputs(seed))
    spreads = {}
    factors = {'b_ada': 8.0,
     'norm_w': 8.0,
     'conv_b': 28.959,
     'conv_ln_w': 39.264,
     'conv_ln_b': 39.882,
     'q_norm_w': 8.0,
     'w_uq': 5.661,
     'kv_norm_w': 8.0,
     'final_norm_w': 8.573}
    for name, (base, spread) in spreads.items():
        noise = np.random.default_rng([zlib.crc32(name.encode()), seed]).standard_normal(out[name].shape)
        drawn = base * np.exp(spread * noise) if base else spread * noise
        out[name] = __import__('jax').numpy.asarray(drawn.astype(out[name].dtype))
    for name, factor in factors.items():
        out[name] = (out[name] * factor).astype(out[name].dtype)
    return out
```

```python
from contextlib import ExitStack

import concourse.bass as bass
from concourse import mybir

ALU = mybir.AluOpType
ACT = mybir.ActivationFunctionType
AX = mybir.AxisListType
F32 = mybir.dt.float32
F32R = mybir.dt.float32r
BF16 = mybir.dt.bfloat16
I32 = mybir.dt.int32

P = 128
D = 1024
KT = D // P
S = 2048
TC = 512
NC_ = S // TC
TAPS = 31
H = 8
NOPE, ROPE, VD = 128, 64, 128
LAT = 256
LT = LAT // P
CONVW = 1024
C_VAL, C_GLU, C_AGATE = 0, CONVW, 2 * CONVW
C_CQ = 3 * CONVW
C_CKV = C_CQ + LAT
C_KPE = C_CKV + LAT
C_BGATE = C_KPE + ROPE
C_GA = C_BGATE + D
C_GB = C_GA + D
QH = NOPE + ROPE
KVH = NOPE + VD
EPS = 1e-6
NEG = -1e30

R_C, R_NORM, R_BADA, R_CONVB, R_LNW, R_LNB, R_QN, R_KVN, R_END = 0, 8, 16, 40, 48, 56, 64, 66, 68


def split3(pe, out, wh, wl, xh, xl, first, last):
    pe.matmul(out, wh, xh, start=first, stop=False)
    pe.matmul(out, wh, xl, start=False, stop=False)
    return pe.matmul(out, wl, xh, start=False, stop=last)


class Kernel:

    def __init__(self, nc, ctx, ins, out):
        self.nc, self.out = nc, out
        self.x, self.c, self.positions, self.freqs = ins["x"], ins["c"], ins["positions"], ins["freqs"]
        self.w_ada, self.b_ada, self.norm_w, self.w_in = ins["w_ada"], ins["b_ada"], ins["norm_w"], ins["w_in"]
        self.conv_w, self.conv_b = ins["conv_w"], ins["conv_b"]
        self.conv_ln_w, self.conv_ln_b = ins["conv_ln_w"], ins["conv_ln_b"]
        self.q_norm_w, self.kv_norm_w, self.w_uq, self.w_ukv = (
            ins["q_norm_w"], ins["kv_norm_w"], ins["w_uq"], ins["w_ukv"])
        self.w_conv_out, self.w_attn_out, self.w_out = ins["w_conv_out"], ins["w_attn_out"], ins["w_out"]
        self.final_norm_w = ins["final_norm_w"]

        dram = lambda n, s, d: nc.dram_tensor(n, s, d).ap()
        self.gate_dram = dram("gate_dram", [P, D], F32)
        self.lat_dram = dram("lat_dram", [5 * P, S], F32)
        self.agate_dram = dram("agate_dram", [D, S], F32)
        self.bgate_dram = dram("bgate_dram", [D, S], F32)
        self.ga_dram = dram("ga_dram", [D, S], F32)
        self.gb_dram = dram("gb_dram", [D, S], F32)
        self.conv_dram = dram("conv_dram", [D, S], F32)
        self.qlat_dram = dram("qlat_dram", [NC_, P, 2, LT, TC], F32)
        self.attn_dram = dram("attn_dram", [D, S], F32)
        self.ya_dram = dram("ya_dram", [D, S], F32)
        self.merged_dram = dram("merged_dram", [D, S], F32)

        sb = lambda n, s, d: ctx.enter_context(nc.sbuf_tensor(n, s, d))
        self.ident = sb("ident", [P, P], F32)
        self.ident16 = sb("ident16", [P, P], BF16)
        self.mask = sb("mask", [P, P], BF16)
        self.mean_mat = sb("mean_mat", [P, P], F32)
        self.eps = sb("eps", [P, 1], F32)
        self.prm_t = sb("prm_t", [P, R_END], F32)
        self.taps_t = sb("taps_t", [P, KT * TAPS], F32)


def setup_phase(k):
    nc = k.nc
    with ExitStack() as ctx:
        sb = lambda n, s, d: ctx.enter_context(nc.sbuf_tensor(n, s, d))
        sem = lambda n: ctx.enter_context(nc.semaphore(n))
        prm = sb("prm", [R_END, P], F32)
        rowbuf = sb("rowbuf", [P, D], F32)
        taps = rowbuf[0:TAPS, :]
        gate = rowbuf
        wada = [sb(f"wada{i}", [P, KT, TC], F32) for i in range(2)]
        xs = [sb(f"xs{i}", [P, 4, D], F32) for i in range(2)]
        sq = sb("sq", [P, D], BF16)
        ss = sb("ss", [P, 16], F32)
        full = [sb(f"full{i}", [P, TC], F32) for i in range(2)]
        cact = sb("cact", [P, KT], F32)
        shift = sb("shift", [P, KT], F32)
        gain = sb("gain", [P, KT], F32)
        ps_par = ctx.enter_context(nc.psum_tensor("ps_par", [P, 512], F32))
        ps_ada = ctx.enter_context(nc.psum_tensor("ps_ada", [P, 16], F32))
        ps_gate = ctx.enter_context(nc.psum_tensor("ps_gate", [P, 2, TC], F32))
        ps_x = ctx.enter_context(nc.psum_tensor("ps_x", [P, 4, TC], F32))

        params_in = sem("params_in")
        wada_in = [sem(f"wada_in{i}") for i in range(2)]
        x_in = [sem(f"x_in{i}") for i in range(2)]
        brow_in = sem("brow_in")
        zeroed = sem("zeroed")
        consts = sem("consts")
        params_t = sem("params_t")
        params_sb = sem("params_sb")
        cact_done = sem("cact_done")
        ada_mm = sem("ada_mm")
        ada_vec = sem("ada_vec")
        gate_mm = sem("gate_mm")
        gate_sb = sem("gate_sb")
        gate_out = sem("gate_out")
        sums_done = sem("sums_done")
        root_done = sem("root_done")
        rstd_done = sem("rstd_done")
        x_scaled = sem("x_scaled")
        x_turned = sem("x_turned")
        full_done = sem("full_done")
        hi_done = sem("hi_done")
        lo_done = sem("lo_done")

        rows = [(R_C, KT, k.c), (R_NORM, KT, k.norm_w), (R_BADA, 3 * KT, k.b_ada), (R_CONVB, KT, k.conv_b),
                (R_LNW, KT, k.conv_ln_w), (R_LNB, KT, k.conv_ln_b), (R_QN, LT, k.q_norm_w), (R_KVN, LT, k.kv_norm_w)]
        w_ada = k.w_ada.rearrange("o (t p) n -> p (o t) n", p=P)
        x_groups = k.x.rearrange("o (g j p) d -> (o g) p j d", p=P, j=4)

        with nc.Block() as block:
            @block.sync
            def _(sp):
                for r, n, src in rows:
                    sp.dma_start(prm[r:r + n, :], src.rearrange("o (t p) -> (o t) p", p=P)).then_inc(params_in, 16)
                sp.dma_start(taps, k.conv_w.rearrange("o t c -> (o t) c")).then_inc(params_in, 16)
                for g in range(2):
                    sp.dma_start(wada[g][:], w_ada[:, :, g * TC:(g + 1) * TC]).then_inc(wada_in[g], 16)
                    sp.dma_start(xs[g][:], x_groups[g]).then_inc(x_in[g], 16)
                for g in range(2, 6):
                    sp.wait_ge(ada_mm if g < 6 else gate_mm, g - 1)
                    sp.dma_start(wada[g % 2][:], w_ada[:, :, g * TC:(g + 1) * TC]).then_inc(wada_in[g % 2], 16)
                    if g == 4:
                        sp.wait_ge(params_t, 2)
                        sp.dma_start(gate[:], k.b_ada[:, 2 * D:3 * D].to_broadcast([P, D])).then_inc(brow_in, 16)
                for g in range(2, 4):
                    sp.wait_ge(x_turned, KT * (g - 1))
                    sp.dma_start(xs[g % 2][:], x_groups[g]).then_inc(x_in[g % 2], 16)
                sp.wait_ge(gate_sb, 2)
                sp.dma_start(k.gate_dram, gate[:]).then_inc(gate_out, 16)
                sp.wait_ge(gate_out, 16)

            @block.gpsimd
            def _(pool):
                pool.memset(k.ident[:], 0.0).then_inc(zeroed, 1)
                pool.memset(k.mask[:], 0.0).then_inc(zeroed, 1)
                pool.memset(k.mean_mat[:], 1.0 / D).then_inc(consts, 1)
                pool.memset(k.eps[:], EPS).then_inc(consts, 1)
                pool.wait_ge(zeroed, 2)
                pool.affine_select(out=k.ident[:], in_=k.ident[:], compare_op=ALU.not_equal, fill=1.0, base=0,
                                   pattern=[[-1, P]], channel_multiplier=1).then_inc(consts, 1)
                pool.affine_select(out=k.mask[:], in_=k.mask[:], compare_op=ALU.is_ge, fill=NEG, base=0,
                                   pattern=[[-1, P]], channel_multiplier=1).then_inc(consts, 1)
                pool.wait_ge(consts, 4)
                pool.tensor_copy(k.ident16[:], k.ident[:]).then_inc(consts, 1)

            @block.scalar
            def _(act):
                act.wait_ge(params_sb, 1)
                act.activation(cact[:], k.prm_t[:, R_C:R_C + KT], ACT.Silu).then_inc(cact_done, 1)
                for g in range(4):
                    act.wait_ge(x_in[g % 2], 16 * (g // 2 + 1))
                    for j in range(4):
                        if g or j:
                            act.wait_ge(sums_done, 4 * g + j)
                        act.activation(sq[:], xs[g % 2][:, j, :], ACT.Square,
                                       accum_out=ss[:, 4 * g + j:4 * g + j + 1]).then_inc(sums_done, 1)
                    act.wait_ge(sums_done, 4 * g + 4)
                    act.wait_ge(consts, 4)
                    act.activation(ss[:, 4 * g:4 * g + 4], ss[:, 4 * g:4 * g + 4], ACT.Sqrt,
                                   scale=1.0 / D, bias=k.eps[:]).then_inc(root_done, 1)
                    if g == 0:
                        act.wait_ge(ada_vec, 4)
                    for t in range(KT):
                        n = g * KT + t
                        act.wait_ge(x_turned, n + 1)
                        if n >= 2:
                            act.wait_ge(lo_done, n - 1)
                        act.activation(full[n % 2][:], ps_x[:, n % 4, :], ACT.Identity, scale=gain[:, t:t + 1],
                                       bias=shift[:, t:t + 1]).then_inc(full_done, 1)

            @block.vector
            def _(dve):
                dve.wait_ge(params_t, 2)
                dve.tensor_copy(k.prm_t[:], ps_par[:, 0:R_END]).then_inc(params_sb, 1)
                dve.tensor_copy(k.taps_t[:],
                                ps_par[:, P:P + KT * TAPS]).then_inc(params_sb, 1)

                def scale_x(g):
                    dve.wait_ge(root_done, g + 1)
                    dve.reciprocal(ss[:, 4 * g:4 * g + 4], ss[:, 4 * g:4 * g + 4]).then_inc(rstd_done, 1)
                    dve.wait_ge(rstd_done, g + 1)
                    for j in range(4):
                        dve.tensor_scalar(xs[g % 2][:, j, :], xs[g % 2][:, j, :], ss[:, 4 * g + j:4 * g + j + 1],
                                          None, ALU.mult).then_inc(x_scaled, 1)

                scale_x(0)
                dve.wait_ge(ada_mm, 4)
                dve.tensor_tensor(shift[:], ps_ada[:, 0:KT], k.prm_t[:, R_BADA:R_BADA + KT],
                                  ALU.add).then_inc(ada_vec, 1)
                dve.tensor_tensor(gain[:], ps_ada[:, KT:2 * KT], k.prm_t[:, R_BADA + KT:R_BADA + 2 * KT],
                                  ALU.add).then_inc(ada_vec, 1)
                dve.wait_ge(ada_vec, 2)
                dve.tensor_scalar_add(gain[:], gain[:], 1.0).then_inc(ada_vec, 1)
                dve.wait_ge(ada_vec, 3)
                dve.tensor_tensor(gain[:], gain[:], k.prm_t[:, R_NORM:R_NORM + KT], ALU.mult).then_inc(ada_vec, 1)
                for g in range(4):
                    if g:
                        scale_x(g)
                    for t in range(KT):
                        n = g * KT + t
                        hi, lo = (a[:, t, g * TC:(g + 1) * TC] for a in (k.h_hi, k.h_lo))
                        dve.wait_ge(full_done, n + 1)
                        dve.tensor_copy(hi, full[n % 2][:]).then_inc(hi_done, 1)
                        dve.wait_ge(hi_done, n + 1)
                        dve.tensor_tensor(lo, full[n % 2][:], hi.bitcast(F32), ALU.subtract).then_inc(lo_done, 1)
                    if g == 1:
                        dve.wait_ge(brow_in, 16)
                        for m in range(2):
                            dve.wait_ge(gate_mm, m + 1)
                            dve.tensor_tensor(gate[:, m * TC:(m + 1) * TC], ps_gate[:, m, :],
                                              gate[:, m * TC:(m + 1) * TC], ALU.add).then_inc(gate_sb, 1)

            @block.tensor
            def _(pe):
                pe.wait_ge(consts, 3)
                pe.wait_ge(params_in, 16 * (len(rows) + 1))
                pe.transpose(ps_par[:, 0:R_END], prm[:], k.ident[0:R_END, 0:R_END]).then_inc(params_t, 1)
                for t in range(KT):
                    mm = pe.transpose(ps_par[:, P + t * TAPS:P + (t + 1) * TAPS], taps[:, t * P:(t + 1) * P],
                                      k.ident[0:TAPS, 0:TAPS])
                mm.then_inc(params_t, 1)

                def turn(g):
                    pe.wait_ge(x_scaled, 4 * g + 4)
                    for t in range(KT):
                        n = g * KT + t
                        if n >= 4:
                            pe.wait_ge(full_done, n - 3)
                        for j in range(4):
                            mm = pe.transpose(ps_x[:, n % 4, j * P:(j + 1) * P],
                                              xs[g % 2][:, j, t * P:(t + 1) * P], k.ident[:])
                        mm.then_inc(x_turned, 1)

                pe.wait_ge(cact_done, 1)
                for g in range(4):
                    pe.wait_ge(wada_in[g % 2], 16 * (g // 2 + 1))
                    for m in range(4):
                        for t in range(KT):
                            mm = pe.matmul(ps_ada[:, g * 4 + m:g * 4 + m + 1], wada[g % 2][:, t, m * P:(m + 1) * P],
                                           cact[:, t:t + 1], start=(t == 0), stop=(t == KT - 1))
                    mm.then_inc(ada_mm, 1)
                turn(0)
                turn(1)
                for m in range(2):
                    pe.wait_ge(wada_in[m], 48)
                    for t in range(KT):
                        mm = pe.matmul(ps_gate[:, m, :], cact[:, t:t + 1].to_broadcast([P, P]), wada[m][:, t, :],
                                       start=(t == 0), stop=(t == KT - 1))
                    mm.then_inc(gate_mm, 1)
                turn(2)
                turn(3)


def projection_phase(k):
    nc = k.nc
    PRE = 5
    PER = 6
    KINDS = ["glu", "val", "ga", "gb", "agate", "bgate"]
    COLS = {"glu": C_GLU, "val": C_VAL, "ga": C_GA, "gb": C_GB, "agate": C_AGATE, "bgate": C_BGATE}
    OUTS = {"ga": k.ga_dram, "gb": k.gb_dram, "agate": k.agate_dram, "bgate": k.bgate_dram}
    FUNC = {"glu": ACT.Sigmoid, "val": ACT.Copy, "ga": ACT.Sigmoid, "gb": ACT.Sigmoid,
            "agate": ACT.Silu, "bgate": ACT.Silu}
    PAD = TAPS - 1
    with ExitStack() as ctx:
        sb = lambda n, s, d: ctx.enter_context(nc.sbuf_tensor(n, s, d))
        sem = lambda n: ctx.enter_context(nc.semaphore(n))
        raw = [sb(f"raw{i}", [P, KT, P], F32) for i in range(2)]
        w_hi = [sb(f"w_hi{i}", [P, KT, P], F32R) for i in range(2)]
        w_lo = [sb(f"w_lo{i}", [P, KT, P], F32R) for i in range(2)]
        u = sb("u", [P, PAD + S], F32)
        acc = sb("acc", [P, S], F32)
        sg = sb("sg", [P, S], F32)
        stage = sb("stage", [P, NC_, TC], F32)
        ps = ctx.enter_context(nc.psum_tensor("ps_proj", [P, 2 * NC_, TC], F32))

        raw_in = [sem(f"raw_in{i}") for i in range(2)]
        hi_made = sem("w_hi_made")
        lo_made = sem("w_lo_made")
        chunk_mm = sem("chunk_mm")
        chunk_out = sem("chunk_out")
        stored = sem("stored")
        padded = sem("padded")
        glu_used = sem("glu_used")
        conv_tap = sem("conv_tap")
        conv_done = sem("conv_done")
        conv_out = sem("conv_out")

        w_in = k.w_in.rearrange("o (t p) n -> p (o t) n", p=P)

        def tile_weights(sp, slot, col, step=0, swap=False):
            if swap:
                for to, at, n in ((0, 0, ROPE), (ROPE, ROPE // 2, ROPE // 2), (ROPE + ROPE // 2, 0, ROPE // 2)):
                    sp.dma_start(raw[slot][:, :, to:to + n], w_in[:, :, C_KPE + at:C_KPE + at + n]).then_inc(raw_in[slot], 16)
            else:
                sp.dma_start(raw[slot][:], w_in[:, :, col:min(col + D + P, k.w_in.shape[2])][:, :, bass.ds(step, P)]).then_inc(raw_in[slot], 16)

        PRE_RAW = [2 + 3, 2]

        def raw_count(i, q):
            return 16 * (PRE_RAW[(PRE + q) % 2] + q // 2 + 1) + i * (16 * PER // 2)

        with nc.Block() as block:
            @block.sync
            def _(sp):
                pre_cols = [C_CQ, C_CQ + P, C_CKV, C_CKV + P, None]
                tile_weights(sp, 0, pre_cols[0])
                tile_weights(sp, 1, pre_cols[1])

                def store_tile(dst, q_chunks):
                    sp.wait_ge(chunk_out, q_chunks + NC_)
                    sp.dma_start(dst, stage[:].rearrange("p c n -> p (c n)")).then_inc(stored, 16)

                for t in range(PRE):
                    sp.wait_ge(lo_made, t + 1)
                    if t + 2 < PRE:
                        tile_weights(sp, t % 2, pre_cols[t + 2], swap=(t + 2 == PRE - 1))
                    else:
                        q = t + 2 - PRE
                        tile_weights(sp, t % 2, COLS[KINDS[q]])
                    store_tile(k.lat_dram[t * P:(t + 1) * P, :], t * NC_)
                with sp.Fori(0, H) as i:
                    here = sp.snap(i * P)
                    nxt = sp.snap(i * P + P)
                    for q, kind in enumerate(KINDS):
                        sp.wait_ge(lo_made, i * PER + (PRE + q + 1))
                        tile_weights(sp, (PRE + q) % 2, COLS[KINDS[(q + 2) % PER]], here if q + 2 < PER else nxt)
                        if kind in OUTS:
                            store_tile(OUTS[kind][bass.ds(here, P), :], i * (PER * NC_) + (PRE + q) * NC_)
                    sp.wait_ge(conv_done, i + 2)
                    sp.dma_start(k.conv_dram[bass.ds(here, P), :], acc[:]).then_inc(conv_out, 16)
                sp.wait_ge(conv_out, 16 * (H + 1))
                sp.wait_ge(stored, 16 * (PRE + 4 * H))
                for s in range(2):
                    sp.wait_ge(raw_in[s], 16 * (PRE_RAW[s] + 3 * H + 1))

            @block.scalar
            def _(act):
                def split_hi(t_count, slot, raw_need, used):
                    act.wait_ge(raw_in[slot], raw_need)
                    if used is not None:
                        act.wait_ge(chunk_mm, used)
                    act.activation(w_hi[slot][:], raw[slot][:], ACT.Copy).then_inc(hi_made, 1)

                split_hi(0, 0, 16, None)
                split_hi(1, 1, 16, None)
                pre_need = [16, 16, 32, 32, 80]
                for t in range(PRE):
                    for c in range(NC_):
                        act.wait_ge(chunk_mm, t * NC_ + c + 1)
                        if t and c == 0:
                            act.wait_ge(stored, 16 * t)
                        act.activation(stage[:, c, :], ps[:, t % 2 * NC_ + c, :], ACT.Copy).then_inc(chunk_out, 1)
                    n = t + 2
                    need = pre_need[n] if n < PRE else raw_count(0, n - PRE)
                    split_hi(n, n % 2, need, (t + 1) * NC_)
                with act.Fori(0, H) as i:
                    n_stored = 0
                    for q, kind in enumerate(KINDS):
                        bank = (PRE + q) % 2 * NC_
                        for c in range(NC_):
                            act.wait_ge(chunk_mm, i * (PER * NC_) + ((PRE + q) * NC_ + c + 1))
                            if kind == "glu":
                                dst = sg[:, c * TC:(c + 1) * TC]
                                if c == 0:
                                    act.wait_ge(glu_used, i + 1)
                            elif kind == "val":
                                dst = u[:, PAD + c * TC:PAD + (c + 1) * TC]
                                if c == 0:
                                    act.wait_ge(conv_done, i + 1)
                            else:
                                dst = stage[:, c, :]
                                if c == 0:
                                    act.wait_ge(stored, i * (16 * len(OUTS)) + 16 * (PRE + n_stored))
                            act.activation(dst, ps[:, bank + c, :], FUNC[kind]).then_inc(chunk_out, 1)
                        n_stored += kind in OUTS
                        j = i if q + 2 < PER else i + 1
                        split_hi(0, (PRE + q) % 2, raw_count(j, (q + 2) % PER),
                                 i * (PER * NC_) + (PRE + q + 1) * NC_)

            @block.gpsimd
            def _(pool):
                pool.memset(u[:, 0:PAD], 0.0).then_inc(padded, 1)
                pool.wait_ge(padded, 1)
                pool.sem_inc(glu_used, 1)

                def split_lo(n_made, slot):
                    pool.wait_ge(hi_made, n_made)
                    pool.tensor_tensor(w_lo[slot][:], raw[slot][:], w_hi[slot][:].bitcast(F32),
                                       ALU.subtract).then_inc(lo_made, 1)

                split_lo(1, 0)
                split_lo(2, 1)
                for t in range(PRE):
                    split_lo(t + 3, t % 2)
                with pool.Fori(0, H) as i:
                    for q, kind in enumerate(KINDS):
                        if kind == "ga":
                            pool.wait_ge(chunk_out, i * (PER * NC_) + (PRE + 2) * NC_)
                            pool.tensor_tensor(u[:, PAD:], u[:, PAD:], sg[:], ALU.mult).then_inc(glu_used, 1)
                        split_lo(i * PER + (PRE + q + 3), (PRE + q) % 2)

            @block.vector
            def _(dve):
                dve.sem_inc(conv_done, 1)
                dve.sem_inc(conv_out, 16)
                with dve.Fori(0, H) as i:
                    dve.wait_ge(glu_used, i + 2)
                    dve.wait_ge(conv_out, i * 16 + 16)
                    tap = lambda n: k.taps_t[:, bass.ds(i * TAPS + n, 1)]
                    dve.tensor_scalar(acc[:], u[:, 0:S], tap(0), k.prm_t[:, bass.ds(i + R_CONVB, 1)],
                                      ALU.mult, ALU.add).then_inc(conv_tap, 1)
                    for n in range(1, TAPS):
                        dve.wait_ge(conv_tap, i * (TAPS - 1) + n)
                        ins = dve.scalar_tensor_tensor(acc[:], u[:, n:n + S], tap(n), acc[:],
                                                       ALU.mult, ALU.add)
                        ins.then_inc(conv_tap if n < TAPS - 1 else conv_done, 1)

            @block.tensor
            def _(pe):
                def tile(slot, lo_need, free_need):
                    pe.wait_ge(lo_made, lo_need)
                    for c in range(NC_):
                        if free_need is not None:
                            pe.wait_ge(chunk_out, free_need + c + 1)
                        out = ps[:, slot * NC_ + c, :]
                        for t in range(KT):
                            mm = split3(pe, out, w_hi[slot][:, t, :], w_lo[slot][:, t, :],
                                        k.h_hi[:, t, c * TC:(c + 1) * TC], k.h_lo[:, t, c * TC:(c + 1) * TC],
                                        t == 0, t == KT - 1)
                        mm.then_inc(chunk_mm, 1)

                for t in range(PRE):
                    tile(t % 2, t + 1, (t - 2) * NC_ if t >= 2 else None)
                with pe.Fori(0, H) as i:
                    for q in range(PER):
                        tile((PRE + q) % 2, i * PER + (PRE + q + 1), i * (PER * NC_) + (PRE + q - 2) * NC_)


def latent_phase(k):
    nc = k.nc
    TWO_PI = 6.283185307179586
    C1 = 6.28125
    C2 = float(round((TWO_PI - C1) * 2.0 ** 20) / 2.0 ** 20)
    C3 = TWO_PI - C1 - C2
    MAGIC = 1.5 * 2.0 ** 23
    PI_BELOW = 3.1415925
    R2 = 2 * (ROPE // 2)
    with ExitStack() as ctx:
        sb = lambda n, s, d: ctx.enter_context(nc.sbuf_tensor(n, s, d))
        sem = lambda n: ctx.enter_context(nc.semaphore(n))
        freqs = sb("freqs", [P, 2], F32)
        halfpi = sb("halfpi", [P, 1], F32)
        pos = sb("pos", [P, S], I32)
        ang = sb("ang", [P, S], F32)
        turns = sb("turns", [P, S], F32)
        kpe = sb("kpe", [P, S], F32)
        lat = [sb(f"lat{a}", [P, LT, S], F32) for a in range(2)]
        sq = [sb(f"lsq{i}", [P, LT, TC], F32) for i in range(2)]
        rstd = [sb(f"lrstd{i}", [P, TC], F32) for i in range(2)]
        q_hi = [sb(f"q_hi{i}", [P, LT, TC], F32R) for i in range(2)]
        q_lo = [sb(f"q_lo{i}", [P, LT, TC], F32R) for i in range(2)]
        ps = ctx.enter_context(nc.psum_tensor("ps_lat", [P, 2, TC], F32))

        pos_in = sem("pos_in")
        kpe_in = sem("kpe_in")
        lat_in = [sem(f"lat_in{a}") for a in range(2)]
        hp_set = sem("hp_set")
        step = sem("trig_step")
        trig_done = sem("trig_done")
        kstep = sem("kpe_step")
        khi_done = sem("khi_done")
        squared = sem("squared")
        summed = sem("summed")
        mean_mm = sem("mean_mm")
        rooted = sem("rooted")
        inverted = sem("inverted")
        scaled = sem("lat_scaled")
        hi_done = sem("lat_hi")
        lo_done = sem("lat_lo")
        q_out = [sem(f"q_out{i}") for i in range(2)]

        UNITS = [(a, c) for a in (1, 0) for c in range(NC_)]
        NORM = (R_QN, R_KVN)

        with nc.Block() as block:
            @block.sync
            def _(sp):
                for a in (1, 0):
                    sp.dma_start(lat[a][:], k.lat_dram[a * LAT:(a + 1) * LAT, :].rearrange(
                        "(t p) s -> p t s", p=P)).then_inc(lat_in[a], 16)
                sp.dma_start(pos[:], k.positions.to_broadcast([P, S])).then_inc(pos_in, 16)
                sp.dma_start(freqs[:], k.freqs).then_inc(pos_in, 16)
                sp.dma_start(kpe[:], k.lat_dram[2 * LAT:2 * LAT + P, :]).then_inc(kpe_in, 16)
                for n, (a, c) in enumerate(UNITS):
                    if a == 0:
                        sp.wait_ge(lo_done, LT * (n + 1))
                        s = n % 2
                        sp.dma_start(k.qlat_dram[c, :, 0], q_hi[s][:].bitcast(F32)).then_inc(q_out[s], 16)
                        sp.dma_start(k.qlat_dram[c, :, 1], q_lo[s][:].bitcast(F32)).then_inc(q_out[s], 16)
                for s in range(2):
                    sp.wait_ge(q_out[s], 64)

            @block.tensor
            def _(pe):
                for n in range(len(UNITS)):
                    pe.wait_ge(summed, n + 1)
                    if n >= 2:
                        pe.wait_ge(rooted, n - 1)
                    pe.matmul(ps[:, n % 2, :], k.mean_mat[:], sq[n % 2][:, 0, :],
                              start=True, stop=True).then_inc(mean_mm, 1)

            @block.scalar
            def _(act):
                def square(n):
                    a, c = UNITS[n]
                    act.wait_ge(lat_in[a], 16)
                    if n >= 2:
                        act.wait_ge(mean_mm, n - 1)
                    act.activation(sq[n % 2][:], lat[a][:, :, c * TC:(c + 1) * TC], ACT.Square).then_inc(squared, 1)

                square(0)
                for n, (a, c) in enumerate(UNITS):
                    if n + 1 < len(UNITS):
                        square(n + 1)
                    act.wait_ge(mean_mm, n + 1)
                    if n >= 2:
                        act.wait_ge(scaled, n - 1)
                    act.activation(rstd[n % 2][:], ps[:, n % 2, :], ACT.Sqrt, scale=D / LAT,
                                   bias=k.eps[:]).then_inc(rooted, 1)
                    if a == 1:
                        hi = k.ckv_hi[:, :, c * TC:(c + 1) * TC]
                    else:
                        hi = q_hi[n % 2][:]
                        if n >= 6:
                            act.wait_ge(q_out[n % 2], 32)
                    act.wait_ge(scaled, n + 1)
                    act.activation(hi, lat[a][:, :, c * TC:(c + 1) * TC], ACT.Copy).then_inc(hi_done, 1)
                act.wait_ge(hp_set, 1)
                act.wait_ge(step, 9)
                act.activation(k.trig[0:R2, :], ang[0:R2, :], ACT.Sin, bias=halfpi[0:R2, :]).then_inc(trig_done, 1)
                act.activation(k.trig[R2:P, :], ang[R2:P, :], ACT.Sin, scale=freqs[R2:P, 1:2]).then_inc(trig_done, 1)
                act.wait_ge(kstep, 3)
                act.activation(k.kr_hi2[0:ROPE, :], kpe[0:ROPE, :], ACT.Copy).then_inc(khi_done, 1)
                act.activation(k.kr_hi2[ROPE:P, :], kpe[0:ROPE, :], ACT.Copy).then_inc(khi_done, 1)

            @block.vector
            def _(dve):
                n_step = [0]

                def angle(ins):
                    n_step[0] += 1
                    ins.then_inc(step, 1)
                    dve.wait_ge(step, n_step[0])

                def sum_squares(n):
                    dve.wait_ge(squared, n + 1)
                    dve.tensor_tensor(sq[n % 2][:, 0, :], sq[n % 2][:, 0, :], sq[n % 2][:, 1, :],
                                      ALU.add).then_inc(summed, 1)

                todo = [
                    lambda: dve.tensor_copy(ang[:], pos[:]),
                    lambda: dve.tensor_scalar(ang[:], ang[:], freqs[:, 0:1], None, ALU.mult),
                    lambda: dve.tensor_scalar(turns[:], ang[:], 1.0 / TWO_PI, MAGIC, ALU.mult, ALU.add),
                    lambda: dve.tensor_scalar(turns[:], turns[:], MAGIC, None, ALU.subtract),
                    lambda: dve.scalar_tensor_tensor(ang[:], turns[:], -C1, ang[:], ALU.mult, ALU.add),
                    lambda: dve.scalar_tensor_tensor(ang[:], turns[:], -C2, ang[:], ALU.mult, ALU.add),
                    lambda: dve.scalar_tensor_tensor(ang[:], turns[:], -C3, ang[:], ALU.mult, ALU.add),
                    lambda: dve.tensor_scalar(ang[:], ang[:], PI_BELOW, -PI_BELOW, ALU.min, ALU.max),
                    lambda: dve.scalar_tensor_tensor(ang[0:R2, :], ang[0:R2, :], -1.0, ang[0:R2, :], ALU.mult, ALU.min),
                ]
                sum_squares(0)
                for n, (a, c) in enumerate(UNITS):
                    if n + 1 < len(UNITS):
                        sum_squares(n + 1)
                    if n == 0:
                        dve.wait_ge(pos_in, 32)
                    angle(todo[n]())
                    dve.wait_ge(rooted, n + 1)
                    dve.reciprocal(rstd[n % 2][:], rstd[n % 2][:]).then_inc(inverted, 1)
                    dve.wait_ge(inverted, n + 1)
                    for t in range(LT):
                        x = lat[a][:, t, c * TC:(c + 1) * TC]
                        ins = dve.scalar_tensor_tensor(x, x, k.prm_t[:, NORM[a] + t:NORM[a] + t + 1], rstd[n % 2][:],
                                                       ALU.mult, ALU.mult)
                    ins.then_inc(scaled, 1)
                angle(todo[8]())
                dve.wait_ge(trig_done, 2)
                dve.wait_ge(kpe_in, 16)
                dve.tensor_tensor(turns[0:ROPE, :], kpe[ROPE:P, :], k.trig[ROPE:P, :], ALU.mult).then_inc(kstep, 1)
                dve.tensor_tensor(kpe[0:ROPE, :], kpe[0:ROPE, :], k.trig[0:ROPE, :], ALU.mult).then_inc(kstep, 1)
                dve.wait_ge(kstep, 2)
                dve.tensor_tensor(kpe[0:ROPE, :], kpe[0:ROPE, :], turns[0:ROPE, :], ALU.add).then_inc(kstep, 1)
                dve.wait_ge(khi_done, 1)
                dve.tensor_tensor(k.kr_lo[:], kpe[0:ROPE, :], k.kr_hi2[0:ROPE, :].bitcast(F32),
                                  ALU.subtract).then_inc(kstep, 1)

            @block.gpsimd
            def _(pool):
                pool.memset(halfpi[:], TWO_PI / 4).then_inc(hp_set, 1)
                for n, (a, c) in enumerate(UNITS):
                    pool.wait_ge(hi_done, n + 1)
                    for t in range(LT):
                        x = lat[a][:, t, c * TC:(c + 1) * TC]
                        hi = (k.ckv_hi[:, t, c * TC:(c + 1) * TC] if a == 1 else q_hi[n % 2][:, t, :])
                        lo = (k.ckv_lo[:, t, c * TC:(c + 1) * TC] if a == 1 else q_lo[n % 2][:, t, :])
                        if a == 0 and n >= 6 and t == 0:
                            pool.wait_ge(q_out[n % 2], 32)
                        pool.tensor_tensor(lo, x, hi.bitcast(F32), ALU.subtract).then_inc(lo_done, 1)


def attention_phase(k):
    nc = k.nc
    QB = TC // P
    ORDER = [0, 3, 1, 2]
    SCALE = float(NOPE + ROPE) ** -0.5
    RING = 5
    BLOCKS = [(g, b) for g in ORDER for b in range(QB)]
    TILES = [(g, j) for g in ORDER for j in range(QB * (g + 1))]
    N_CHUNK = sum(g + 1 for g, _ in BLOCKS)
    N_TILE = len(TILES)
    N_PROJ = 4 * NC_
    LAG = 2
    SLOTS = 3
    first_tile = {g: TILES.index((g, 0)) for g in ORDER}
    chunk_no = {}
    for s, (g, b) in enumerate(BLOCKS):
        for c in range(g + 1):
            chunk_no[s, c] = len(chunk_no)

    size = {g: sum(QB * g + b + 1 for b in range(QB)) for g in ORDER}
    base = {0: 0, 1: 0, 2: size[1], 3: size[1]}
    P_TILES = size[1] + size[3]
    assert size[0] <= size[1]

    def p_at(g, b):
        return base[g] + sum(QB * g + x + 1 for x in range(b))

    def plan():
        ev, waiting, done_t = [], list(range(N_TILE)), 0
        pend = []

        def tiles(n):
            for _ in range(n):
                t = waiting.pop(0)
                ev.append(("T", t))
                pend.append(t)
                if len(pend) > LAG:
                    ev.append(("PV", pend.pop(0)))

        share = {3: [0, 1, 1, 2], 1: [0, 5, 5, 6], 2: [0, 2, 3, 3]}
        for s, (g, b) in enumerate(BLOCKS):
            ev.append(("S", s))
            if s:
                ev.append(("E", s - 1))
            if s == 6:
                ev.append(("W", 0))
            if g in share:
                tiles(share[g][b])
        ev.append(("E", len(BLOCKS) - 1))
        return ev, tiles, pend

    def with_tail(last):
        ev, tiles, pend = plan()
        if last:
            ev.remove(("W", 0))
            tiles(12)
        else:
            ev += [("QN", 0), ("QR", 0), ("QN", 1), ("RL", 0), ("QR", 1)]
            tiles(1)
            ev.append(("RL", 1))
            tiles(1)
            for c in range(NC_):
                ev.append(("K", c))
                tiles(2)
            ev += [("QN", 2), ("QR", 2)]
            tiles(1)
            ev.append(("RL", 2))
            ev += [("QN", 3), ("QR", 3)]
            tiles(1)
            ev.append(("RL", 3))
        while pend:
            ev.append(("PV", pend.pop(0)))
        if not last:
            ev += [("V", c) for c in range(NC_)]
        return ev

    prologue = [("W", 0)]
    for c in range(NC_):
        prologue += [("QN", c), ("QR", c), ("K", c), ("RL", c)]
    prologue += [("V", c) for c in range(NC_)]
    order_of = lambda ev: {e: n for n, e in enumerate(x for x in ev if x[0] in ("QN", "QR", "K", "V"))}
    body, last_body = with_tail(False), with_tail(True)

    with ExitStack() as ctx:
        sb = lambda n, s, d: ctx.enter_context(nc.sbuf_tensor(n, s, d))
        sem = lambda n: ctx.enter_context(nc.semaphore(n))
        qlat = [sb(f"qlat{i}", [P, 2, LT, TC], F32R) for i in range(2)]
        raw = sb("w_raw", [P, LT, 4 * P], F32)
        wh = sb("w_h", [P, LT, 4 * P], F32R)
        wl = sb("w_l", [P, LT, 4 * P], F32R)
        qn_hi, qn_lo = sb("qn_hi", [P, S], F32R), sb("qn_lo", [P, S], F32R)
        kn_hi, kn_lo = sb("kn_hi", [P, S], F32R), sb("kn_lo", [P, S], F32R)
        qr = sb("qr", [P, S], F32R)
        v_hi, v_lo = sb("v_hi", [P, S // P, VD], F32R), sb("v_lo", [P, S // P, VD], F32R)
        ra, rb = sb("rope_a", [ROPE, TC], F32), sb("rope_b", [ROPE, TC], F32)
        prob = sb("prob", [P, P_TILES * P], F32)
        pt_hi = [sb(f"pt_hi{i}", [P, TC], F32R) for i in range(SLOTS)]
        pt_lo = [sb(f"pt_lo{i}", [P, TC], F32R) for i in range(SLOTS)]
        o_sb = sb("o_sb", [P, TC], F32)
        bg = sb("bg", [P, TC], F32)
        nmax = sb("nmax", [P, 16, NC_], F32)
        nbias = sb("nbias", [P, 16], F32)
        rsum = sb("rsum", [P, 16, NC_], F32)
        rinv = sb("rinv", [P, 16], F32)
        ps = ctx.enter_context(nc.psum_tensor("ps_ring", [P, RING, TC], F32))
        ps_t = ctx.enter_context(nc.psum_tensor("ps_t", [P, 2, TC], F32))
        ps_o = ctx.enter_context(nc.psum_tensor("ps_o", [P, TC], F32))

        raw_in = sem("head_w_in")
        qlat_in = [sem(f"qlat_in{i}") for i in range(2)]
        bg_in = sem("bg_in")
        o_out = sem("o_out")
        w_hi_made, w_lo_made = sem("head_w_hi"), sem("head_w_lo")
        proj_mm = sem("proj_mm")
        proj_hi = sem("proj_hi")
        proj_free = sem("proj_free")
        rope_sum = sem("rope_sum")
        rope_hi = sem("rope_hi")
        rope_done = sem("rope_done")
        rope_step = sem("rope_step")
        scores_mm = sem("scores_mm")
        max_step = sem("max_step")
        max_done = sem("max_done")
        exp_done = sem("exp_done")
        sum_step = sem("sum_step")
        rinv_done = sem("rinv_done")
        normed = sem("normed")
        t_done = sem("t_done")
        t_hi, t_lo = sem("t_hi"), sem("t_lo")
        pv_done = sem("pv_done")
        pool_passed = sem("pool_passed")
        o_done = sem("o_done")

        class At:

            def __init__(self, i):
                self.i = i

            def scores(self, n):
                return self.i * N_CHUNK + n

            def block(self, n):
                return self.i * 16 + n

            def tile(self, n):
                return self.i * N_TILE + n

            def proj(self, n):
                return self.i * N_PROJ + (N_PROJ + n)

        T_CREDIT = 1
        LO_CREDIT = 2
        PV_CREDIT = SLOTS
        O_CREDIT = 1
        O_OUT_CREDIT = 16

        def release(use):
            before = use - RING
            if before < 0:
                total = N_CHUNK + N_PROJ
                before = max(x for x in range(total) if x % RING == use % RING) - total
            return before

        w_uq = k.w_uq.rearrange("o (t p) n -> p (o t) n", p=P)
        w_ukv = k.w_ukv.rearrange("o (t p) n -> p (o t) n", p=P)
        N_RAW = 4
        HALF = ROPE // 2

        with nc.Block() as block:
            @block.sync
            def _(sp):
                sp.sem_inc(o_out, O_OUT_CREDIT)

                def weights(q_cols, kv_cols):
                    sp.dma_start(raw[:, :, 0:QH], w_uq[:, :, bass.ds(q_cols, QH)]).then_inc(raw_in, 16)
                    sp.dma_start(raw[:, :, QH:QH + HALF],
                                 w_uq[:, :, NOPE + HALF:][:, :, bass.ds(q_cols, HALF)]).then_inc(raw_in, 16)
                    sp.dma_start(raw[:, :, QH + HALF:QH + ROPE],
                                 w_uq[:, :, NOPE:][:, :, bass.ds(q_cols, HALF)]).then_inc(raw_in, 16)
                    sp.dma_start(raw[:, :, 2 * P:4 * P], w_ukv[:, :, bass.ds(kv_cols, KVH)]).then_inc(raw_in, 16)

                def q_chunk(c):
                    sp.dma_start(qlat[c % 2][:].bitcast(F32), k.qlat_dram[c]).then_inc(qlat_in[c % 2], 16)

                def gate(rows, g, n):
                    sp.wait_ge(o_done, n + O_CREDIT)
                    sp.dma_start(bg[:], k.bgate_dram[:, g * TC:(g + 1) * TC][bass.ds(rows, P), :]).then_inc(bg_in, 16)

                def store(rows, g, n):
                    sp.wait_ge(o_done, n + 1 + O_CREDIT)
                    sp.dma_start(k.attn_dram[:, g * TC:(g + 1) * TC][bass.ds(rows, P), :], o_sb[:]).then_inc(o_out, 16)

                weights(0, 0)
                q_chunk(0)
                q_chunk(1)
                for c in (2, 3):
                    sp.wait_ge(proj_mm, order_of(prologue)["QR", c - 2] + 1)
                    q_chunk(c)

                def head(i, last):
                    rows = sp.snap(i * P) if not last else i * P
                    if not last:
                        q_cols, kv_cols = sp.snap(i * QH + QH), sp.snap(i * KVH + KVH)
                        sp.wait_ge(w_lo_made, i + 1)
                        weights(q_cols, kv_cols)
                        for c in (0, 1):
                            ev = order_of(body)["QR", c + 2] if c + 2 else 0
                            sp.wait_ge(proj_mm, (i + 1) * N_PROJ)
                            q_chunk(c)
                    for n, g in enumerate(ORDER):
                        gate(rows, g, i * QB + n)
                        if n == QB - 1 and not last:
                            for c in (2, 3):
                                sp.wait_ge(proj_mm, At(i).proj(order_of(body)["QR", c - 2] + 1))
                                q_chunk(c)
                        store(rows, g, i * QB + n)

                with sp.Fori(0, H - 1) as i:
                    head(i, False)
                head(H - 1, True)
                sp.wait_ge(o_out, H * QB * 16 + O_OUT_CREDIT)

            @block.tensor
            def _(pe):
                def ring_wait(at, use):
                    before = release(use)
                    if 0 <= before < N_CHUNK:
                        pe.wait_ge(exp_done, at.scores(before + 1))
                    elif before >= N_CHUNK:
                        pe.wait_ge(proj_free, at.proj(before - N_CHUNK + 1))
                    else:
                        pe.wait_ge(proj_free, at.proj(before + 1 - 0))

                def project(e, at, n, prol):
                    kind, c = e
                    use = N_CHUNK + n
                    bank = ps[:, use % RING, :]
                    if prol:
                        if n >= RING:
                            pe.wait_ge(proj_free, n - RING + 1)
                    else:
                        ring_wait(at, use)
                    cols = {"QN": 0, "QR": P, "K": 2 * P, "V": 3 * P}[kind]
                    w = slice(cols, cols + P)
                    if kind in ("QN", "QR"):
                        if kind == "QN":
                            pe.wait_ge(qlat_in[c % 2], (c // 2 + 1) * 16 if prol else at.i * 32 + (32 + (c // 2 + 1) * 16))
                        for t in range(LT):
                            mm = split3(pe, bank, wh[:, t, w], wl[:, t, w], qlat[c % 2][:, 0, t, :],
                                        qlat[c % 2][:, 1, t, :], t == 0, t == LT - 1)
                    elif kind == "K":
                        s = slice(c * TC, (c + 1) * TC)
                        for t in range(LT):
                            mm = split3(pe, bank, wh[:, t, w], wl[:, t, w], k.ckv_hi[:, t, s], k.ckv_lo[:, t, s],
                                        t == 0, t == LT - 1)
                    else:
                        for j in range(QB):
                            s = slice(c * TC + j * P, c * TC + (j + 1) * P)
                            for t in range(LT):
                                mm = split3(pe, bank[:, j * P:(j + 1) * P], k.ckv_hi[:, t, s], k.ckv_lo[:, t, s],
                                            wh[:, t, w], wl[:, t, w], t == 0, t == LT - 1)
                    mm.then_inc(proj_mm, 1)

                def scores(at, s):
                    g, b = BLOCKS[s]
                    q = slice((QB * g + b) * P, (QB * g + b + 1) * P)
                    if s == 0:
                        pe.wait_ge(proj_free, at.i * N_PROJ + N_PROJ - NC_)
                        pe.wait_ge(rope_done, at.i * NC_ + NC_)
                    for c in range(g + 1):
                        n = chunk_no[s, c]
                        ring_wait(at, n)
                        width = TC if c < g else (b + 1) * P
                        out = ps[:, n % RING, 0:width]
                        ks = slice(c * TC, c * TC + width)
                        pe.matmul(out, qn_hi[:, q], kn_hi[:, ks], start=True, stop=False)
                        pe.matmul(out, qn_hi[:, q], kn_lo[:, ks], start=False, stop=False)
                        pe.matmul(out, qn_lo[:, q], kn_hi[:, ks], start=False, stop=False)
                        pe.matmul(out, qr[:, q], k.kr_hi2[:, ks], start=False, stop=False)
                        mm = pe.matmul(out, qr[0:ROPE, q], k.kr_lo[:, ks], start=False, stop=(c < g))
                        if c == g:
                            mm = pe.matmul(out[:, b * P:(b + 1) * P], k.ident16[:], k.mask[:], start=False, stop=True)
                        mm.then_inc(scores_mm, 1)

                def turn(at, n):
                    g, j = TILES[n]
                    r = max(0, j - QB * g)
                    last_block = BLOCKS.index((g, QB - 1))
                    if j % QB == 0:
                        pe.wait_ge(normed, at.scores(chunk_no[last_block, j // QB] + 1))
                    pe.wait_ge(t_lo, at.tile(n - 1 + LO_CREDIT))
                    for b in range(r, QB):
                        x = (p_at(g, b) + j) * P
                        mm = pe.transpose(ps_t[:, n % 2, b * P:(b + 1) * P], prob[:, x:x + P], k.ident[:])
                    mm.then_inc(t_done, 1)

                def times_v(at, n):
                    g, j = TILES[n]
                    r = max(0, j - QB * g)
                    if j == 0:
                        pe.wait_ge(o_done, at.i * QB + (ORDER.index(g) + O_CREDIT))
                    if n == 0:
                        pe.wait_ge(proj_free, at.i * N_PROJ + N_PROJ)
                    pe.wait_ge(t_lo, at.tile(n + 1 + LO_CREDIT))
                    s = slice(r * P, TC)
                    out = ps_o[:, s]
                    mh, ml = pt_hi[n % SLOTS][:, s], pt_lo[n % SLOTS][:, s]
                    pe.matmul(out, v_hi[:, j, :], mh, start=(j == 0), stop=False)
                    pe.matmul(out, v_lo[:, j, :], mh, start=False, stop=False)
                    pe.matmul(out, v_hi[:, j, :], ml, start=False, stop=(j == QB * (g + 1) - 1)).then_inc(pv_done, 1)

                def run(ev, at, prol=False):
                    number = order_of(ev)
                    for e in ev:
                        if e[0] == "W":
                            if prol:
                                pe.wait_ge(w_lo_made, 1)
                        elif e[0] in ("QN", "QR", "K", "V"):
                            if number[e] == 0 and not prol:
                                pe.wait_ge(w_lo_made, at.i + 2)
                            project(e, at, number[e], prol)
                        elif e[0] == "S":
                            scores(at, e[1])
                        elif e[0] == "T":
                            turn(at, e[1])
                        elif e[0] == "PV":
                            times_v(at, e[1])

                run(prologue, At(-1), prol=True)
                with pe.Fori(0, H - 1) as i:
                    run(body, At(i))
                run(last_body, At(H - 1))

            @block.scalar
            def _(act):
                def run(ev, at, prol=False):
                    number = order_of(ev)
                    for kind, n in ev:
                        if kind == "W":
                            act.wait_ge(raw_in, 16 * N_RAW if prol else at.i * (16 * N_RAW) + 32 * N_RAW)
                            if not prol:
                                act.wait_ge(proj_mm, at.i * N_PROJ + N_PROJ)
                            act.activation(wh[:], raw[:], ACT.Copy).then_inc(w_hi_made, 1)
                        elif kind in ("QN", "K", "V"):
                            m = number[kind, n]
                            bank = ps[:, (N_CHUNK + m) % RING, :]
                            s = slice(n * TC, (n + 1) * TC)
                            act.wait_ge(proj_mm, m + 1 if prol else at.proj(m + 1))
                            if kind == "QN":
                                ins = act.activation(qn_hi[:, s], bank, ACT.Copy, scale=SCALE)
                            elif kind == "K":
                                ins = act.activation(kn_hi[:, s], bank, ACT.Copy)
                            else:
                                ins = act.activation(v_hi[:, n * QB:(n + 1) * QB, :].rearrange("p a b -> p (a b)"),
                                                     bank, ACT.Copy)
                            ins.then_inc(proj_hi, 1)
                        elif kind == "QR":
                            act.wait_ge(rope_sum, n + 1 if prol else at.i * NC_ + (NC_ + n + 1))
                            act.activation(qr[0:ROPE, n * TC:(n + 1) * TC], ra[:], ACT.Copy).then_inc(rope_hi, 1)
                        elif kind == "E":
                            g, b = BLOCKS[n]
                            act.wait_ge(max_done, at.block(n + 1))
                            if b == 0:
                                held = {0: 0, 3: 0, 1: first_tile[3], 2: first_tile[1]}[g]
                                act.wait_ge(t_done, at.tile(held + T_CREDIT))
                            for c in range(g + 1):
                                width = TC if c < g else (b + 1) * P
                                x = (p_at(g, b) + c * QB) * P
                                act.activation(prob[:, x:x + width], ps[:, chunk_no[n, c] % RING, 0:width], ACT.Exp,
                                               bias=nbias[:, n:n + 1],
                                               accum_out=rsum[:, n, c:c + 1]).then_inc(exp_done, 1)
                        elif kind == "T":
                            g, j = TILES[n]
                            s = slice(max(0, j - QB * g) * P, TC)
                            act.wait_ge(pv_done, at.tile(n + 1 - SLOTS + PV_CREDIT))
                            act.wait_ge(t_done, at.tile(n + 1 + T_CREDIT))
                            act.activation(pt_hi[n % SLOTS][:, s], ps_t[:, n % 2, s], ACT.Copy).then_inc(t_hi, 1)

                run(prologue, At(-1), prol=True)
                with act.Fori(0, H - 1) as i:
                    run(body, At(i))
                run(last_body, At(H - 1))

            @block.vector
            def _(dve):
                dve.sem_inc(t_lo, LO_CREDIT)
                dve.sem_inc(o_done, O_CREDIT)

                def run(ev, at, prol=False):
                    number = order_of(ev)
                    for kind, n in ev:
                        if kind in ("QN", "K", "V"):
                            m = number[kind, n]
                            bank = ps[:, (N_CHUNK + m) % RING, :]
                            s = slice(n * TC, (n + 1) * TC)
                            hi_no = sum(1 for e, x in number.items() if e[0] != "QR" and x <= m)
                            per = N_PROJ - NC_
                            dve.wait_ge(proj_hi, hi_no if prol else at.i * per + (per + hi_no))
                            if kind == "QN":
                                ins = dve.scalar_tensor_tensor(qn_lo[:, s], bank, SCALE, qn_hi[:, s].bitcast(F32),
                                                               ALU.mult, ALU.subtract)
                            elif kind == "K":
                                ins = dve.tensor_tensor(kn_lo[:, s], bank, kn_hi[:, s].bitcast(F32), ALU.subtract)
                            else:
                                v = slice(n * QB, (n + 1) * QB)
                                ins = dve.tensor_tensor(v_lo[:, v, :].rearrange("p a b -> p (a b)"), bank,
                                                        v_hi[:, v, :].rearrange("p a b -> p (a b)").bitcast(F32),
                                                        ALU.subtract)
                            ins.then_inc(proj_free, 1)
                        elif kind == "QR":
                            m = number[kind, n]
                            bank = ps[:, (N_CHUNK + m) % RING, :]
                            s = slice(n * TC, (n + 1) * TC)
                            if n or not prol:
                                dve.wait_ge(rope_done, n if prol else at.i * NC_ + (NC_ + n))
                            dve.wait_ge(proj_mm, m + 1 if prol else at.proj(m + 1))
                            dve.scalar_tensor_tensor(ra[:], bank[0:ROPE, :], SCALE, k.trig[0:ROPE, s],
                                                     ALU.mult, ALU.mult)
                            dve.scalar_tensor_tensor(rb[:], bank[ROPE:P, :], SCALE, k.trig[ROPE:P, s],
                                                     ALU.mult, ALU.mult).then_inc(proj_free, 1)
                            dve.wait_ge(proj_free, m + 1 if prol else at.proj(m + 1))
                            dve.tensor_tensor(ra[:], ra[:], rb[:], ALU.add).then_inc(rope_sum, 1)
                        elif kind == "RL":
                            s = slice(n * TC, (n + 1) * TC)
                            dve.wait_ge(rope_hi, n + 1 if prol else at.i * NC_ + (NC_ + n + 1))
                            dve.tensor_tensor(qr[ROPE:P, s], ra[:], qr[0:ROPE, s].bitcast(F32),
                                              ALU.subtract).then_inc(rope_done, 1)
                        elif kind == "S":
                            g, b = BLOCKS[n]
                            for c in range(g + 1):
                                width = TC if c < g else (b + 1) * P
                                to = nmax[:, n, c:c + 1] if g else nbias[:, n:n + 1]
                                dve.wait_ge(scores_mm, at.scores(chunk_no[n, c] + 1))
                                ins = dve.tensor_reduce(to, ps[:, chunk_no[n, c] % RING, 0:width], AX.X, ALU.max,
                                                        negate=True)
                                ins.then_inc(max_step if g else max_done, 1)
                            if g:
                                n_max = chunk_no[n, g] + 1 - QB
                                dve.wait_ge(max_step, at.i * (N_CHUNK - QB) + n_max)
                                dve.tensor_reduce(nbias[:, n:n + 1], nmax[:, n, 0:g + 1], AX.X,
                                                  ALU.min).then_inc(max_done, 1)
                        elif kind == "E":
                            g, b = BLOCKS[n]
                            dve.wait_ge(exp_done, at.scores(chunk_no[n, g] + 1))
                            if g:
                                dve.tensor_reduce(rinv[:, n:n + 1], rsum[:, n, 0:g + 1], AX.X,
                                                  ALU.add).then_inc(sum_step, 1)
                                dve.wait_ge(sum_step, at.i * (16 - QB) + (n + 1 - QB))
                                src = rinv[:, n:n + 1]
                            else:
                                src = rsum[:, n, 0:1]
                            dve.reciprocal(rinv[:, n:n + 1], src).then_inc(rinv_done, 1)
                        elif kind == "T":
                            g, j = TILES[n]
                            s = slice(max(0, j - QB * g) * P, TC)
                            dve.wait_ge(t_hi, at.tile(n + 1))
                            dve.tensor_tensor(pt_lo[n % SLOTS][:, s], ps_t[:, n % 2, s],
                                              pt_hi[n % SLOTS][:, s].bitcast(F32), ALU.subtract).then_inc(t_lo, 1)
                        elif kind == "PV":
                            g, j = TILES[n]
                            if j == QB * (g + 1) - 1:
                                m = ORDER.index(g)
                                dve.wait_ge(pv_done, at.tile(n + 1 + PV_CREDIT))
                                dve.wait_ge(bg_in, at.i * (16 * QB) + 16 * (m + 1))
                                dve.wait_ge(o_out, at.i * (16 * QB) + (16 * m + O_OUT_CREDIT))
                                dve.tensor_tensor(o_sb[:], ps_o[:], bg[:], ALU.mult).then_inc(o_done, 1)

                run(prologue, At(-1), prol=True)
                with dve.Fori(0, H - 1) as i:
                    run(body, At(i))
                run(last_body, At(H - 1))

            @block.gpsimd
            def _(pool):
                pool.sem_inc(t_done, T_CREDIT)
                pool.sem_inc(pv_done, PV_CREDIT)

                def run(ev, at, prol=False):
                    for kind, n in ev:
                        if kind == "W":
                            pool.wait_ge(w_hi_made, 1 if prol else at.i + 2)
                            pool.tensor_tensor(wl[:], raw[:], wh[:].bitcast(F32), ALU.subtract).then_inc(w_lo_made, 1)
                        elif kind == "E":
                            g, b = BLOCKS[n]
                            pool.wait_ge(rinv_done, at.block(n + 1))
                            pool.sem_inc(pool_passed, 1)
                            for c in range(g + 1):
                                width = TC if c < g else (b + 1) * P
                                x = (p_at(g, b) + c * QB) * P
                                pool.tensor_scalar(prob[:, x:x + width], prob[:, x:x + width], rinv[:, n:n + 1], 1.0,
                                                   ALU.mult, ALU.mult).then_inc(normed, 1)

                run(prologue, At(-1), prol=True)
                with pool.Fori(0, H - 1) as i:
                    run(body, At(i))
                run(last_body, At(H - 1))


def load_column_pieces(sp, raw, raw_in, w, lo_made):
    for m in range(KT):
        if m >= 2:
            sp.wait_ge(lo_made, m - 1)
        sp.dma_start(raw[m % 2][:], w[:, :, m * P:(m + 1) * P]).then_inc(raw_in[m % 2], 16)


def conv_out_phase(k):
    nc = k.nc
    BANKS = 6
    with ExitStack() as ctx:
        sb = lambda n, s, d: ctx.enter_context(nc.sbuf_tensor(n, s, d))
        sem = lambda n: ctx.enter_context(nc.semaphore(n))
        raw = [sb(f"c_raw{i}", [P, KT, P], F32) for i in range(2)]
        w_hi, w_lo = sb("c_w_hi", [P, KT, D], F32R), sb("c_w_lo", [P, KT, D], F32R)
        v = sb("c_v", [P, KT, TC], F32)
        z = sb("c_z", [P, KT, TC], F32)
        ag = sb("c_ag", [P, KT, TC], F32)
        z_hi = [sb(f"c_z_hi{i}", [P, KT, TC], F32R) for i in range(2)]
        z_lo = [sb(f"c_z_lo{i}", [P, KT, TC], F32R) for i in range(2)]
        tot = sb("c_tot", [P, TC], F32)
        rstd = sb("c_rstd", [P, TC], F32)
        ga = [sb(f"c_ga{i}", [P, TC], F32) for i in range(2)]
        y = [sb(f"c_y{i}", [P, TC], F32) for i in range(2)]
        ps = ctx.enter_context(nc.psum_tensor("c_ps", [P, BANKS, TC], F32))
        ps_m = ctx.enter_context(nc.psum_tensor("c_ps_m", [P, 2, TC], F32))

        raw_in = [sem(f"c_raw_in{i}") for i in range(2)]
        hi_made, lo_made = sem("c_w_hi_made"), sem("c_w_lo_made")
        v_in, ag_in = sem("c_v_in"), sem("c_ag_in")
        ga_in = [sem(f"c_ga_in{i}") for i in range(2)]
        y_out = [sem(f"c_y_out{i}") for i in range(2)]
        summed = sem("c_summed")
        mean_mm = sem("c_mean_mm")
        centred = sem("c_centred")
        squared = sem("c_squared")
        rooted = sem("c_rooted")
        inverted = sem("c_inverted")
        scaled = sem("c_scaled")
        silu_done = sem("c_silu_done")
        z_done = sem("c_z_done")
        z_hi_done, z_lo_done = sem("c_z_hi_done"), sem("c_z_lo_done")
        tile_mm = sem("c_tile_mm")
        tile_out = sem("c_tile_out")

        by_tile = lambda ap: ap.rearrange("(t p) s -> p t s", p=P)
        w = k.w_conv_out.rearrange("o (t p) n -> p (o t) n", p=P)
        chunk = lambda n: slice(n * TC, (n + 1) * TC)
        N = NC_

        with nc.Block() as block:
            @block.sync
            def _(sp):
                sp.dma_start(v[:], by_tile(k.conv_dram)[:, :, chunk(0)]).then_inc(v_in, 16)
                sp.dma_start(ag[:], by_tile(k.agate_dram)[:, :, chunk(0)]).then_inc(ag_in, 16)
                load_column_pieces(sp, raw, raw_in, w, lo_made)

                def gate(u):
                    if u >= 2:
                        sp.wait_ge(tile_out, u - 1)
                    n, m = divmod(u, KT)
                    sp.dma_start(ga[u % 2][:], k.ga_dram[m * P:(m + 1) * P, chunk(n)]).then_inc(ga_in[u % 2], 16)

                gate(0)
                for u in range(N * KT):
                    n, m = divmod(u, KT)
                    if m == 0 and n + 1 < N:
                        sp.wait_ge(silu_done, KT * (n + 1))
                        sp.dma_start(v[:], by_tile(k.conv_dram)[:, :, chunk(n + 1)]).then_inc(v_in, 16)
                        sp.wait_ge(z_done, KT * (n + 1))
                        sp.dma_start(ag[:], by_tile(k.agate_dram)[:, :, chunk(n + 1)]).then_inc(ag_in, 16)
                    if u + 1 < N * KT:
                        gate(u + 1)
                    sp.wait_ge(tile_out, u + 1)
                    sp.dma_start(k.ya_dram[m * P:(m + 1) * P, chunk(n)], y[u % 2][:]).then_inc(y_out[u % 2], 16)
                for s in range(2):
                    sp.wait_ge(y_out[s], 16 * N * KT // 2)

            @block.tensor
            def _(pe):
                def mean(n, which):
                    pe.wait_ge(summed, 2 * n + which + 1)
                    if n:
                        pe.wait_ge(rooted if which else centred, n)
                    pe.matmul(ps_m[:, which, :], k.mean_mat[:], tot[:], start=True, stop=True).then_inc(mean_mm, 1)

                mean(0, 0)
                mean(0, 1)
                for n in range(N):
                    for m in range(KT):
                        u = n * KT + m
                        if n == 0:
                            pe.wait_ge(lo_made, m + 1)
                        if u >= BANKS:
                            pe.wait_ge(tile_out, u - BANKS + 1)
                        for t in range(KT):
                            if m == 0:
                                pe.wait_ge(z_lo_done, n * KT + t + 1)
                            c = slice(m * P, (m + 1) * P)
                            mm = split3(pe, ps[:, u % BANKS, :], w_hi[:, t, c], w_lo[:, t, c],
                                        z_hi[n % 2][:, t, :], z_lo[n % 2][:, t, :], t == 0, t == KT - 1)
                        mm.then_inc(tile_mm, 1)
                        if n + 1 < N and m in (1, 3):
                            mean(n + 1, m // 2)

            @block.scalar
            def _(act):
                def weights(m):
                    act.wait_ge(raw_in[m % 2], 16 * (m // 2 + 1))
                    act.activation(w_hi[:, :, m * P:(m + 1) * P], raw[m % 2][:], ACT.Copy).then_inc(hi_made, 1)

                for n in range(N):
                    act.wait_ge(centred, n + 1)
                    if n:
                        act.wait_ge(z_lo_done, KT * n)
                    act.activation(z[:], v[:], ACT.Square).then_inc(squared, 1)
                    if n == 0:
                        for m in range(2):
                            weights(m)
                    act.wait_ge(mean_mm, 2 * n + 2)
                    act.activation(rstd[:], ps_m[:, 1, :], ACT.Sqrt, bias=k.eps[:]).then_inc(rooted, 1)
                    act.wait_ge(scaled, n + 1)
                    for t in range(KT):
                        act.activation(z[:, t, :], v[:, t, :], ACT.Silu, scale=k.prm_t[:, R_LNW + t:R_LNW + t + 1],
                                       bias=k.prm_t[:, R_LNB + t:R_LNB + t + 1]).then_inc(silu_done, 1)
                    if n >= 2:
                        act.wait_ge(tile_mm, KT * (n - 1))
                    for t in range(KT):
                        act.wait_ge(z_done, n * KT + t + 1)
                        act.activation(z_hi[n % 2][:, t, :], z[:, t, :], ACT.Copy).then_inc(z_hi_done, 1)
                    if n == 0:
                        for m in range(2, KT):
                            weights(m)

            @block.gpsimd
            def _(pool):
                def weights(m):
                    c = slice(m * P, (m + 1) * P)
                    pool.wait_ge(hi_made, m + 1)
                    pool.tensor_tensor(w_lo[:, :, c], raw[m % 2][:], w_hi[:, :, c].bitcast(F32),
                                       ALU.subtract).then_inc(lo_made, 1)

                for n in range(N):
                    if n == 0:
                        for m in range(2):
                            weights(m)
                    pool.wait_ge(ag_in, 16 * (n + 1))
                    for t in range(KT):
                        pool.wait_ge(silu_done, n * KT + t + 1)
                        pool.tensor_tensor(z[:, t, :], z[:, t, :], ag[:, t, :], ALU.mult).then_inc(z_done, 1)
                    if n == 0:
                        for m in range(2, KT):
                            weights(m)

            @block.vector
            def _(dve):
                wide = lambda ap: ap.unsqueeze(1).to_broadcast([P, KT, TC])

                def total(n, which, src):
                    if n or which:
                        dve.wait_ge(mean_mm, 2 * n + which)
                    dve.tensor_reduce(tot[:], src[:].rearrange("p t s -> p s t"), AX.X, ALU.add).then_inc(summed, 1)

                def prep(n):
                    def a():
                        dve.wait_ge(v_in, 16 * (n + 1))
                        total(n, 0, v)

                    def b():
                        dve.wait_ge(mean_mm, 2 * n + 1)
                        dve.tensor_tensor(v[:], v[:], wide(ps_m[:, 0, :]), ALU.subtract).then_inc(centred, 1)

                    def c():
                        dve.wait_ge(squared, n + 1)
                        total(n, 1, z)

                    def d():
                        dve.wait_ge(rooted, n + 1)
                        dve.reciprocal(rstd[:], rstd[:]).then_inc(inverted, 1)
                        dve.wait_ge(inverted, n + 1)
                        dve.tensor_tensor(v[:], v[:], wide(rstd[:]), ALU.mult).then_inc(scaled, 1)

                    def lo(t):
                        dve.wait_ge(z_hi_done, n * KT + t + 1)
                        dve.tensor_tensor(z_lo[n % 2][:, t, :], z[:, t, :], z_hi[n % 2][:, t, :].bitcast(F32),
                                          ALU.subtract).then_inc(z_lo_done, 1)

                    def e():
                        for t in range(4):
                            lo(t)

                    def f():
                        for t in range(4, KT):
                            lo(t)

                    return [a, b, c, d, e, f]

                for s in prep(0):
                    s()
                for n in range(N):
                    steps = prep(n + 1) if n + 1 < N else []
                    for m in range(KT):
                        u = n * KT + m
                        if m in (0, 1, 2, 3, 6, 7) and steps:
                            steps.pop(0)()
                        dve.wait_ge(tile_mm, u + 1)
                        dve.wait_ge(ga_in[u % 2], 16 * (u // 2 + 1))
                        if u >= 2:
                            dve.wait_ge(y_out[u % 2], 16 * (u // 2))
                        dve.tensor_tensor(y[u % 2][:], ps[:, u % BANKS, :], ga[u % 2][:], ALU.mult).then_inc(tile_out, 1)


def attn_out_phase(k):
    nc = k.nc
    BANKS = 8
    SL = 3
    with ExitStack() as ctx:
        sb = lambda n, s, d: ctx.enter_context(nc.sbuf_tensor(n, s, d))
        sem = lambda n: ctx.enter_context(nc.semaphore(n))
        raw = [sb(f"a_raw{i}", [P, KT, P], F32) for i in range(2)]
        w_hi, w_lo = sb("a_w_hi", [P, KT, D], F32R), sb("a_w_lo", [P, KT, D], F32R)
        o = sb("a_o", [P, KT, TC], F32)
        o_hi = [sb(f"a_o_hi{i}", [P, KT, TC], F32R) for i in range(2)]
        o_lo = [sb(f"a_o_lo{i}", [P, KT, TC], F32R) for i in range(2)]
        gb = [sb(f"a_gb{i}", [P, TC], F32) for i in range(SL)]
        ya = [sb(f"a_ya{i}", [P, TC], F32) for i in range(SL)]
        y = [sb(f"a_y{i}", [P, TC], F32) for i in range(SL)]
        ps = ctx.enter_context(nc.psum_tensor("a_ps", [P, BANKS, TC], F32))

        raw_in = [sem(f"a_raw_in{i}") for i in range(2)]
        hi_made, lo_made = sem("a_w_hi_made"), sem("a_w_lo_made")
        o_in = sem("a_o_in")
        gb_in = [sem(f"a_gb_in{i}") for i in range(SL)]
        y_out = [sem(f"a_y_out{i}") for i in range(SL)]
        o_hi_done, o_lo_done = sem("a_o_hi_done"), sem("a_o_lo_done")
        tile_mm = sem("a_tile_mm")
        gated = sem("a_gated")
        tile_out = sem("a_tile_out")

        w = k.w_attn_out.rearrange("o (t p) n -> p (o t) n", p=P)
        chunk = lambda n: slice(n * TC, (n + 1) * TC)
        N = NC_
        o_src = k.attn_dram.rearrange("(t p) s -> p t s", p=P)

        with nc.Block() as block:
            @block.sync
            def _(sp):
                sp.dma_start(o[:], o_src[:, :, chunk(0)]).then_inc(o_in, 16)
                load_column_pieces(sp, raw, raw_in, w, lo_made)

                def gate(u):
                    if u >= SL:
                        sp.wait_ge(tile_out, u - SL + 1)
                    n, m = divmod(u, KT)
                    sp.dma_start(gb[u % SL][:], k.gb_dram[m * P:(m + 1) * P, chunk(n)]).then_inc(gb_in[u % SL], 16)
                    sp.dma_start(ya[u % SL][:], k.ya_dram[m * P:(m + 1) * P, chunk(n)]).then_inc(gb_in[u % SL], 16)

                gate(0)
                gate(1)
                for u in range(N * KT):
                    n, m = divmod(u, KT)
                    if m == 0 and n + 1 < N:
                        sp.wait_ge(o_lo_done, KT * (n + 1))
                        sp.dma_start(o[:], o_src[:, :, chunk(n + 1)]).then_inc(o_in, 16)
                    if u + 2 < N * KT:
                        gate(u + 2)
                    sp.wait_ge(tile_out, u + 1)
                    sp.dma_start(k.merged_dram[m * P:(m + 1) * P, chunk(n)], y[u % SL][:]).then_inc(y_out[u % SL], 16)
                for s in range(SL):
                    sp.wait_ge(y_out[s], 16 * len(range(s, N * KT, SL)))

            @block.tensor
            def _(pe):
                for n in range(N):
                    for m in range(KT):
                        u = n * KT + m
                        if n == 0:
                            pe.wait_ge(lo_made, m + 1)
                        if u >= BANKS:
                            pe.wait_ge(gated, u - BANKS + 1)
                        c = slice(m * P, (m + 1) * P)
                        for t in range(KT):
                            if m == 0:
                                pe.wait_ge(o_lo_done, n * KT + t + 1)
                            mm = split3(pe, ps[:, u % BANKS, :], w_hi[:, t, c], w_lo[:, t, c],
                                        o_hi[n % 2][:, t, :], o_lo[n % 2][:, t, :], t == 0, t == KT - 1)
                        mm.then_inc(tile_mm, 1)

            @block.scalar
            def _(act):
                def weights(m):
                    act.wait_ge(raw_in[m % 2], 16 * (m // 2 + 1))
                    act.activation(w_hi[:, :, m * P:(m + 1) * P], raw[m % 2][:], ACT.Copy).then_inc(hi_made, 1)

                for n in range(N):
                    act.wait_ge(o_in, 16 * (n + 1))
                    if n >= 2:
                        act.wait_ge(tile_mm, KT * (n - 1))
                    for t in range(KT):
                        act.activation(o_hi[n % 2][:, t, :], o[:, t, :], ACT.Copy).then_inc(o_hi_done, 1)
                        if n == 0 and t == 3:
                            weights(0)
                    if n == 0:
                        for m in range(1, KT):
                            weights(m)

            @block.gpsimd
            def _(pool):
                for m in range(KT):
                    c = slice(m * P, (m + 1) * P)
                    pool.wait_ge(hi_made, m + 1)
                    pool.tensor_tensor(w_lo[:, :, c], raw[m % 2][:], w_hi[:, :, c].bitcast(F32),
                                       ALU.subtract).then_inc(lo_made, 1)
                for u in range(N * KT):
                    pool.wait_ge(gated, u + 1)
                    pool.tensor_tensor(y[u % SL][:], y[u % SL][:], ya[u % SL][:], ALU.add).then_inc(tile_out, 1)

            @block.vector
            def _(dve):
                def split_lo(n):
                    for t in range(KT):
                        dve.wait_ge(o_hi_done, n * KT + t + 1)
                        dve.tensor_tensor(o_lo[n % 2][:, t, :], o[:, t, :], o_hi[n % 2][:, t, :].bitcast(F32),
                                          ALU.subtract).then_inc(o_lo_done, 1)

                split_lo(0)
                for n in range(N):
                    for m in range(KT):
                        u = n * KT + m
                        if m == 3 and n + 1 < N:
                            split_lo(n + 1)
                        dve.wait_ge(tile_mm, u + 1)
                        dve.wait_ge(gb_in[u % SL], 32 * (u // SL + 1))
                        if u >= SL:
                            dve.wait_ge(y_out[u % SL], 16 * (u // SL))
                        dve.tensor_tensor(y[u % SL][:], ps[:, u % BANKS, :], gb[u % SL][:], ALU.mult).then_inc(gated, 1)


def final_phase(k):
    nc = k.nc
    TT = S // P
    PER = TC // P
    PAIRS = 4
    SL = 3
    with ExitStack() as ctx:
        sb = lambda n, s, d: ctx.enter_context(nc.sbuf_tensor(n, s, d))
        sem = lambda n: ctx.enter_context(nc.semaphore(n))
        raw = [sb(f"f_raw{i}", [P, D], F32) for i in range(2)]
        w_hi, w_lo = sb("f_w_hi", [P, KT, D], F32R), sb("f_w_lo", [P, KT, D], F32R)
        mg = sb("f_mg", [P, KT, TC], F32)
        m_hi = [sb(f"f_m_hi{i}", [P, KT, TC], F32R) for i in range(2)]
        m_lo = [sb(f"f_m_lo{i}", [P, KT, TC], F32R) for i in range(2)]
        gate = sb("f_gate", [P, D], F32)
        norm = sb("f_norm", [P, D], F32)
        x = [sb(f"f_x{i}", [P, D], F32) for i in range(SL)]
        y = [sb(f"f_y{i}", [P, D], F32) for i in range(SL)]
        sq = sb("f_sq", [P, D], BF16)
        ss = sb("f_ss", [P, TT], F32)
        ps = ctx.enter_context(nc.psum_tensor("f_ps", [P, PAIRS, D], F32))

        raw_in = [sem(f"f_raw_in{i}") for i in range(2)]
        hi_made, lo_made = sem("f_w_hi_made"), sem("f_w_lo_made")
        rows_in = sem("f_rows_in")
        m_in = sem("f_m_in")
        x_in = [sem(f"f_x_in{i}") for i in range(SL)]
        y_out = [sem(f"f_y_out{i}") for i in range(SL)]
        m_hi_done, m_lo_done = sem("f_m_hi_done"), sem("f_m_lo_done")
        tile_mm = sem("f_tile_mm")
        gated = sem("f_gated")
        added = sem("f_added")
        squared = sem("f_squared")
        rooted = sem("f_rooted")
        inverted = sem("f_inverted")
        y_done = sem("f_y_done")

        w = k.w_out.rearrange("o (t p) n -> p (o t) n", p=P)
        chunk = lambda n: slice(n * TC, (n + 1) * TC)
        src = k.merged_dram.rearrange("(t p) s -> p t s", p=P)
        x_rows = k.x.rearrange("o (n p) d -> (o n) p d", p=P)
        out_rows = k.out.rearrange("o (n p) d -> (o n) p d", p=P)
        N = NC_

        with nc.Block() as block:
            @block.sync
            def _(sp):
                sp.dma_start(mg[:], src[:, :, chunk(0)]).then_inc(m_in, 16)
                for t in range(KT):
                    if t >= 2:
                        sp.wait_ge(lo_made, t - 1)
                    sp.dma_start(raw[t % 2][:], w[:, t, :]).then_inc(raw_in[t % 2], 16)
                sp.dma_start(gate[:], k.gate_dram).then_inc(rows_in, 16)
                sp.dma_start(norm[:], k.final_norm_w.rearrange("(o d) -> o d", o=1).to_broadcast([P, D])).then_inc(rows_in, 16)

                def load_x(u):
                    if u >= SL:
                        sp.wait_ge(added, u - SL + 1)
                    sp.dma_start(x[u % SL][:], x_rows[u]).then_inc(x_in[u % SL], 16)

                load_x(0)
                load_x(1)
                for u in range(TT):
                    n, m = divmod(u, PER)
                    if m == 0 and n + 1 < N:
                        sp.wait_ge(m_lo_done, KT * (n + 1))
                        sp.dma_start(mg[:], src[:, :, chunk(n + 1)]).then_inc(m_in, 16)
                    if u + 2 < TT:
                        load_x(u + 2)
                    sp.wait_ge(y_done, u + 1)
                    sp.dma_start(out_rows[u], y[u % SL][:]).then_inc(y_out[u % SL], 16)
                for s in range(SL):
                    sp.wait_ge(y_out[s], 16 * len(range(s, TT, SL)))

            @block.tensor
            def _(pe):
                for u in range(TT):
                    n, m = divmod(u, PER)
                    if u >= PAIRS:
                        pe.wait_ge(gated, u - PAIRS + 1)
                    q = slice(m * P, (m + 1) * P)
                    for t in range(KT):
                        if u == 0:
                            pe.wait_ge(lo_made, t + 1)
                        if m == 0:
                            pe.wait_ge(m_lo_done, n * KT + t + 1)
                        for half in range(2):
                            c = slice(half * TC, (half + 1) * TC)
                            mm = split3(pe, ps[:, u % PAIRS, c], m_hi[n % 2][:, t, q], m_lo[n % 2][:, t, q],
                                        w_hi[:, t, c], w_lo[:, t, c], t == 0, t == KT - 1)
                    mm.then_inc(tile_mm, 1)

            @block.scalar
            def _(act):
                def split_hi(n):
                    act.wait_ge(m_in, 16 * (n + 1))
                    if n >= 2:
                        act.wait_ge(tile_mm, PER * (n - 1))
                    for t in range(KT):
                        act.activation(m_hi[n % 2][:, t, :], mg[:, t, :], ACT.Copy).then_inc(m_hi_done, 1)
                        if n == 0:
                            act.wait_ge(raw_in[t % 2], 16 * (t // 2 + 1))
                            act.activation(w_hi[:, t, :], raw[t % 2][:], ACT.Copy).then_inc(hi_made, 1)

                split_hi(0)
                for u in range(TT):
                    n, m = divmod(u, PER)
                    act.wait_ge(added, u + 1)
                    if u:
                        act.wait_ge(squared, u)
                    act.activation(sq[:], y[u % SL][:], ACT.Square, accum_out=ss[:, u:u + 1]).then_inc(squared, 1)
                    act.wait_ge(squared, u + 1)
                    act.activation(ss[:, u:u + 1], ss[:, u:u + 1], ACT.Sqrt, scale=1.0 / D,
                                   bias=k.eps[:]).then_inc(rooted, 1)
                    if m == 1 and n + 1 < N:
                        split_hi(n + 1)

            @block.gpsimd
            def _(pool):
                for t in range(KT):
                    pool.wait_ge(hi_made, t + 1)
                    pool.tensor_tensor(w_lo[:, t, :], raw[t % 2][:], w_hi[:, t, :].bitcast(F32),
                                       ALU.subtract).then_inc(lo_made, 1)
                for u in range(TT):
                    pool.wait_ge(x_in[u % SL], 16 * (u // SL + 1))
                    pool.wait_ge(gated, u + 1)
                    pool.tensor_tensor(y[u % SL][:], y[u % SL][:], x[u % SL][:], ALU.add).then_inc(added, 1)

            @block.vector
            def _(dve):
                def split_lo(n):
                    for t in range(KT):
                        dve.wait_ge(m_hi_done, n * KT + t + 1)
                        dve.tensor_tensor(m_lo[n % 2][:, t, :], mg[:, t, :], m_hi[n % 2][:, t, :].bitcast(F32),
                                          ALU.subtract).then_inc(m_lo_done, 1)

                def finish(u):
                    dve.wait_ge(rooted, u + 1)
                    dve.reciprocal(ss[:, u:u + 1], ss[:, u:u + 1]).then_inc(inverted, 1)
                    dve.wait_ge(inverted, u + 1)
                    dve.scalar_tensor_tensor(y[u % SL][:], y[u % SL][:], ss[:, u:u + 1], norm[:],
                                             ALU.mult, ALU.mult).then_inc(y_done, 1)

                split_lo(0)
                dve.wait_ge(rows_in, 32)
                for u in range(TT):
                    n, m = divmod(u, PER)
                    dve.wait_ge(tile_mm, u + 1)
                    if u >= SL:
                        dve.wait_ge(y_out[u % SL], 16 * (u // SL))
                    dve.tensor_tensor(y[u % SL][:], ps[:, u % PAIRS, :], gate[:], ALU.mult).then_inc(gated, 1)
                    if u:
                        finish(u - 1)
                    if m == 1 and n + 1 < N:
                        split_lo(n + 1)
                finish(TT - 1)


PHASES = ["setup", "proj", "latent", "attn", "conv_out", "attn_out", "final"]


def build(nc, ins, out, phases=PHASES):
    with ExitStack() as ctx:
        k = Kernel(nc, ctx, ins, out)
        with ExitStack() as hctx:
            k.h_hi = hctx.enter_context(nc.sbuf_tensor("h_hi", [P, KT, S], F32R))
            k.h_lo = hctx.enter_context(nc.sbuf_tensor("h_lo", [P, KT, S], F32R))
            if "setup" in phases:
                setup_phase(k)
            if "proj" in phases:
                projection_phase(k)
        with ExitStack() as actx:
            k.ckv_hi = actx.enter_context(nc.sbuf_tensor("ckv_hi", [P, LT, S], F32R))
            k.ckv_lo = actx.enter_context(nc.sbuf_tensor("ckv_lo", [P, LT, S], F32R))
            k.kr_hi2 = actx.enter_context(nc.sbuf_tensor("kr_hi2", [P, S], F32R))
            k.kr_lo = actx.enter_context(nc.sbuf_tensor("kr_lo", [ROPE, S], F32R))
            k.trig = actx.enter_context(nc.sbuf_tensor("trig", [P, S], F32))
            if "latent" in phases:
                latent_phase(k)
            if "attn" in phases:
                attention_phase(k)
        if "conv_out" in phases:
            conv_out_phase(k)
        if "attn_out" in phases:
            attn_out_phase(k)
        if "final" in phases:
            final_phase(k)


_INS = ["x", "c", "positions", "w_ada", "b_ada", "norm_w", "w_in", "conv_w", "conv_b", "conv_ln_w", "conv_ln_b",
        "w_conv_out", "q_norm_w", "w_uq", "kv_norm_w", "w_ukv", "w_attn_out", "w_out", "final_norm_w"]


def _freqs():
    import numpy as np

    f = np.float32(10000.0) ** (-np.arange(0, 64, 2, dtype=np.float32) / np.float32(64))
    sign = np.repeat(np.array([1, 1, -1, 1], np.float32), 32)
    return np.ascontiguousarray(np.stack([np.tile(f, 4), sign], axis=1).astype(np.float32))


def kernel(**inputs):
    import numpy as _np
    import concourse.bacc as _bacc
    from concourse import mybir as _mybir
    from concourse.bass_utils import run_bass_kernel_spmd as _run

    nc = _bacc.Bacc("TRN2", target_bir_lowering=False, num_devices=1)
    arrays, ins = {}, {}
    for name in _INS:
        arrays[f"in_{name}_dram"] = _np.ascontiguousarray(inputs[name])
    arrays["in_freqs_dram"] = _freqs()
    for name in _INS + ["freqs"]:
        a = arrays[f"in_{name}_dram"]
        ins[name] = nc.dram_tensor(f"in_{name}_dram", a.shape, _mybir.dt.from_np(a.dtype), kind="ExternalInput").ap()
    out = nc.dram_tensor("out_0_dram", (1, S, D), _mybir.dt.float32, kind="ExternalOutput").ap()
    build(nc, ins, out)
    r = _run(nc, [arrays], core_ids=[0])
    return r.results[0]["out_0_dram"]
```

```python
from contextlib import ExitStack

import concourse.bass as bass
from concourse import mybir

ALU = mybir.AluOpType
ACT = mybir.ActivationFunctionType
AX = mybir.AxisListType
F32 = mybir.dt.float32
F32R = mybir.dt.float32r
BF16 = mybir.dt.bfloat16
I32 = mybir.dt.int32

P = 128
D = 1024
KT = D // P
S = 2048
TC = 512
NC_ = S // TC
TAPS = 31
H = 8
NOPE, ROPE, VD = 128, 64, 128
LAT = 256
LT = LAT // P
CONVW = 1024
C_VAL, C_GLU, C_AGATE = 0, CONVW, 2 * CONVW
C_CQ = 3 * CONVW
C_CKV = C_CQ + LAT
C_KPE = C_CKV + LAT
C_BGATE = C_KPE + ROPE
C_GA = C_BGATE + D
C_GB = C_GA + D
QH = NOPE + ROPE
KVH = NOPE + VD
EPS = 1e-6
NEG = -1e30

R_C, R_NORM, R_BADA, R_CONVB, R_LNW, R_LNB, R_QN, R_KVN, R_END = 0, 8, 16, 40, 48, 56, 64, 66, 68


def split3(pe, out, wh, wl, xh, xl, first, last):
    pe.matmul(out, wh, xh, start=first, stop=False)
    pe.matmul(out, wh, xl, start=False, stop=False)
    return pe.matmul(out, wl, xh, start=False, stop=last)


class Kernel:

    def __init__(self, nc, ctx, ins, out):
        self.nc, self.out = nc, out
        self.x, self.c, self.positions, self.freqs = ins["x"], ins["c"], ins["positions"], ins["freqs"]
        self.w_ada, self.b_ada, self.norm_w, self.w_in = ins["w_ada"], ins["b_ada"], ins["norm_w"], ins["w_in"]
        self.conv_w, self.conv_b = ins["conv_w"], ins["conv_b"]
        self.conv_ln_w, self.conv_ln_b = ins["conv_ln_w"], ins["conv_ln_b"]
        self.q_norm_w, self.kv_norm_w, self.w_uq, self.w_ukv = (
            ins["q_norm_w"], ins["kv_norm_w"], ins["w_uq"], ins["w_ukv"])
        self.w_conv_out, self.w_attn_out, self.w_out = ins["w_conv_out"], ins["w_attn_out"], ins["w_out"]
        self.final_norm_w = ins["final_norm_w"]

        dram = lambda n, s, d: nc.dram_tensor(n, s, d).ap()
        self.gate_dram = dram("gate_dram", [P, D], F32)
        self.ckv_dram = dram("ckv_dram", [2, P, LT, S], F32)
        self.kr_dram = dram("kr_dram", [2, ROPE, S], F32)
        self.trig_dram = dram("trig_dram", [P, S], F32)
        self.agate_dram = dram("agate_dram", [D, S], F32)
        self.bgate_dram = dram("bgate_dram", [D, S], F32)
        self.ga_dram = dram("ga_dram", [D, S], F32)
        self.gb_dram = dram("gb_dram", [D, S], F32)
        self.conv_dram = dram("conv_dram", [D, S], F32)
        self.qlat_dram = dram("qlat_dram", [NC_, P, 2, LT, TC], F32)
        self.v_dram = dram("v_dram", [H * P, S // P, VD], F32)
        self.attn_dram = dram("attn_dram", [D, S], F32)
        self.yb_dram = dram("yb_dram", [D, S], F32)
        self.merged_dram = dram("merged_dram", [D, S], F32)

        sb = lambda n, s, d: ctx.enter_context(nc.sbuf_tensor(n, s, d))
        self.ident = sb("ident", [P, P], F32)
        self.ident16 = sb("ident16", [P, P], BF16)
        self.mask = sb("mask", [P, P], BF16)
        self.mean_mat = sb("mean_mat", [P, P], F32)
        self.eps = sb("eps", [P, 1], F32)
        self.prm_t = sb("prm_t", [P, R_END], F32)
        self.taps_t = sb("taps_t", [P, KT * TAPS], F32)


def setup_phase(k):
    nc = k.nc
    with ExitStack() as ctx:
        sb = lambda n, s, d: ctx.enter_context(nc.sbuf_tensor(n, s, d))
        sem = lambda n: ctx.enter_context(nc.semaphore(n))
        prm = sb("prm", [R_END, P], F32)
        rowbuf = sb("rowbuf", [P, D], F32)
        taps = rowbuf[0:TAPS, :]
        gate = rowbuf
        wada = [sb(f"wada{i}", [P, KT, TC], F32) for i in range(2)]
        xs = [sb(f"xs{i}", [P, 4, D], F32) for i in range(2)]
        sq = sb("sq", [P, D], BF16)
        ss = sb("ss", [P, 16], F32)
        full = [sb(f"full{i}", [P, TC], F32) for i in range(2)]
        cact = sb("cact", [P, KT], F32)
        shift = sb("shift", [P, KT], F32)
        gain = sb("gain", [P, KT], F32)
        ps_par = ctx.enter_context(nc.psum_tensor("ps_par", [P, 512], F32))
        ps_ada = ctx.enter_context(nc.psum_tensor("ps_ada", [P, 16], F32))
        ps_gate = ctx.enter_context(nc.psum_tensor("ps_gate", [P, 2, TC], F32))
        ps_x = ctx.enter_context(nc.psum_tensor("ps_x", [P, 4, TC], F32))

        params_in = sem("params_in")
        wada_in = [sem(f"wada_in{i}") for i in range(2)]
        x_in = [sem(f"x_in{i}") for i in range(2)]
        brow_in = sem("brow_in")
        consts = sem("consts")
        params_t = sem("params_t")
        params_sb = sem("params_sb")
        cact_done = sem("cact_done")
        ada_mm = sem("ada_mm")
        ada_vec = sem("ada_vec")
        gate_mm = sem("gate_mm")
        gate_sb = sem("gate_sb")
        gate_out = sem("gate_out")
        sums_done = sem("sums_done")
        root_done = sem("root_done")
        rstd_done = sem("rstd_done")
        x_scaled = sem("x_scaled")
        x_turned = sem("x_turned")
        full_done = sem("full_done")
        hi_done = sem("hi_done")
        lo_done = sem("lo_done")

        rows = [(R_C, KT, k.c), (R_NORM, KT, k.norm_w), (R_BADA, 3 * KT, k.b_ada), (R_CONVB, KT, k.conv_b),
                (R_LNW, KT, k.conv_ln_w), (R_LNB, KT, k.conv_ln_b), (R_QN, LT, k.q_norm_w), (R_KVN, LT, k.kv_norm_w)]
        w_ada = k.w_ada.rearrange("o (t p) n -> p (o t) n", p=P)
        x_groups = k.x.rearrange("o (g j p) d -> (o g) p j d", p=P, j=4)

        with nc.Block() as block:
            @block.sync
            def _(sp):
                for r, n, src in rows:
                    sp.dma_start(prm[r:r + n, :], src.rearrange("o (t p) -> (o t) p", p=P)).then_inc(params_in, 16)
                sp.dma_start(taps, k.conv_w.rearrange("o t c -> (o t) c")).then_inc(params_in, 16)
                for g in range(2):
                    sp.dma_start(wada[g][:], w_ada[:, :, g * TC:(g + 1) * TC]).then_inc(wada_in[g], 16)
                    sp.dma_start(xs[g][:], x_groups[g]).then_inc(x_in[g], 16)
                for g in range(2, 6):
                    sp.wait_ge(ada_mm if g < 6 else gate_mm, g - 1)
                    sp.dma_start(wada[g % 2][:], w_ada[:, :, g * TC:(g + 1) * TC]).then_inc(wada_in[g % 2], 16)
                    if g == 4:
                        sp.wait_ge(params_t, 2)
                        sp.dma_start(gate[:], k.b_ada[:, 2 * D:3 * D].to_broadcast([P, D])).then_inc(brow_in, 16)
                for g in range(2, 4):
                    sp.wait_ge(x_turned, KT * (g - 1))
                    sp.dma_start(xs[g % 2][:], x_groups[g]).then_inc(x_in[g % 2], 16)
                sp.wait_ge(gate_sb, 2)
                sp.dma_start(k.gate_dram, gate[:]).then_inc(gate_out, 16)
                sp.wait_ge(gate_out, 16)

            @block.gpsimd
            def _(pool):
                pool.memset(k.ident[:], 0.0).then_inc(consts, 1)
                pool.memset(k.mask[:], 0.0).then_inc(consts, 1)
                pool.memset(k.mean_mat[:], 1.0 / D).then_inc(consts, 1)
                pool.memset(k.eps[:], EPS).then_inc(consts, 1)
                pool.wait_ge(consts, 4)
                pool.affine_select(out=k.ident[:], in_=k.ident[:], compare_op=ALU.not_equal, fill=1.0, base=0,
                                   pattern=[[-1, P]], channel_multiplier=1).then_inc(consts, 1)
                pool.affine_select(out=k.mask[:], in_=k.mask[:], compare_op=ALU.is_ge, fill=NEG, base=0,
                                   pattern=[[-1, P]], channel_multiplier=1).then_inc(consts, 1)
                pool.wait_ge(consts, 6)
                pool.tensor_copy(k.ident16[:], k.ident[:]).then_inc(consts, 1)

            @block.scalar
            def _(act):
                act.wait_ge(params_sb, 1)
                act.activation(cact[:], k.prm_t[:, R_C:R_C + KT], ACT.Silu).then_inc(cact_done, 1)
                for g in range(4):
                    act.wait_ge(x_in[g % 2], 16 * (g // 2 + 1))
                    for j in range(4):
                        if g or j:
                            act.wait_ge(sums_done, 4 * g + j)
                        act.activation(sq[:], xs[g % 2][:, j, :], ACT.Square,
                                       accum_out=ss[:, 4 * g + j:4 * g + j + 1]).then_inc(sums_done, 1)
                    act.wait_ge(sums_done, 4 * g + 4)
                    act.wait_ge(consts, 4)
                    act.activation(ss[:, 4 * g:4 * g + 4], ss[:, 4 * g:4 * g + 4], ACT.Sqrt,
                                   scale=1.0 / D, bias=k.eps[:]).then_inc(root_done, 1)
                    if g == 0:
                        act.wait_ge(ada_vec, 4)
                    for t in range(KT):
                        n = g * KT + t
                        act.wait_ge(x_turned, n + 1)
                        if n >= 2:
                            act.wait_ge(lo_done, n - 1)
                        act.activation(full[n % 2][:], ps_x[:, n % 4, :], ACT.Identity, scale=gain[:, t:t + 1],
                                       bias=shift[:, t:t + 1]).then_inc(full_done, 1)

            @block.vector
            def _(dve):
                dve.wait_ge(params_t, 2)
                dve.tensor_copy(k.prm_t[:], ps_par[:, 0:R_END]).then_inc(params_sb, 1)
                dve.tensor_copy(k.taps_t[:],
                                ps_par[:, P:P + KT * TAPS]).then_inc(params_sb, 1)

                def scale_x(g):
                    dve.wait_ge(root_done, g + 1)
                    dve.reciprocal(ss[:, 4 * g:4 * g + 4], ss[:, 4 * g:4 * g + 4]).then_inc(rstd_done, 1)
                    dve.wait_ge(rstd_done, g + 1)
                    for j in range(4):
                        dve.tensor_scalar(xs[g % 2][:, j, :], xs[g % 2][:, j, :], ss[:, 4 * g + j:4 * g + j + 1],
                                          None, ALU.mult).then_inc(x_scaled, 1)

                scale_x(0)
                dve.wait_ge(ada_mm, 4)
                dve.tensor_tensor(shift[:], ps_ada[:, 0:KT], k.prm_t[:, R_BADA:R_BADA + KT],
                                  ALU.add).then_inc(ada_vec, 1)
                dve.tensor_tensor(gain[:], ps_ada[:, KT:2 * KT], k.prm_t[:, R_BADA + KT:R_BADA + 2 * KT],
                                  ALU.add).then_inc(ada_vec, 1)
                dve.wait_ge(ada_vec, 2)
                dve.tensor_scalar_add(gain[:], gain[:], 1.0).then_inc(ada_vec, 1)
                dve.wait_ge(ada_vec, 3)
                dve.tensor_tensor(gain[:], gain[:], k.prm_t[:, R_NORM:R_NORM + KT], ALU.mult).then_inc(ada_vec, 1)
                for g in range(4):
                    if g:
                        scale_x(g)
                    for t in range(KT):
                        n = g * KT + t
                        hi, lo = (a[:, t, g * TC:(g + 1) * TC] for a in (k.h_hi, k.h_lo))
                        dve.wait_ge(full_done, n + 1)
                        dve.tensor_copy(hi, full[n % 2][:]).then_inc(hi_done, 1)
                        dve.wait_ge(hi_done, n + 1)
                        dve.tensor_tensor(lo, full[n % 2][:], hi.bitcast(F32), ALU.subtract).then_inc(lo_done, 1)
                    if g == 1:
                        dve.wait_ge(brow_in, 16)
                        for m in range(2):
                            dve.wait_ge(gate_mm, m + 1)
                            dve.tensor_tensor(gate[:, m * TC:(m + 1) * TC], ps_gate[:, m, :],
                                              gate[:, m * TC:(m + 1) * TC], ALU.add).then_inc(gate_sb, 1)

            @block.tensor
            def _(pe):
                pe.wait_ge(consts, 6)
                pe.wait_ge(params_in, 16 * (len(rows) + 1))
                pe.transpose(ps_par[:, 0:R_END], prm[:], k.ident[0:R_END, 0:R_END]).then_inc(params_t, 1)
                for t in range(KT):
                    mm = pe.transpose(ps_par[:, P + t * TAPS:P + (t + 1) * TAPS], taps[:, t * P:(t + 1) * P],
                                      k.ident[0:TAPS, 0:TAPS])
                mm.then_inc(params_t, 1)

                def turn(g):
                    pe.wait_ge(x_scaled, 4 * g + 4)
                    for t in range(KT):
                        n = g * KT + t
                        if n >= 4:
                            pe.wait_ge(full_done, n - 3)
                        for j in range(4):
                            mm = pe.transpose(ps_x[:, n % 4, j * P:(j + 1) * P],
                                              xs[g % 2][:, j, t * P:(t + 1) * P], k.ident[:])
                        mm.then_inc(x_turned, 1)

                pe.wait_ge(cact_done, 1)
                for g in range(4):
                    pe.wait_ge(wada_in[g % 2], 16 * (g // 2 + 1))
                    for m in range(4):
                        for t in range(KT):
                            mm = pe.matmul(ps_ada[:, g * 4 + m:g * 4 + m + 1], wada[g % 2][:, t, m * P:(m + 1) * P],
                                           cact[:, t:t + 1], start=(t == 0), stop=(t == KT - 1))
                    mm.then_inc(ada_mm, 1)
                turn(0)
                turn(1)
                for m in range(2):
                    pe.wait_ge(wada_in[m], 48)
                    for t in range(KT):
                        mm = pe.matmul(ps_gate[:, m, :], cact[:, t:t + 1].to_broadcast([P, P]), wada[m][:, t, :],
                                       start=(t == 0), stop=(t == KT - 1))
                    mm.then_inc(gate_mm, 1)
                turn(2)
                turn(3)


def projection_phase(k):
    nc = k.nc
    PRE = 5
    PER = 6
    KINDS = ["glu", "val", "ga", "gb", "agate", "bgate"]
    COLS = {"glu": C_GLU, "val": C_VAL, "ga": C_GA, "gb": C_GB, "agate": C_AGATE, "bgate": C_BGATE}
    OUTS = {"ga": k.ga_dram, "gb": k.gb_dram, "agate": k.agate_dram, "bgate": k.bgate_dram}
    FUNC = {"glu": ACT.Sigmoid, "val": ACT.Copy, "ga": ACT.Sigmoid, "gb": ACT.Sigmoid,
            "agate": ACT.Silu, "bgate": ACT.Silu}
    PAD = TAPS - 1
    TWO_PI = 6.283185307179586
    C1 = 6.28125
    C2 = float(round((TWO_PI - C1) * 2.0 ** 20) / 2.0 ** 20)
    C3 = TWO_PI - C1 - C2
    MAGIC = 1.5 * 2.0 ** 23
    PI_BELOW = 3.1415925
    NORM = (R_QN, R_KVN)
    LAT_TILES = 2 * LT
    N_ANGLE = 9
    KPE_HALF = 2 * TC
    with ExitStack() as ctx:
        sb = lambda n, s, d: ctx.enter_context(nc.sbuf_tensor(n, s, d))
        sem = lambda n: ctx.enter_context(nc.semaphore(n))
        raw = [sb(f"raw{i}", [P, KT, P], F32) for i in range(2)]
        w_hi = [sb(f"w_hi{i}", [P, KT, P], F32R) for i in range(2)]
        w_lo = [sb(f"w_lo{i}", [P, KT, P], F32R) for i in range(2)]
        u = sb("u", [P, PAD + S], F32)
        acc = sb("acc", [P, S], F32)
        sg = sb("sg", [P, S], F32)
        lat = sb("lat", [P, LT, S], F32)
        stage = lat[:, LT - 1, :].rearrange("p (c n) -> p c n", c=NC_)
        part_hi = sb("part_hi", [P, LT, TC], F32R)
        part_lo = sb("part_lo", [P, LT, TC], F32R)
        freqs = sb("freqs", [P, 2], F32)
        halfpi = sb("halfpi", [P, 1], F32)
        ang, turns = u[:, PAD:], sg[:]
        kpe = lat[:, LT - 1, :]
        sq = acc[:].rearrange("p (i t n) -> p i t n", i=2, t=LT)
        ps = ctx.enter_context(nc.psum_tensor("ps_proj", [P, 2 * NC_, TC], F32))

        raw_in = [sem(f"raw_in{i}") for i in range(2)]
        hi_made = sem("w_hi_made")
        lo_made = sem("w_lo_made")
        chunk_mm = sem("chunk_mm")
        chunk_out = sem("chunk_out")
        stored = sem("stored")
        glu_used = sem("glu_used")
        conv_tap = sem("conv_tap")
        conv_done = sem("conv_done")
        conv_out = sem("conv_out")
        pos_in = sem("pos_in")
        filled = sem("filled")
        angle_step = sem("angle_step")
        trig_done = sem("trig_done")
        trig_out = sem("trig_out")
        squared = sem("squared")
        summed = sem("summed")
        mean_mm = sem("mean_mm")
        rooted = sem("rooted")
        inverted = sem("inverted")
        scaled = sem("lat_scaled")
        part_hi_done, part_lo_done = sem("part_hi_done"), sem("part_lo_done")
        part_out = sem("part_out")
        kpe_step = sem("kpe_step")

        w_in = k.w_in.rearrange("o (t p) n -> p (o t) n", p=P)

        def tile_weights(sp, slot, col, step=0, swap=False):
            if swap:
                for to, at, n in ((0, 0, ROPE), (ROPE, ROPE // 2, ROPE // 2), (ROPE + ROPE // 2, 0, ROPE // 2)):
                    sp.dma_start(raw[slot][:, :, to:to + n], w_in[:, :, C_KPE + at:C_KPE + at + n]).then_inc(raw_in[slot], 16)
            else:
                sp.dma_start(raw[slot][:], w_in[:, :, col:min(col + D + P, k.w_in.shape[2])][:, :, bass.ds(step, P)]).then_inc(raw_in[slot], 16)

        PRE_RAW = [2 + 3, 2]

        def raw_count(i, q):
            return 16 * (PRE_RAW[(PRE + q) % 2] + q // 2 + 1) + i * (16 * PER // 2)

        with nc.Block() as block:
            @block.sync
            def _(sp):
                pre_cols = [C_CQ, C_CQ + P, C_CKV, C_CKV + P, None]
                tile_weights(sp, 0, pre_cols[0])
                tile_weights(sp, 1, pre_cols[1])
                sp.dma_start(kpe.bitcast(I32), k.positions.to_broadcast([P, S])).then_inc(pos_in, 16)
                sp.dma_start(freqs[:], k.freqs).then_inc(pos_in, 16)

                def store_tile(dst, q_chunks):
                    sp.wait_ge(chunk_out, q_chunks + NC_)
                    sp.dma_start(dst, lat[:, LT - 1, :]).then_inc(stored, 16)

                for t in range(PRE):
                    sp.wait_ge(lo_made, t + 1)
                    if t + 2 < PRE:
                        tile_weights(sp, t % 2, pre_cols[t + 2], swap=(t + 2 == PRE - 1))
                    else:
                        q = t + 2 - PRE
                        tile_weights(sp, t % 2, COLS[KINDS[q]])
                    if t == 0:
                        sp.wait_ge(trig_done, 2)
                        sp.dma_start(k.trig_dram, ang).then_inc(trig_out, 16)
                    if t in (LT, 2 * LT):
                        for c in range(NC_):
                            n = (t // LT - 1) * NC_ + c
                            sp.wait_ge(part_lo_done, n + 1)
                            dst = (k.qlat_dram[c].rearrange("p h t n -> h p t n") if t == LT else
                                   k.ckv_dram[:, :, :, c * TC:(c + 1) * TC])
                            sp.dma_start(dst[0], part_hi[:].bitcast(F32)).then_inc(part_out, 16)
                            sp.dma_start(dst[1], part_lo[:].bitcast(F32)).then_inc(part_out, 16)
                for c in range(2):
                    sp.wait_ge(part_lo_done, 2 * NC_ + c + 1)
                    for h, part in enumerate((part_hi, part_lo)):
                        sp.dma_start(k.kr_dram[h, :, c * KPE_HALF:(c + 1) * KPE_HALF],
                                     part[0:ROPE].rearrange("p t n -> p (t n)").bitcast(F32)).then_inc(part_out, 16)
                sp.sem_inc(stored, 16)
                with sp.Fori(0, H) as i:
                    here = sp.snap(i * P)
                    nxt = sp.snap(i * P + P)
                    for q, kind in enumerate(KINDS):
                        sp.wait_ge(lo_made, i * PER + (PRE + q + 1))
                        tile_weights(sp, (PRE + q) % 2, COLS[KINDS[(q + 2) % PER]], here if q + 2 < PER else nxt)
                        if kind in OUTS:
                            store_tile(OUTS[kind][bass.ds(here, P), :], i * (PER * NC_) + (PRE + q) * NC_)
                    sp.wait_ge(conv_done, i + 2)
                    sp.dma_start(k.conv_dram[bass.ds(here, P), :], acc[:]).then_inc(conv_out, 16)
                sp.wait_ge(conv_out, 16 * (H + 1))
                sp.wait_ge(stored, 16 * (1 + len(OUTS) * H))
                sp.wait_ge(part_out, 32 * (2 * NC_ + 2))
                sp.wait_ge(trig_out, 16)
                for s in range(2):
                    sp.wait_ge(raw_in[s], 16 * (PRE_RAW[s] + 3 * H + 1))

            @block.scalar
            def _(act):
                def split_hi(t_count, slot, raw_need, used):
                    act.wait_ge(raw_in[slot], raw_need)
                    if used is not None:
                        act.wait_ge(chunk_mm, used)
                    act.activation(w_hi[slot][:], raw[slot][:], ACT.Copy).then_inc(hi_made, 1)

                split_hi(0, 0, 16, None)
                split_hi(1, 1, 16, None)
                pre_need = [16, 16, 32, 32, 80]
                act.wait_ge(filled, 1)
                act.wait_ge(angle_step, N_ANGLE)
                act.activation(ang[0:ROPE, :], ang[0:ROPE, :], ACT.Sin, bias=halfpi[0:ROPE, :]).then_inc(trig_done, 1)
                act.activation(ang[ROPE:P, :], ang[ROPE:P, :], ACT.Sin, scale=freqs[ROPE:P, 1:2]).then_inc(trig_done, 1)

                def square(n):
                    c = n % NC_
                    if n >= 2:
                        act.wait_ge(scaled, n - 1)
                    act.activation(sq[:, n % 2], lat[:, :, c * TC:(c + 1) * TC], ACT.Square).then_inc(squared, 1)

                for t in range(PRE):
                    for c in range(NC_):
                        x = lat[:, :, c * TC:(c + 1) * TC]
                        if t in (LT, 2 * LT):
                            n = (t // LT - 1) * NC_ + c
                            act.wait_ge(mean_mm, n + 1)
                            act.activation(sq[:, n % 2, 1, :], ps[:, NC_ + c, :], ACT.Sqrt, scale=D / LAT,
                                           bias=k.eps[:]).then_inc(rooted, 1)
                            act.wait_ge(scaled, n + 1)
                            if n:
                                act.wait_ge(part_out, 32 * n)
                            act.activation(part_hi[:], x, ACT.Copy).then_inc(part_hi_done, 1)
                            if c + 2 < NC_:
                                square(n + 2)
                        act.wait_ge(chunk_mm, t * NC_ + c + 1)
                        if t >= LT:
                            act.wait_ge(part_lo_done, ((t - LT) // LT) * NC_ + c + 1)
                        if t < LAT_TILES:
                            dst = lat[:, t % LT, c * TC:(c + 1) * TC]
                        else:
                            dst = stage[:, c, :]
                        act.activation(dst, ps[:, t % 2 * NC_ + c, :], ACT.Copy).then_inc(chunk_out, 1)
                        if t in (LT - 1, 2 * LT - 1) and c < 2:
                            act.wait_ge(chunk_out, t * NC_ + c + 1)
                            square(t // LT * NC_ + c)
                    n = t + 2
                    need = pre_need[n] if n < PRE else raw_count(0, n - PRE)
                    split_hi(n, n % 2, need, (t + 1) * NC_)
                for c in range(2):
                    act.wait_ge(kpe_step, 3)
                    act.wait_ge(part_out, 32 * (2 * NC_ + c))
                    act.activation(part_hi[0:ROPE].rearrange("p t n -> p (t n)"),
                                   kpe[0:ROPE, c * KPE_HALF:(c + 1) * KPE_HALF], ACT.Copy).then_inc(part_hi_done, 1)
                with act.Fori(0, H) as i:
                    n_stored = 0
                    for q, kind in enumerate(KINDS):
                        bank = (PRE + q) % 2 * NC_
                        for c in range(NC_):
                            act.wait_ge(chunk_mm, i * (PER * NC_) + ((PRE + q) * NC_ + c + 1))
                            if kind == "glu":
                                dst = sg[:, c * TC:(c + 1) * TC]
                                if c == 0:
                                    act.wait_ge(glu_used, i + 1)
                            elif kind == "val":
                                dst = u[:, PAD + c * TC:PAD + (c + 1) * TC]
                                if c == 0:
                                    act.wait_ge(conv_done, i + 1)
                            else:
                                dst = stage[:, c, :]
                                if c == 0:
                                    act.wait_ge(stored, i * (16 * len(OUTS)) + 16 * (1 + n_stored))
                            act.activation(dst, ps[:, bank + c, :], FUNC[kind]).then_inc(chunk_out, 1)
                        n_stored += kind in OUTS
                        j = i if q + 2 < PER else i + 1
                        split_hi(0, (PRE + q) % 2, raw_count(j, (q + 2) % PER),
                                 i * (PER * NC_) + (PRE + q + 1) * NC_)

            @block.gpsimd
            def _(pool):
                pool.memset(halfpi[:], TWO_PI / 4).then_inc(filled, 1)
                pool.memset(u[:, 0:PAD], 0.0).then_inc(filled, 1)
                pool.wait_ge(filled, 2)
                pool.sem_inc(glu_used, 1)

                def split_lo(n_made, slot):
                    pool.wait_ge(hi_made, n_made)
                    pool.tensor_tensor(w_lo[slot][:], raw[slot][:], w_hi[slot][:].bitcast(F32),
                                       ALU.subtract).then_inc(lo_made, 1)

                split_lo(1, 0)
                split_lo(2, 1)
                for t in range(PRE):
                    split_lo(t + 3, t % 2)
                with pool.Fori(0, H) as i:
                    for q, kind in enumerate(KINDS):
                        if kind == "ga":
                            pool.wait_ge(chunk_out, i * (PER * NC_) + (PRE + 2) * NC_)
                            pool.tensor_tensor(u[:, PAD:], u[:, PAD:], sg[:], ALU.mult).then_inc(glu_used, 1)
                        split_lo(i * PER + (PRE + q + 3), (PRE + q) % 2)

            @block.vector
            def _(dve):
                dve.wait_ge(pos_in, 32)
                cs = ang[0:ROPE, :]
                for n, angle in enumerate([
                        lambda: dve.tensor_copy(ang, kpe.bitcast(I32)),
                        lambda: dve.tensor_scalar(ang, ang, freqs[:, 0:1], None, ALU.mult),
                        lambda: dve.tensor_scalar(turns, ang, 1.0 / TWO_PI, MAGIC, ALU.mult, ALU.add),
                        lambda: dve.tensor_scalar(turns, turns, MAGIC, None, ALU.subtract),
                        lambda: dve.scalar_tensor_tensor(ang, turns, -C1, ang, ALU.mult, ALU.add),
                        lambda: dve.scalar_tensor_tensor(ang, turns, -C2, ang, ALU.mult, ALU.add),
                        lambda: dve.scalar_tensor_tensor(ang, turns, -C3, ang, ALU.mult, ALU.add),
                        lambda: dve.tensor_scalar(ang, ang, PI_BELOW, -PI_BELOW, ALU.min, ALU.max),
                        lambda: dve.scalar_tensor_tensor(cs, cs, -1.0, cs, ALU.mult, ALU.min)]):
                    if n:
                        dve.wait_ge(angle_step, n)
                    angle().then_inc(angle_step, 1)

                def sum_squares(n):
                    dve.wait_ge(squared, n + 1)
                    dve.tensor_tensor(sq[:, n % 2, 0, :], sq[:, n % 2, 0, :], sq[:, n % 2, 1, :],
                                      ALU.add).then_inc(summed, 1)

                def normalise(n):
                    a, c = divmod(n, NC_)
                    root = sq[:, n % 2, 1, :]
                    x = lat[:, :, c * TC:(c + 1) * TC]
                    dve.wait_ge(rooted, n + 1)
                    dve.reciprocal(root, root).then_inc(inverted, 1)
                    dve.wait_ge(inverted, n + 1)
                    for t in range(LT):
                        ins = dve.scalar_tensor_tensor(x[:, t, :], x[:, t, :], k.prm_t[:, NORM[a] + t:NORM[a] + t + 1],
                                                       root, ALU.mult, ALU.mult)
                    ins.then_inc(scaled, 1)
                    dve.wait_ge(part_hi_done, n + 1)
                    dve.tensor_tensor(part_lo[:], x, part_hi[:].bitcast(F32), ALU.subtract).then_inc(part_lo_done, 1)

                for a in range(2):
                    sum_squares(a * NC_)
                    sum_squares(a * NC_ + 1)
                    for c in range(NC_):
                        normalise(a * NC_ + c)
                        if c + 2 < NC_:
                            sum_squares(a * NC_ + c + 2)
                dve.wait_ge(trig_done, 2)
                dve.wait_ge(chunk_out, PRE * NC_)
                dve.tensor_tensor(turns[0:ROPE, :], kpe[ROPE:P, :], ang[ROPE:P, :], ALU.mult).then_inc(kpe_step, 1)
                dve.tensor_tensor(kpe[0:ROPE, :], kpe[0:ROPE, :], ang[0:ROPE, :], ALU.mult).then_inc(kpe_step, 1)
                dve.wait_ge(kpe_step, 2)
                dve.tensor_tensor(kpe[0:ROPE, :], kpe[0:ROPE, :], turns[0:ROPE, :], ALU.add).then_inc(kpe_step, 1)
                for c in range(2):
                    dve.wait_ge(part_hi_done, 2 * NC_ + c + 1)
                    dve.tensor_tensor(part_lo[0:ROPE].rearrange("p t n -> p (t n)"),
                                      kpe[0:ROPE, c * KPE_HALF:(c + 1) * KPE_HALF],
                                      part_hi[0:ROPE].rearrange("p t n -> p (t n)").bitcast(F32),
                                      ALU.subtract).then_inc(part_lo_done, 1)

                dve.sem_inc(conv_done, 1)
                dve.sem_inc(conv_out, 16)
                with dve.Fori(0, H) as i:
                    dve.wait_ge(glu_used, i + 2)
                    dve.wait_ge(conv_out, i * 16 + 16)
                    tap = lambda n: k.taps_t[:, bass.ds(i * TAPS + n, 1)]
                    dve.tensor_scalar(acc[:], u[:, 0:S], tap(0), k.prm_t[:, bass.ds(i + R_CONVB, 1)],
                                      ALU.mult, ALU.add).then_inc(conv_tap, 1)
                    for n in range(1, TAPS):
                        dve.wait_ge(conv_tap, i * (TAPS - 1) + n)
                        ins = dve.scalar_tensor_tensor(acc[:], u[:, n:n + S], tap(n), acc[:],
                                                       ALU.mult, ALU.add)
                        ins.then_inc(conv_tap if n < TAPS - 1 else conv_done, 1)

            @block.tensor
            def _(pe):
                def tile(slot, lo_need, free_need, means=None, roots=None):
                    pe.wait_ge(lo_made, lo_need)
                    for c in range(NC_):
                        if means is not None:
                            pe.wait_ge(summed, means + c + 1)
                            pe.matmul(ps[:, NC_ + c, :], k.mean_mat[:], sq[:, (means + c) % 2, 0, :],
                                      start=True, stop=True).then_inc(mean_mm, 1)
                        if roots is not None:
                            pe.wait_ge(rooted, roots + c + 1)
                        if free_need is not None:
                            pe.wait_ge(chunk_out, free_need + c + 1)
                        out = ps[:, slot * NC_ + c, :]
                        for t in range(KT):
                            mm = split3(pe, out, w_hi[slot][:, t, :], w_lo[slot][:, t, :],
                                        k.h_hi[:, t, c * TC:(c + 1) * TC], k.h_lo[:, t, c * TC:(c + 1) * TC],
                                        t == 0, t == KT - 1)
                        mm.then_inc(chunk_mm, 1)

                for t in range(PRE):
                    tile(t % 2, t + 1, (t - 2) * NC_ if t >= 2 else None,
                         (t // LT - 1) * NC_ if t in (LT, 2 * LT) else None, 0 if t == LT + 1 else None)
                pe.wait_ge(rooted, 2 * NC_)
                with pe.Fori(0, H) as i:
                    for q in range(PER):
                        tile((PRE + q) % 2, i * PER + (PRE + q + 1), i * (PER * NC_) + (PRE + q - 2) * NC_)


def value_phase(k):
    nc = k.nc
    V_BANKS = 8
    SLOTS = 3
    QB = TC // P
    HALVES = H * VD // TC
    HH = TC // VD
    TT = S // P
    with ExitStack() as ctx:
        sb = lambda n, s, d: ctx.enter_context(nc.sbuf_tensor(n, s, d))
        sem = lambda n: ctx.enter_context(nc.semaphore(n))
        raw = [sb(f"wv_raw{i}", [P, LT, TC], F32) for i in range(HALVES)]
        w_hi = [sb(f"wv_hi{i}", [P, LT, TC], F32R) for i in range(HALVES)]
        w_lo = [sb(f"wv_lo{i}", [P, LT, TC], F32R) for i in range(HALVES)]
        v = [sb(f"v_st{i}", [P, H * VD], F32) for i in range(SLOTS)]
        ps = ctx.enter_context(nc.psum_tensor("ps_v", [P, V_BANKS, TC], F32))

        raw_in = [sem(f"wv_in{i}") for i in range(HALVES)]
        ckv_in = [sem(f"ckv_in{c}") for c in range(NC_)]
        next_in = sem("next_in")
        w_hi_made, w_lo_made = sem("wv_hi_made"), sem("wv_lo_made")
        v_mm = sem("v_mm")
        v_done = [sem(f"v_done{half}") for half in range(HALVES)]
        head_in = sem("head_w_first_in")
        head_hi_made = sem("head_w_first_hi")
        v_out = [sem(f"v_out{i}") for i in range(SLOTS)]

        w = k.w_ukv.rearrange("o (t p) (h n) -> p (o t) h n", p=P, n=KVH)[:, :, :, NOPE:]

        def copy_half(eng, copy, half):
            for j in range(TT):
                eng.wait_ge(v_mm, j * HALVES + half + 1)
                if j >= SLOTS:
                    eng.wait_ge(v_out[j % SLOTS], 16 * (j // SLOTS))
                copy(v[j % SLOTS][:, half * TC:(half + 1) * TC],
                     ps[:, (j * HALVES + half) % V_BANKS, :]).then_inc(v_done[half], 1)

        with nc.Block() as block:
            @block.sync
            def _(sp):
                def latents(c):
                    s = slice(c * TC, (c + 1) * TC)
                    for part, to in ((0, k.ckv_hi), (1, k.ckv_lo)):
                        sp.dma_start(to[:, :, s].bitcast(F32), k.ckv_dram[part, :, :, s]).then_inc(ckv_in[c], 16)

                for half in range(HALVES):
                    for t in range(LT):
                        sp.dma_start(raw[half][:, t, :].rearrange("p (h n) -> p h n", n=VD),
                                     w[:, t, half * HH:(half + 1) * HH]).then_inc(raw_in[half], 16)
                    latents(half)
                for c in range(HALVES, NC_):
                    latents(c)
                n_next = 0

                def load(to, src):
                    sp.dma_start(to, src).then_inc(next_in, 16)
                    return 1

                v_rows = k.v_dram.rearrange("(h p) j n -> j p h n", p=P)
                for j in range(TT):
                    for half in range(HALVES):
                        sp.wait_ge(v_done[half], j + 1)
                    sp.dma_start(v_rows[j], v[j % SLOTS][:].rearrange("p (h n) -> p h n",
                                                                      n=VD)).then_inc(v_out[j % SLOTS], 16)
                    if j == 0:
                        for to, src in first_weights(k):
                            sp.dma_start(to, src).then_inc(head_in, 16)
                    if j in (1, 2):
                        n_next += load(k.qlat[j - 1][:].bitcast(F32), k.qlat_dram[j - 1])
                    if j == 3:
                        n_next += load(k.trig[:], k.trig_dram)
                    if j == 4:
                        n_next += load(k.kr_hi2[0:ROPE].bitcast(F32), k.kr_dram[0])
                        n_next += load(k.kr_hi2[ROPE:P].bitcast(F32), k.kr_dram[0])
                        n_next += load(k.kr_lo[:].bitcast(F32), k.kr_dram[1])
                sp.wait_ge(next_in, 16 * n_next)
                for s in range(SLOTS):
                    sp.wait_ge(v_out[s], 16 * len(range(s, TT, SLOTS)))

            @block.tensor
            def _(pe):
                for j in range(TT):
                    if j % QB == 0:
                        pe.wait_ge(ckv_in[j // QB], 32)
                    for half in range(HALVES):
                        m = j * HALVES + half
                        if j == 0:
                            pe.wait_ge(w_lo_made, half + 1)
                        if m >= V_BANKS:
                            pe.wait_ge(v_done[half], j - V_BANKS // HALVES + 1)
                        q = slice(j * P, (j + 1) * P)
                        for t in range(LT):
                            mm = split3(pe, ps[:, m % V_BANKS, :], k.ckv_hi[:, t, q], k.ckv_lo[:, t, q],
                                        w_hi[half][:, t, :], w_lo[half][:, t, :], t == 0, t == LT - 1)
                        mm.then_inc(v_mm, 1)

            @block.scalar
            def _(act):
                for half in range(HALVES):
                    act.wait_ge(raw_in[half], 16 * LT)
                    act.activation(w_hi[half][:], raw[half][:], ACT.Copy).then_inc(w_hi_made, 1)
                copy_half(act, lambda to, src: act.activation(to, src, ACT.Copy), 0)
                act.wait_ge(head_in, 16 * 4)
                act.activation(k.wh[:], k.head_raw[:], ACT.Copy).then_inc(head_hi_made, 1)

            @block.vector
            def _(dve):
                for half in range(HALVES):
                    dve.wait_ge(w_hi_made, half + 1)
                    dve.tensor_tensor(w_lo[half][:], raw[half][:], w_hi[half][:].bitcast(F32),
                                      ALU.subtract).then_inc(w_lo_made, 1)
                copy_half(dve, lambda to, src: dve.tensor_copy(to, src), 1)
                dve.wait_ge(head_hi_made, 1)
                dve.tensor_tensor(k.wl[:], k.head_raw[:], k.wh[:].bitcast(F32), ALU.subtract)


def first_weights(k):
    w_uq = k.w_uq.rearrange("o (t p) n -> p (o t) n", p=P)
    w_ukv = k.w_ukv.rearrange("o (t p) n -> p (o t) n", p=P)
    half = ROPE // 2
    return [(k.head_raw[:, :, 0:QH], w_uq[:, :, 0:QH]),
            (k.head_raw[:, :, QH:QH + half], w_uq[:, :, NOPE + half:QH]),
            (k.head_raw[:, :, QH + half:QH + ROPE], w_uq[:, :, NOPE:NOPE + half]),
            (k.head_raw[:, :, 2 * P:3 * P], w_ukv[:, :, 0:NOPE])]


def attention_phase(k):
    nc = k.nc
    QB = TC // P
    ORDER = [0, 3, 1, 2]
    SCALE = float(NOPE + ROPE) ** -0.5
    RING = 5
    BLOCKS = [(g, b) for g in ORDER for b in range(QB)]
    TILES = [(g, j) for g in ORDER for j in range(QB * (g + 1))]
    N_CHUNK = sum(g + 1 for g, _ in BLOCKS)
    N_TILE = len(TILES)
    N_PROJ = 3 * NC_
    LAG = 2
    SLOTS = 3
    first_tile = {g: TILES.index((g, 0)) for g in ORDER}
    chunk_no = {}
    for s, (g, b) in enumerate(BLOCKS):
        for c in range(g + 1):
            chunk_no[s, c] = len(chunk_no)

    size = {g: sum(QB * g + b + 1 for b in range(QB)) for g in ORDER}
    base = {0: 0, 1: 0, 2: size[1], 3: size[1]}
    P_TILES = size[1] + size[3]
    assert size[0] <= size[1]

    def p_at(g, b):
        return base[g] + sum(QB * g + x + 1 for x in range(b))

    def plan():
        ev, waiting, done_t = [], list(range(N_TILE)), 0
        pend = []

        def tiles(n):
            for _ in range(n):
                t = waiting.pop(0)
                ev.append(("T", t))
                pend.append(t)
                if len(pend) > LAG:
                    ev.append(("PV", pend.pop(0)))

        share = {3: [0, 1, 1, 2], 1: [0, 5, 5, 6], 2: [0, 2, 3, 3]}
        for s, (g, b) in enumerate(BLOCKS):
            ev.append(("S", s))
            if s:
                ev.append(("E", s - 1))
            if s == 6:
                ev.append(("W", 0))
            if s in (6, 7):
                ev.append(("VS", s - 4))
            if g in share:
                tiles(share[g][b])
        ev.append(("E", len(BLOCKS) - 1))
        return ev, tiles, pend

    def with_tail(last):
        ev, tiles, pend = plan()
        if last:
            ev.remove(("W", 0))
            tiles(12)
        else:
            ev += [("QN", 0), ("QR", 0), ("K", 0), ("RH", 0), ("QN", 1), ("RL", 0), ("QR", 1)]
            tiles(1)
            ev.append(("RH", 1))
            tiles(1)
            ev += [("RL", 1), ("K", 1)]
            tiles(2)
            ev.append(("K", 2))
            tiles(1)
            ev.append(("VS", 0))
            tiles(1)
            for c in (2, 3):
                ev += [("QN", c), ("QR", c)]
                tiles(1)
                ev.append(("RH", c))
                tiles(1)
                ev.append(("RL", c))
            ev.append(("K", 3))
            tiles(2)
        while pend:
            ev.append(("PV", pend.pop(0)))
        if not last:
            ev.append(("VS", 1))
        return ev

    prologue = []
    for c in range(NC_):
        prologue += [("QN", c), ("QR", c), ("K", c), ("RH", c), ("RL", c)]
    prologue += [("VS", 0), ("VS", 1)]
    order_of = lambda ev: {e: n for n, e in enumerate(x for x in ev if x[0] in ("QN", "QR", "K"))}
    body, last_body = with_tail(False), with_tail(True)

    with ExitStack() as ctx:
        sb = lambda n, s, d: ctx.enter_context(nc.sbuf_tensor(n, s, d))
        sem = lambda n: ctx.enter_context(nc.semaphore(n))
        qlat, raw, wh, wl = k.qlat, k.head_raw, k.wh, k.wl
        qn_hi, qn_lo = sb("qn_hi", [P, S], F32R), sb("qn_lo", [P, S], F32R)
        kn_hi, kn_lo = sb("kn_hi", [P, S], F32R), sb("kn_lo", [P, S], F32R)
        qr = sb("qr", [P, S], F32R)
        v_hi, v_lo = sb("v_hi", [P, S // P, VD], F32R), sb("v_lo", [P, S // P, VD], F32R)
        ra = [sb(f"rope_a{i}", [ROPE, TC], F32) for i in range(2)]
        rb = sb("rope_b", [ROPE, TC], F32)
        v_raw = [sb(f"v_raw{i}", [P, QB, VD], F32) for i in range(2)]
        prob = sb("prob", [P, P_TILES * P], F32)
        pt_hi = [sb(f"pt_hi{i}", [P, TC], F32R) for i in range(SLOTS)]
        pt_lo = [sb(f"pt_lo{i}", [P, TC], F32R) for i in range(SLOTS)]
        bg = sb("bg", [P, TC], F32)
        nmax = sb("nmax", [P, 16, NC_], F32)
        nbias = sb("nbias", [P, 16], F32)
        rsum = sb("rsum", [P, 16, NC_], F32)
        rinv = sb("rinv", [P, 16], F32)
        ps = ctx.enter_context(nc.psum_tensor("ps_ring", [P, RING, TC], F32))
        ps_t = ctx.enter_context(nc.psum_tensor("ps_t", [P, 2, TC], F32))
        ps_o = ctx.enter_context(nc.psum_tensor("ps_o", [P, TC], F32))

        raw_in = sem("head_w_in")
        qlat_in = [sem(f"qlat_in{i}") for i in range(2)]
        bg_in = sem("bg_in")
        v_in = [sem(f"v_in{i}") for i in range(2)]
        v_hi_made, v_lo_made = sem("v_hi_made"), sem("v_lo_made")
        o_out = sem("o_out")
        w_hi_made, w_lo_made = sem("head_w_hi"), sem("head_w_lo")
        proj_mm = sem("proj_mm")
        proj_hi = sem("proj_hi")
        proj_free = sem("proj_free")
        rope_sum = sem("rope_sum")
        rope_hi = sem("rope_hi")
        rope_done = sem("rope_done")
        rope_step = sem("rope_step")
        scores_mm = sem("scores_mm")
        max_step = sem("max_step")
        max_done = sem("max_done")
        exp_done = sem("exp_done")
        sum_step = sem("sum_step")
        rinv_done = sem("rinv_done")
        normed = sem("normed")
        t_done = sem("t_done")
        t_hi, t_lo = sem("t_hi"), sem("t_lo")
        pv_done = sem("pv_done")
        passed = sem("passed")
        o_done = sem("o_done")

        class At:

            def __init__(self, i):
                self.i = i

            def scores(self, n):
                return self.i * N_CHUNK + n

            def block(self, n):
                return self.i * 16 + n

            def tile(self, n):
                return self.i * N_TILE + n

            def values(self, c):
                return self.i * NC_ + c

            def proj(self, n):
                return self.i * N_PROJ + (N_PROJ + n)

        T_CREDIT = 1
        LO_CREDIT = 2
        PV_CREDIT = SLOTS
        O_CREDIT = 1
        O_OUT_CREDIT = 16

        def release(use):
            before = use - RING
            if before < 0:
                total = N_CHUNK + N_PROJ
                before = max(x for x in range(total) if x % RING == use % RING) - total
            return before

        w_uq = k.w_uq.rearrange("o (t p) n -> p (o t) n", p=P)
        w_ukv = k.w_ukv.rearrange("o (t p) n -> p (o t) n", p=P)
        N_RAW = 4
        HALF = ROPE // 2

        with nc.Block() as block:
            @block.sync
            def _(sp):
                sp.sem_inc(o_out, O_OUT_CREDIT)

                def weights(q_cols, kv_cols):
                    sp.dma_start(raw[:, :, 0:QH], w_uq[:, :, bass.ds(q_cols, QH)]).then_inc(raw_in, 16)
                    sp.dma_start(raw[:, :, QH:QH + HALF],
                                 w_uq[:, :, NOPE + HALF:][:, :, bass.ds(q_cols, HALF)]).then_inc(raw_in, 16)
                    sp.dma_start(raw[:, :, QH + HALF:QH + ROPE],
                                 w_uq[:, :, NOPE:][:, :, bass.ds(q_cols, HALF)]).then_inc(raw_in, 16)
                    sp.dma_start(raw[:, :, 2 * P:3 * P], w_ukv[:, :, bass.ds(kv_cols, NOPE)]).then_inc(raw_in, 16)

                def values(rows, c):
                    sp.dma_start(v_raw[c % 2][:], k.v_dram[:, c * QB:(c + 1) * QB][bass.ds(rows, P)]).then_inc(
                        v_in[c % 2], 16)

                def q_chunk(c):
                    sp.dma_start(qlat[c % 2][:].bitcast(F32), k.qlat_dram[c]).then_inc(qlat_in[c % 2], 16)

                def gate(rows, g, n):
                    sp.wait_ge(o_out, n * 16 + O_OUT_CREDIT)
                    sp.sem_inc(passed, 1)
                    sp.dma_start(bg[:], k.bgate_dram[:, g * TC:(g + 1) * TC][bass.ds(rows, P), :]).then_inc(bg_in, 16)

                def store(rows, g, n):
                    sp.wait_ge(o_done, n + 1 + O_CREDIT)
                    sp.dma_start(k.attn_dram[:, g * TC:(g + 1) * TC][bass.ds(rows, P), :], bg[:]).then_inc(o_out, 16)

                sp.sem_inc(raw_in, 16 * N_RAW)
                sp.sem_inc(qlat_in[0], 16)
                sp.sem_inc(qlat_in[1], 16)
                values(0, 0)
                values(0, 1)
                for c in (2, 3):
                    sp.wait_ge(proj_mm, order_of(prologue)["QR", c - 2] + 1)
                    q_chunk(c)

                def head(i, last):
                    rows = sp.snap(i * P) if not last else i * P
                    for c in (2, 3):
                        sp.wait_ge(v_lo_made, At(i).values(c - 2) + 1)
                        sp.sem_inc(passed, 1)
                        values(rows, c)
                    if not last:
                        next_rows = sp.snap(i * P + P)
                        q_cols, kv_cols = sp.snap(i * QH + QH), sp.snap(i * KVH + KVH)
                        sp.wait_ge(w_lo_made, i + 1)
                        weights(q_cols, kv_cols)
                        sp.wait_ge(proj_mm, (i + 1) * N_PROJ)
                        q_chunk(0)
                        q_chunk(1)
                    for n, g in enumerate(ORDER):
                        gate(rows, g, i * QB + n)
                        if n == QB - 1 and not last:
                            for c in (2, 3):
                                sp.wait_ge(proj_mm, At(i).proj(order_of(body)["QR", c - 2] + 1))
                                q_chunk(c)
                        if g == 1 and not last:
                            for c in (0, 1):
                                sp.wait_ge(v_lo_made, At(i).values(c + 2) + 1)
                                sp.sem_inc(passed, 1)
                                values(next_rows, c)
                        store(rows, g, i * QB + n)

                with sp.Fori(0, H - 1) as i:
                    head(i, False)
                head(H - 1, True)
                sp.wait_ge(o_out, H * QB * 16 + O_OUT_CREDIT)

            @block.tensor
            def _(pe):
                def ring_wait(at, use):
                    before = release(use)
                    if 0 <= before < N_CHUNK:
                        pe.wait_ge(exp_done, at.scores(before + 1))
                    elif before >= N_CHUNK:
                        pe.wait_ge(proj_free, at.proj(before - N_CHUNK + 1))
                    else:
                        pe.wait_ge(proj_free, at.proj(before + 1 - 0))

                def project(e, at, n, prol):
                    kind, c = e
                    use = N_CHUNK + n
                    bank = ps[:, use % RING, :]
                    if prol:
                        if n >= RING:
                            pe.wait_ge(proj_free, n - RING + 1)
                    else:
                        ring_wait(at, use)
                    cols = {"QN": 0, "QR": P, "K": 2 * P}[kind]
                    w = slice(cols, cols + P)
                    if kind in ("QN", "QR"):
                        if kind == "QN":
                            pe.wait_ge(qlat_in[c % 2], (c // 2 + 1) * 16 if prol else at.i * 32 + (32 + (c // 2 + 1) * 16))
                        for t in range(LT):
                            mm = split3(pe, bank, wh[:, t, w], wl[:, t, w], qlat[c % 2][:, 0, t, :],
                                        qlat[c % 2][:, 1, t, :], t == 0, t == LT - 1)
                    else:
                        s = slice(c * TC, (c + 1) * TC)
                        for t in range(LT):
                            mm = split3(pe, bank, wh[:, t, w], wl[:, t, w], k.ckv_hi[:, t, s], k.ckv_lo[:, t, s],
                                        t == 0, t == LT - 1)
                    mm.then_inc(proj_mm, 1)

                def scores(at, s):
                    g, b = BLOCKS[s]
                    q = slice((QB * g + b) * P, (QB * g + b + 1) * P)
                    if s == 0:
                        pe.wait_ge(proj_free, at.i * N_PROJ + N_PROJ)
                        pe.wait_ge(rope_done, at.i * NC_ + NC_)
                    for c in range(g + 1):
                        n = chunk_no[s, c]
                        ring_wait(at, n)
                        width = TC if c < g else (b + 1) * P
                        out = ps[:, n % RING, 0:width]
                        ks = slice(c * TC, c * TC + width)
                        pe.matmul(out, qn_hi[:, q], kn_hi[:, ks], start=True, stop=False)
                        pe.matmul(out, qn_hi[:, q], kn_lo[:, ks], start=False, stop=False)
                        pe.matmul(out, qn_lo[:, q], kn_hi[:, ks], start=False, stop=False)
                        pe.matmul(out, qr[:, q], k.kr_hi2[:, ks], start=False, stop=False)
                        mm = pe.matmul(out, qr[0:ROPE, q], k.kr_lo[:, ks], start=False, stop=(c < g))
                        if c == g:
                            mm = pe.matmul(out[:, b * P:(b + 1) * P], k.ident16[:], k.mask[:], start=False, stop=True)
                        mm.then_inc(scores_mm, 1)

                def turn(at, n):
                    g, j = TILES[n]
                    r = max(0, j - QB * g)
                    last_block = BLOCKS.index((g, QB - 1))
                    if j % QB == 0:
                        pe.wait_ge(normed, at.scores(chunk_no[last_block, j // QB] + 1))
                    pe.wait_ge(t_lo, at.tile(n - 1 + LO_CREDIT))
                    for b in range(r, QB):
                        x = (p_at(g, b) + j) * P
                        mm = pe.transpose(ps_t[:, n % 2, b * P:(b + 1) * P], prob[:, x:x + P], k.ident[:])
                    mm.then_inc(t_done, 1)

                def times_v(at, n):
                    g, j = TILES[n]
                    r = max(0, j - QB * g)
                    if j == 0:
                        pe.wait_ge(o_done, at.i * QB + (ORDER.index(g) + O_CREDIT))
                    if j % QB == 0 and (g == 0 or (g == NC_ - 1 and j)):
                        pe.wait_ge(v_lo_made, at.values(j // QB) + 1)
                    pe.wait_ge(t_lo, at.tile(n + 1 + LO_CREDIT))
                    s = slice(r * P, TC)
                    out = ps_o[:, s]
                    mh, ml = pt_hi[n % SLOTS][:, s], pt_lo[n % SLOTS][:, s]
                    pe.matmul(out, v_hi[:, j, :], mh, start=(j == 0), stop=False)
                    pe.matmul(out, v_lo[:, j, :], mh, start=False, stop=False)
                    pe.matmul(out, v_hi[:, j, :], ml, start=False, stop=(j == QB * (g + 1) - 1)).then_inc(pv_done, 1)

                def run(ev, at, prol=False):
                    number = order_of(ev)
                    for e in ev:
                        if e[0] in ("QN", "QR", "K"):
                            if number[e] == 0 and not prol:
                                pe.wait_ge(w_lo_made, at.i + 2)
                            project(e, at, number[e], prol)
                        elif e[0] == "S":
                            scores(at, e[1])
                        elif e[0] == "T":
                            turn(at, e[1])
                        elif e[0] == "PV":
                            times_v(at, e[1])

                run(prologue, At(-1), prol=True)
                with pe.Fori(0, H - 1) as i:
                    run(body, At(i))
                run(last_body, At(H - 1))

            @block.scalar
            def _(act):
                def run(ev, at, prol=False):
                    number = order_of(ev)
                    for kind, n in ev:
                        if kind == "W":
                            act.wait_ge(raw_in, at.i * (16 * N_RAW) + 32 * N_RAW)
                            act.wait_ge(proj_mm, at.i * N_PROJ + N_PROJ)
                            act.activation(wh[:], raw[:], ACT.Copy).then_inc(w_hi_made, 1)
                        elif kind in ("QN", "K"):
                            m = number[kind, n]
                            bank = ps[:, (N_CHUNK + m) % RING, :]
                            s = slice(n * TC, (n + 1) * TC)
                            act.wait_ge(proj_mm, m + 1 if prol else at.proj(m + 1))
                            if kind == "QN":
                                ins = act.activation(qn_hi[:, s], bank, ACT.Copy, scale=SCALE)
                            else:
                                ins = act.activation(kn_hi[:, s], bank, ACT.Copy)
                            ins.then_inc(proj_hi, 1)
                        elif kind == "RH":
                            act.wait_ge(rope_sum, n + 1 if prol else at.i * NC_ + (NC_ + n + 1))
                            act.activation(qr[0:ROPE, n * TC:(n + 1) * TC], ra[n % 2][:], ACT.Copy).then_inc(rope_hi, 1)
                        elif kind == "VS":
                            i = at.i + 1 if n < 2 else at.i
                            act.wait_ge(v_in[n % 2], i * 32 + 16 * (n // 2 + 1))
                            if not prol:
                                act.wait_ge(pv_done, at.tile((TILES.index((2, n * QB + QB - 1)) + 1 if n < 2 else 0)
                                                             + PV_CREDIT))
                            act.activation(v_hi[:, n * QB:(n + 1) * QB, :], v_raw[n % 2][:],
                                           ACT.Copy).then_inc(v_hi_made, 1)
                        elif kind == "E":
                            g, b = BLOCKS[n]
                            act.wait_ge(max_done, at.block(n + 1))
                            if b == 0:
                                held = {0: 0, 3: 0, 1: first_tile[3], 2: first_tile[1]}[g]
                                act.wait_ge(t_done, at.tile(held + T_CREDIT))
                            for c in range(g + 1):
                                width = TC if c < g else (b + 1) * P
                                x = (p_at(g, b) + c * QB) * P
                                act.activation(prob[:, x:x + width], ps[:, chunk_no[n, c] % RING, 0:width], ACT.Exp,
                                               bias=nbias[:, n:n + 1],
                                               accum_out=rsum[:, n, c:c + 1]).then_inc(exp_done, 1)
                        elif kind == "T":
                            g, j = TILES[n]
                            s = slice(max(0, j - QB * g) * P, TC)
                            act.wait_ge(pv_done, at.tile(n + 1 - SLOTS + PV_CREDIT))
                            act.wait_ge(t_done, at.tile(n + 1 + T_CREDIT))
                            act.activation(pt_hi[n % SLOTS][:, s], ps_t[:, n % 2, s], ACT.Copy).then_inc(t_hi, 1)

                run(prologue, At(-1), prol=True)
                with act.Fori(0, H - 1) as i:
                    run(body, At(i))
                run(last_body, At(H - 1))

            @block.vector
            def _(dve):
                dve.sem_inc(t_lo, LO_CREDIT)
                dve.sem_inc(o_done, O_CREDIT)

                def run(ev, at, prol=False):
                    number = order_of(ev)
                    for kind, n in ev:
                        if kind in ("QN", "K"):
                            m = number[kind, n]
                            bank = ps[:, (N_CHUNK + m) % RING, :]
                            s = slice(n * TC, (n + 1) * TC)
                            hi_no = sum(1 for e, x in number.items() if e[0] != "QR" and x <= m)
                            per = N_PROJ - NC_
                            dve.wait_ge(proj_hi, hi_no if prol else at.i * per + (per + hi_no))
                            if kind == "QN":
                                ins = dve.scalar_tensor_tensor(qn_lo[:, s], bank, SCALE, qn_hi[:, s].bitcast(F32),
                                                               ALU.mult, ALU.subtract)
                            else:
                                ins = dve.tensor_tensor(kn_lo[:, s], bank, kn_hi[:, s].bitcast(F32), ALU.subtract)
                            ins.then_inc(proj_free, 1)
                        elif kind == "QR":
                            m = number[kind, n]
                            bank = ps[:, (N_CHUNK + m) % RING, :]
                            s = slice(n * TC, (n + 1) * TC)
                            a = ra[n % 2]
                            if n >= 2 or not prol:
                                dve.wait_ge(rope_done, n - 1 if prol else at.i * NC_ + (NC_ + n - 1))
                            dve.wait_ge(proj_mm, m + 1 if prol else at.proj(m + 1))
                            dve.scalar_tensor_tensor(a[:], bank[0:ROPE, :], SCALE, k.trig[0:ROPE, s],
                                                     ALU.mult, ALU.mult)
                            dve.scalar_tensor_tensor(rb[:], bank[ROPE:P, :], SCALE, k.trig[ROPE:P, s],
                                                     ALU.mult, ALU.mult).then_inc(proj_free, 1)
                            dve.wait_ge(proj_free, m + 1 if prol else at.proj(m + 1))
                            dve.tensor_tensor(a[:], a[:], rb[:], ALU.add).then_inc(rope_sum, 1)
                        elif kind == "RL":
                            s = slice(n * TC, (n + 1) * TC)
                            dve.wait_ge(rope_hi, n + 1 if prol else at.i * NC_ + (NC_ + n + 1))
                            dve.tensor_tensor(qr[ROPE:P, s], ra[n % 2][:], qr[0:ROPE, s].bitcast(F32),
                                              ALU.subtract).then_inc(rope_done, 1)
                        elif kind == "S":
                            g, b = BLOCKS[n]
                            for c in range(g + 1):
                                width = TC if c < g else (b + 1) * P
                                to = nmax[:, n, c:c + 1] if g else nbias[:, n:n + 1]
                                dve.wait_ge(scores_mm, at.scores(chunk_no[n, c] + 1))
                                ins = dve.tensor_reduce(to, ps[:, chunk_no[n, c] % RING, 0:width], AX.X, ALU.max,
                                                        negate=True)
                                ins.then_inc(max_step if g else max_done, 1)
                            if g:
                                n_max = chunk_no[n, g] + 1 - QB
                                dve.wait_ge(max_step, at.i * (N_CHUNK - QB) + n_max)
                                dve.tensor_reduce(nbias[:, n:n + 1], nmax[:, n, 0:g + 1], AX.X,
                                                  ALU.min).then_inc(max_done, 1)
                        elif kind == "E":
                            g, b = BLOCKS[n]
                            dve.wait_ge(exp_done, at.scores(chunk_no[n, g] + 1))
                            if g:
                                dve.tensor_reduce(rinv[:, n:n + 1], rsum[:, n, 0:g + 1], AX.X,
                                                  ALU.add).then_inc(sum_step, 1)
                                dve.wait_ge(sum_step, at.i * (16 - QB) + (n + 1 - QB))
                                src = rinv[:, n:n + 1]
                            else:
                                src = rsum[:, n, 0:1]
                            dve.reciprocal(rinv[:, n:n + 1], src).then_inc(rinv_done, 1)
                        elif kind == "T":
                            g, j = TILES[n]
                            s = slice(max(0, j - QB * g) * P, TC)
                            dve.wait_ge(t_hi, at.tile(n + 1))
                            dve.tensor_tensor(pt_lo[n % SLOTS][:, s], ps_t[:, n % 2, s],
                                              pt_hi[n % SLOTS][:, s].bitcast(F32), ALU.subtract).then_inc(t_lo, 1)
                        elif kind == "PV":
                            g, j = TILES[n]
                            if j == QB * (g + 1) - 1:
                                m = ORDER.index(g)
                                dve.wait_ge(pv_done, at.tile(n + 1 + PV_CREDIT))
                                dve.wait_ge(bg_in, at.i * (16 * QB) + 16 * (m + 1))
                                dve.tensor_tensor(bg[:], ps_o[:], bg[:], ALU.mult).then_inc(o_done, 1)

                run(prologue, At(-1), prol=True)
                with dve.Fori(0, H - 1) as i:
                    run(body, At(i))
                run(last_body, At(H - 1))

            @block.gpsimd
            def _(pool):
                pool.sem_inc(w_hi_made, 1)
                pool.sem_inc(w_lo_made, 1)
                pool.sem_inc(t_done, T_CREDIT)
                pool.sem_inc(pv_done, PV_CREDIT)

                def run(ev, at, prol=False):
                    for kind, n in ev:
                        if kind == "W":
                            pool.wait_ge(w_hi_made, at.i + 2)
                            pool.tensor_tensor(wl[:], raw[:], wh[:].bitcast(F32), ALU.subtract).then_inc(w_lo_made, 1)
                        elif kind == "VS":
                            i = at.i + 1 if n < 2 else at.i
                            pool.wait_ge(v_hi_made, i * NC_ + n + 1)
                            v = slice(n * QB, (n + 1) * QB)
                            pool.tensor_tensor(v_lo[:, v, :], v_raw[n % 2][:], v_hi[:, v, :].bitcast(F32),
                                               ALU.subtract).then_inc(v_lo_made, 1)
                        elif kind == "E":
                            g, b = BLOCKS[n]
                            pool.wait_ge(rinv_done, at.block(n + 1))
                            pool.sem_inc(passed, 1)
                            for c in range(g + 1):
                                width = TC if c < g else (b + 1) * P
                                x = (p_at(g, b) + c * QB) * P
                                pool.tensor_scalar(prob[:, x:x + width], prob[:, x:x + width], rinv[:, n:n + 1], 1.0,
                                                   ALU.mult, ALU.mult).then_inc(normed, 1)

                run(prologue, At(-1), prol=True)
                with pool.Fori(0, H - 1) as i:
                    run(body, At(i))
                run(last_body, At(H - 1))


def output_phase(k):
    nc = k.nc
    N = NC_
    BANKS = 6
    SL = 3
    U_CONV, U_END = N * KT, 2 * N * KT
    PER = TC // P
    TT = S // P
    XS = 4
    HALF = KT // 2
    FINAL = [(i, h) for h in range(2) for i in range(PER)] + [(i, h) for i in range(PER, TT) for h in range(2)]

    SOURCE_AT = {1: (0, 0), **{c: (c - 2, 4) for c in range(2, N + 1)},
                 N + 1: (N - 1, 4), **{c: (c - 2, 6) for c in range(N + 2, 2 * N + 2)}}
    STEPS = ["total", "centre", "squares", "scale", "lo_first", "lo_last"]
    STEP_AT = {(N - 2 + n, m): (N, s) for s, (n, m) in zip(STEPS, [(0, 6), (0, 7), (1, 0), (1, 2), (1, 4), (1, 5)])}
    MEAN_AT = {(N - 2, 7): (N, 0), (N - 1, 1): (N, 1)}
    for c in range(N + 1, 2 * N):
        STEP_AT.update({(c - 1, m): (c, s) for s, m in zip(STEPS, [0, 1, 2, 3, 5, 6])})
        MEAN_AT.update({(c - 1, 1): (c, 0), (c - 1, 3): (c, 1)})
    with ExitStack() as ctx:
        sb = lambda n, s, d: ctx.enter_context(nc.sbuf_tensor(n, s, d))
        sem = lambda n: ctx.enter_context(nc.semaphore(n))
        raw = [sb(f"o_raw{i}", [P, KT, P], F32) for i in range(2)]
        w_hi, w_lo = sb("o_w_hi", [P, KT, D], F32R), sb("o_w_lo", [P, KT, D], F32R)
        v = sb("o_v", [P, KT, TC], F32)
        z = sb("o_z", [P, KT, TC], F32)
        ag = sb("o_ag", [P, KT, TC], F32)
        a_hi = [sb(f"o_a_hi{i}", [P, KT, TC], F32R) for i in range(2)]
        a_lo = [sb(f"o_a_lo{i}", [P, KT, TC], F32R) for i in range(2)]
        tot = sb("o_tot", [P, TC], F32)
        g = [sb(f"o_g{i}", [P, TC], F32) for i in range(SL)]
        yb = [sb(f"o_yb{i}", [P, TC], F32) for i in range(SL)]
        y = [sb(f"o_y{i}", [P, TC], F32) for i in range(SL)]
        ss = sb("o_ss", [P, TT], F32)
        ps = ctx.enter_context(nc.psum_tensor("o_ps", [P, BANKS, TC], F32))
        ps_m = ctx.enter_context(nc.psum_tensor("o_ps_m", [P, 2, TC], F32))
        gate_row, norm_row = (r[:].rearrange("p t n -> p (t n)") for r in raw)
        x = [ag[:, 2 * i:2 * i + 2, :].rearrange("p t n -> p (t n)") for i in range(XS)]
        res = [z[:, 2 * i:2 * i + 2, :].rearrange("p t n -> p (t n)") for i in range(XS)]
        rstd, sq = tot, tot[:].bitcast(BF16)

        raw_in = [sem(f"o_raw_in{i}") for i in range(2)]
        hi_made, lo_made = sem("o_w_hi_made"), sem("o_w_lo_made")
        v_in = [sem(f"o_v_in{i}") for i in range(2)]
        ag_in = sem("o_ag_in")
        g_in = [sem(f"o_g_in{i}") for i in range(SL)]
        y_out = [sem(f"o_y_out{i}") for i in range(SL)]
        summed = sem("o_summed")
        mean_mm = sem("o_mean_mm")
        centred = sem("o_centred")
        squared = sem("o_squared")
        scaled = sem("o_scaled")
        rooted = sem("o_rooted")
        inverted = sem("o_inverted")
        silu_done = sem("o_silu_done")
        z_done = sem("o_z_done")
        hi_done, lo_done = sem("o_a_hi_done"), sem("o_a_lo_done")
        tile_mm = sem("o_tile_mm")
        bank_read = sem("o_bank_read")
        y_added = sem("o_y_added")
        rows_in = [sem(f"o_rows_in{i}") for i in range(2)]
        x_in = [sem(f"o_x_in{i}") for i in range(XS)]
        res_out = [sem(f"o_res_out{i}") for i in range(XS)]
        added = sem("o_added")
        row_squared = sem("o_row_squared")
        row_rooted = sem("o_row_rooted")
        row_inverted = sem("o_row_inverted")
        res_done = sem("o_res_done")

        by_tile = lambda ap: ap.rearrange("(t p) s -> p t s", p=P)
        weights = [ap.rearrange("o (t p) n -> p (o t) n", p=P) for ap in (k.w_attn_out, k.w_conv_out, k.w_out)]
        sources = [by_tile(ap) for ap in (k.attn_dram, k.conv_dram, k.merged_dram)]
        chunk = lambda n: slice(n * TC, (n + 1) * TC)
        cols = lambda m: slice(m * P, (m + 1) * P)
        x_rows = k.x.rearrange("o (n p) d -> (o n) p d", p=P)
        out_rows = k.out.rearrange("o (n p) d -> (o n) p d", p=P)
        is_conv = lambda c: N <= c < 2 * N

        def g_count(u):
            return sum(16 if t < U_CONV else 32 for t in range(u % SL, u + 1, SL))

        with nc.Block() as block:
            @block.sync
            def _(sp):
                def piece(w, m):
                    n = w * KT + m
                    if n >= 2:
                        sp.wait_ge(lo_made, n - 1)
                    sp.dma_start(raw[m % 2][:], weights[w][:, :, cols(m)]).then_inc(raw_in[m % 2], 16)

                def source(c):
                    for h in range(2):
                        t = slice(h * HALF, (h + 1) * HALF)
                        sp.dma_start(v[:, t, :], sources[c // N][:, t, chunk(c % N)]).then_inc(v_in[h], 16)

                def gate_source(c):
                    sp.dma_start(ag[:], by_tile(k.agate_dram)[:, :, chunk(c - N)]).then_inc(ag_in, 16)

                def gates(u):
                    if u >= SL:
                        sp.wait_ge(bank_read, u - SL + 1)
                    if u - SL >= U_CONV:
                        sp.wait_ge(y_added, u - SL - U_CONV + 1)
                    n, m = divmod(u, KT)
                    rows, s = slice(m * P, (m + 1) * P), chunk(n % N)
                    sp.dma_start(g[u % SL][:], (k.gb_dram if n < N else k.ga_dram)[rows, s]).then_inc(g_in[u % SL], 16)
                    if n >= N:
                        o = u - U_CONV
                        sp.wait_ge(y_out[o % SL], 16 * (o // SL + 1))
                        sp.dma_start(yb[u % SL][:], k.yb_dram[rows, s]).then_inc(g_in[u % SL], 16)

                def load_x(i):
                    sp.dma_start(x[i % XS], x_rows[i]).then_inc(x_in[i % XS], 16)

                piece(0, 0)
                source(0)
                piece(0, 1)
                gates(0)
                gates(1)
                for m in range(2, KT):
                    piece(0, m)
                for u in range(U_END):
                    n, m = divmod(u, KT)
                    for c in range(1, 2 * N + 2):
                        if SOURCE_AT[c] == (n, m):
                            if is_conv(c - 1):
                                sp.wait_ge(silu_done, KT * (c - N))
                            else:
                                sp.wait_ge(lo_done, KT * c)
                            if c >= 2 * N:
                                for s in range(SL):
                                    sp.wait_ge(y_out[s], 16 * len(range(s, (c - N + 1) * KT, SL)))
                            source(c)
                            if c == N:
                                gate_source(c)
                    if m == KT - 1 and is_conv(n + 1):
                        sp.wait_ge(z_done, KT * (n + 2 - N))
                        if is_conv(n + 2):
                            gate_source(n + 2)
                        else:
                            for i in range(XS):
                                load_x(i)
                    if n == N - 1 and 3 <= m < 3 + HALF:
                        piece(1, 2 * (m - 3))
                        piece(1, 2 * (m - 3) + 1)
                    if n == 2 * N - 1:
                        if m == 0:
                            piece(2, 0)
                        if m + 1 < KT:
                            piece(2, m + 1)
                    if u + 2 < U_END:
                        gates(u + 2)
                    if n < N:
                        sp.wait_ge(bank_read, u + 1)
                    else:
                        sp.wait_ge(y_added, u - U_CONV + 1)
                    sp.dma_start((k.yb_dram if n < N else k.merged_dram)[m * P:(m + 1) * P, chunk(n % N)],
                                 y[u % SL][:]).then_inc(y_out[u % SL], 16)

                sp.wait_ge(lo_made, 3 * KT - 1)
                sp.dma_start(gate_row, k.gate_dram).then_inc(rows_in[0], 16)
                sp.wait_ge(lo_made, 3 * KT)
                sp.dma_start(norm_row, k.final_norm_w.rearrange("(o d) -> o d", o=1).to_broadcast([P, D])).then_inc(
                    rows_in[1], 16)
                for s in range(SL):
                    sp.wait_ge(y_out[s], 16 * len(range(s, U_END, SL)))
                for i in range(TT):
                    c = 2 * N + i // PER
                    if i % PER == 1 and c + 2 < 3 * N:
                        sp.wait_ge(lo_done, KT * (c + 2))
                        source(c + 2)
                    if i >= 1 and i + XS - 1 < TT:
                        sp.wait_ge(added, i)
                        load_x(i + XS - 1)
                    sp.wait_ge(res_done, i + 1)
                    sp.dma_start(out_rows[i], res[i % XS]).then_inc(res_out[i % XS], 16)
                for s in range(XS):
                    sp.wait_ge(res_out[s], 16 * TT // XS)

            @block.tensor
            def _(pe):
                def mean(c, which):
                    j = c - N
                    pe.wait_ge(summed, 2 * j + which + 1)
                    if j:
                        pe.wait_ge(rooted if which else centred, j if which else 2 * j)
                    pe.matmul(ps_m[:, which, :], k.mean_mat[:], tot[:], start=True, stop=True).then_inc(mean_mm, 1)

                for u in range(U_END):
                    n, m = divmod(u, KT)
                    if n % N == 0:
                        pe.wait_ge(lo_made, n // N * KT + m + 1)
                    if u >= BANKS:
                        pe.wait_ge(bank_read, u - BANKS + 1)
                    for t in range(KT):
                        if m == 0:
                            pe.wait_ge(lo_done, n * KT + t + 1)
                        mm = split3(pe, ps[:, u % BANKS, :], w_hi[:, t, cols(m)], w_lo[:, t, cols(m)],
                                    a_hi[n % 2][:, t, :], a_lo[n % 2][:, t, :], t == 0, t == KT - 1)
                        if t == HALF - 1 and (n, m) in MEAN_AT:
                            mean(*MEAN_AT[n, m])
                    mm.then_inc(tile_mm, 1)
                for f, (i, half) in enumerate(FINAL):
                    u = U_END + f
                    n = 2 * N + i // PER
                    q, s = slice(i % PER * P, (i % PER + 1) * P), slice(half * TC, (half + 1) * TC)
                    if n == 2 * N and i == 0:
                        pe.wait_ge(lo_made, 2 * KT + (half + 1) * HALF)
                    pe.wait_ge(bank_read, u - BANKS + 1)
                    for t in range(KT):
                        if i % PER == 0 and half == 0:
                            pe.wait_ge(lo_done, n * KT + t + 1)
                        mm = split3(pe, ps[:, u % BANKS, :], a_hi[n % 2][:, t, q], a_lo[n % 2][:, t, q],
                                    w_hi[:, t, s], w_lo[:, t, s], t == 0, t == KT - 1)
                    mm.then_inc(tile_mm, 1)

            @block.scalar
            def _(act):
                def weight_hi(w, m):
                    n = w * KT + m
                    act.wait_ge(raw_in[m % 2], 16 * (n // 2 + 1))
                    if w:
                        act.wait_ge(tile_mm, (w * N - 1) * KT + m + 1)
                    act.activation(w_hi[:, :, cols(m)], raw[m % 2][:], ACT.Copy).then_inc(hi_made, 1)

                def operand_hi(c, t, src):
                    if c >= 2 and t == 0:
                        act.wait_ge(tile_mm, KT * (c - 1))
                    act.activation(a_hi[c % 2][:, t, :], src[:, t, :], ACT.Copy).then_inc(hi_done, 1)

                def split_hi(c, ts):
                    for t in ts:
                        act.wait_ge(v_in[t // HALF], 16 * (c + 1))
                        operand_hi(c, t, v)

                def conv_operand(c):
                    j = c - N
                    for h in range(2):
                        t = slice(h * HALF, (h + 1) * HALF)
                        act.wait_ge(centred, 2 * j + h + 1)
                        if j and h == 0:
                            act.wait_ge(lo_done, KT * c)
                        act.activation(z[:, t, :], v[:, t, :], ACT.Square).then_inc(squared, 1)
                    act.wait_ge(mean_mm, 2 * j + 2)
                    act.activation(rstd[:], ps_m[:, 1, :], ACT.Sqrt, bias=k.eps[:]).then_inc(rooted, 1)
                    for t in range(KT):
                        act.wait_ge(scaled, 2 * j + t // HALF + 1)
                        act.activation(z[:, t, :], v[:, t, :], ACT.Silu, scale=k.prm_t[:, R_LNW + t:R_LNW + t + 1],
                                       bias=k.prm_t[:, R_LNB + t:R_LNB + t + 1]).then_inc(silu_done, 1)
                    for t in range(KT):
                        act.wait_ge(z_done, j * KT + t + 1)
                        operand_hi(c, t, z)

                weight_hi(0, 0)
                split_hi(0, range(KT))
                for m in range(1, KT):
                    weight_hi(0, m)
                for c in range(1, 2 * N + 1):
                    if is_conv(c):
                        conv_operand(c)
                    else:
                        split_hi(c, range(KT))
                    if c % N == 0:
                        for m in range(KT):
                            weight_hi(c // N, m)
                for i in range(TT):
                    c = 2 * N + i // PER
                    if i % PER == 0 and c + 1 < 3 * N:
                        split_hi(c + 1, range(KT))
                    act.wait_ge(added, i + 1)
                    if i:
                        act.wait_ge(row_squared, i)
                    act.activation(sq, res[i % XS], ACT.Square, accum_out=ss[:, i:i + 1]).then_inc(row_squared, 1)
                    act.wait_ge(row_squared, i + 1)
                    act.activation(ss[:, i:i + 1], ss[:, i:i + 1], ACT.Sqrt, scale=1.0 / D,
                                   bias=k.eps[:]).then_inc(row_rooted, 1)

            @block.gpsimd
            def _(pool):
                def weight_lo(w, m):
                    pool.wait_ge(hi_made, w * KT + m + 1)
                    pool.tensor_tensor(w_lo[:, :, cols(m)], raw[m % 2][:], w_hi[:, :, cols(m)].bitcast(F32),
                                       ALU.subtract).then_inc(lo_made, 1)

                def gate_z(c, ts):
                    pool.wait_ge(ag_in, 16 * (c - N + 1))
                    for t in ts:
                        pool.wait_ge(silu_done, (c - N) * KT + t + 1)
                        pool.tensor_tensor(z[:, t, :], z[:, t, :], ag[:, t, :], ALU.mult).then_inc(z_done, 1)

                for m in range(KT):
                    weight_lo(0, m)
                gate_z(N, range(KT))
                for m in range(KT):
                    weight_lo(1, m)
                for u in range(U_CONV, U_END):
                    n, m = divmod(u, KT)
                    s = u % SL
                    pool.wait_ge(g_in[s], g_count(u))
                    pool.wait_ge(bank_read, u + 1)
                    pool.tensor_tensor(y[s][:], y[s][:], yb[s][:], ALU.add).then_inc(y_added, 1)
                    if is_conv(n + 1):
                        gate_z(n + 1, {2: (0, 1), 3: (2, 3, 4, 5), 4: (6, 7)}.get(m, ()))
                    else:
                        weight_lo(2, m)
                for i in range(TT):
                    pool.wait_ge(x_in[i % XS], 16 * (i // XS + 1))
                    pool.wait_ge(bank_read, U_END + FINAL.index((i, 1)) + 1)
                    pool.tensor_tensor(res[i % XS], res[i % XS], x[i % XS], ALU.add).then_inc(added, 1)

            @block.vector
            def _(dve):
                wide = lambda ap: ap.unsqueeze(1).to_broadcast([P, HALF, TC])

                def total(j, which, src):
                    if j or which:
                        dve.wait_ge(mean_mm, 2 * j + which)
                    if j and not which:
                        dve.wait_ge(scaled, 2 * j)
                    dve.tensor_reduce(tot[:], src[:].rearrange("p t s -> p s t"), AX.X, ALU.add).then_inc(summed, 1)

                def operand_lo(c, ts):
                    src = z if is_conv(c) else v
                    for t in ts:
                        dve.wait_ge(hi_done, c * KT + t + 1)
                        dve.tensor_tensor(a_lo[c % 2][:, t, :], src[:, t, :], a_hi[c % 2][:, t, :].bitcast(F32),
                                          ALU.subtract).then_inc(lo_done, 1)

                def conv_step(c, step):
                    j = c - N
                    if step == "total":
                        for h in range(2):
                            dve.wait_ge(v_in[h], 16 * (c + 1))
                        total(j, 0, v)
                    elif step == "centre":
                        dve.wait_ge(mean_mm, 2 * j + 1)
                        for h in range(2):
                            t = slice(h * HALF, (h + 1) * HALF)
                            dve.tensor_tensor(v[:, t, :], v[:, t, :], wide(ps_m[:, 0, :]),
                                              ALU.subtract).then_inc(centred, 1)
                    elif step == "squares":
                        dve.wait_ge(squared, 2 * j + 2)
                        total(j, 1, z)
                    elif step == "scale":
                        dve.wait_ge(rooted, j + 1)
                        dve.reciprocal(rstd[:], rstd[:]).then_inc(inverted, 1)
                        dve.wait_ge(inverted, j + 1)
                        for h in range(2):
                            t = slice(h * HALF, (h + 1) * HALF)
                            dve.tensor_tensor(v[:, t, :], v[:, t, :], wide(rstd[:]), ALU.mult).then_inc(scaled, 1)
                    else:
                        operand_lo(c, range(HALF) if step == "lo_first" else range(HALF, KT))

                operand_lo(0, range(KT))
                for u in range(U_END):
                    n, m = divmod(u, KT)
                    if (n, m) in STEP_AT:
                        conv_step(*STEP_AT[n, m])
                    if not is_conv(n + 1) and m == 3:
                        operand_lo(n + 1, range(KT))
                    dve.wait_ge(tile_mm, u + 1)
                    dve.wait_ge(g_in[u % SL], g_count(u))
                    if u >= SL:
                        dve.wait_ge(y_out[u % SL], 16 * (u // SL))
                    dve.tensor_tensor(y[u % SL][:], ps[:, u % BANKS, :], g[u % SL][:], ALU.mult).then_inc(bank_read, 1)

                def finish(i):
                    dve.wait_ge(row_rooted, i + 1)
                    dve.reciprocal(ss[:, i:i + 1], ss[:, i:i + 1]).then_inc(row_inverted, 1)
                    dve.wait_ge(row_inverted, i + 1)
                    dve.wait_ge(rows_in[1], 16)
                    dve.scalar_tensor_tensor(res[i % XS], res[i % XS], ss[:, i:i + 1], norm_row,
                                             ALU.mult, ALU.mult).then_inc(res_done, 1)

                finished = 0
                dve.wait_ge(rows_in[0], 16)
                for f, (i, half) in enumerate(FINAL):
                    u = U_END + f
                    dve.wait_ge(tile_mm, u + 1)
                    if i >= XS and half == 0:
                        dve.wait_ge(res_out[i % XS], 16 * (i // XS))
                    s = slice(half * TC, (half + 1) * TC)
                    dve.tensor_tensor(res[i % XS][:, s], ps[:, u % BANKS, :], gate_row[:, s],
                                      ALU.mult).then_inc(bank_read, 1)
                    if f >= 1 and FINAL[f - 1][1] == 1:
                        finish(finished)
                        finished += 1
                    if f % KT == 3 and f // KT + 1 < N:
                        operand_lo(2 * N + f // KT + 1, range(KT))
                finish(finished)


PHASES = ["setup", "proj", "value", "attn", "output"]


def build(nc, ins, out, phases=PHASES):
    with ExitStack() as ctx:
        k = Kernel(nc, ctx, ins, out)
        with ExitStack() as hctx:
            k.h_hi = hctx.enter_context(nc.sbuf_tensor("h_hi", [P, KT, S], F32R))
            k.h_lo = hctx.enter_context(nc.sbuf_tensor("h_lo", [P, KT, S], F32R))
            if "setup" in phases:
                setup_phase(k)
            if "proj" in phases:
                projection_phase(k)
        with ExitStack() as actx:
            k.ckv_hi = actx.enter_context(nc.sbuf_tensor("ckv_hi", [P, LT, S], F32R))
            k.ckv_lo = actx.enter_context(nc.sbuf_tensor("ckv_lo", [P, LT, S], F32R))
            k.kr_hi2 = actx.enter_context(nc.sbuf_tensor("kr_hi2", [P, S], F32R))
            k.kr_lo = actx.enter_context(nc.sbuf_tensor("kr_lo", [ROPE, S], F32R))
            k.trig = actx.enter_context(nc.sbuf_tensor("trig", [P, S], F32))
            k.qlat = [actx.enter_context(nc.sbuf_tensor(f"qlat{i}", [P, 2, LT, TC], F32R)) for i in range(2)]
            k.head_raw = actx.enter_context(nc.sbuf_tensor("head_raw", [P, LT, 3 * P], F32))
            k.wh = actx.enter_context(nc.sbuf_tensor("head_w_h", [P, LT, 3 * P], F32R))
            k.wl = actx.enter_context(nc.sbuf_tensor("head_w_l", [P, LT, 3 * P], F32R))
            if "value" in phases:
                value_phase(k)
            if "attn" in phases:
                attention_phase(k)
        if "output" in phases:
            output_phase(k)


_INS = ["x", "c", "positions", "w_ada", "b_ada", "norm_w", "w_in", "conv_w", "conv_b", "conv_ln_w", "conv_ln_b",
        "w_conv_out", "q_norm_w", "w_uq", "kv_norm_w", "w_ukv", "w_attn_out", "w_out", "final_norm_w"]


def _freqs():
    import numpy as np

    f = np.float32(10000.0) ** (-np.arange(0, 64, 2, dtype=np.float32) / np.float32(64))
    sign = np.repeat(np.array([1, 1, -1, 1], np.float32), 32)
    return np.ascontiguousarray(np.stack([np.tile(f, 4), sign], axis=1).astype(np.float32))


def kernel(**inputs):
    import numpy as _np
    import concourse.bacc as _bacc
    from concourse import mybir as _mybir
    from concourse.bass_utils import run_bass_kernel_spmd as _run

    nc = _bacc.Bacc("TRN2", target_bir_lowering=False, num_devices=1)
    arrays, ins = {}, {}
    for name in _INS:
        arrays[f"in_{name}_dram"] = _np.ascontiguousarray(inputs[name])
    arrays["in_freqs_dram"] = _freqs()
    for name in _INS + ["freqs"]:
        a = arrays[f"in_{name}_dram"]
        ins[name] = nc.dram_tensor(f"in_{name}_dram", a.shape, _mybir.dt.from_np(a.dtype), kind="ExternalInput").ap()
    out = nc.dram_tensor("out_0_dram", (1, S, D), _mybir.dt.float32, kind="ExternalOutput").ap()
    build(nc, ins, out)
    r = _run(nc, [arrays], core_ids=[0])
    return r.results[0]["out_0_dram"]
```

```python
from contextlib import ExitStack

import concourse.bass as bass
from concourse import mybir

ALU = mybir.AluOpType
ACT = mybir.ActivationFunctionType
AX = mybir.AxisListType
F32 = mybir.dt.float32
F32R = mybir.dt.float32r
BF16 = mybir.dt.bfloat16
I32 = mybir.dt.int32

P = 128
D = 1024
KT = D // P
S = 2048
TC = 512
NC_ = S // TC
TAPS = 31
H = 8
NOPE, ROPE, VD = 128, 64, 128
LAT = 256
LT = LAT // P
CONVW = 1024
C_VAL, C_GLU, C_AGATE = 0, CONVW, 2 * CONVW
C_CQ = 3 * CONVW
C_CKV = C_CQ + LAT
C_KPE = C_CKV + LAT
C_BGATE = C_KPE + ROPE
C_GA = C_BGATE + D
C_GB = C_GA + D
QH = NOPE + ROPE
KVH = NOPE + VD
EPS = 1e-6
NEG = -1e30

R_C, R_NORM, R_BADA, R_CONVB, R_LNW, R_LNB, R_QN, R_KVN, R_END = 0, 8, 16, 40, 48, 56, 64, 66, 68


def split3(pe, out, wh, wl, xh, xl, first, last):
    pe.matmul(out, wh, xh, start=first, stop=False)
    pe.matmul(out, wh, xl, start=False, stop=False)
    return pe.matmul(out, wl, xh, start=False, stop=last)


class Kernel:

    def __init__(self, nc, ctx, ins, out):
        self.nc, self.out = nc, out
        self.x, self.c, self.positions, self.freqs = ins["x"], ins["c"], ins["positions"], ins["freqs"]
        self.w_ada, self.b_ada, self.norm_w, self.w_in = ins["w_ada"], ins["b_ada"], ins["norm_w"], ins["w_in"]
        self.conv_w, self.conv_b = ins["conv_w"], ins["conv_b"]
        self.conv_ln_w, self.conv_ln_b = ins["conv_ln_w"], ins["conv_ln_b"]
        self.q_norm_w, self.kv_norm_w, self.w_uq, self.w_ukv = (
            ins["q_norm_w"], ins["kv_norm_w"], ins["w_uq"], ins["w_ukv"])
        self.w_conv_out, self.w_attn_out, self.w_out = ins["w_conv_out"], ins["w_attn_out"], ins["w_out"]
        self.final_norm_w = ins["final_norm_w"]

        dram = lambda n, s, d: nc.dram_tensor(n, s, d).ap()
        self.gate_dram = dram("gate_dram", [P, D], F32)
        self.ckv_dram = dram("ckv_dram", [2, P, LT, S], F32)
        self.kr_dram = dram("kr_dram", [2, ROPE, S], F32)
        self.trig_dram = dram("trig_dram", [P, S], F32)
        self.agate_dram = dram("agate_dram", [D, S], F32)
        self.bgate_dram = dram("bgate_dram", [D, S], F32)
        self.ga_dram = dram("ga_dram", [D, S], F32)
        self.gb_dram = dram("gb_dram", [D, S], F32)
        self.conv_dram = dram("conv_dram", [D, S], F32)
        self.qlat_dram = dram("qlat_dram", [NC_, P, 2, LT, TC], F32)
        self.v_dram = dram("v_dram", [H * P, S // P, VD], F32)
        self.attn_dram = dram("attn_dram", [D, S], F32)
        self.yb_dram = dram("yb_dram", [D, S], F32)
        self.merged_dram = dram("merged_dram", [D, S], F32)

        sb = lambda n, s, d: ctx.enter_context(nc.sbuf_tensor(n, s, d))
        self.ident = sb("ident", [P, P], F32)
        self.ident16 = sb("ident16", [P, P], BF16)
        self.mask = sb("mask", [P, P], BF16)
        self.mean_mat = sb("mean_mat", [P, P], F32)
        self.eps = sb("eps", [P, 1], F32)
        self.prm_t = sb("prm_t", [P, R_END], F32)
        self.taps_t = sb("taps_t", [P, KT * TAPS], F32)
        self.cact = sb("cact", [P, KT], F32)


def setup_phase(k):
    nc = k.nc
    WCOLS = 256
    W_SLOTS, X_SLOTS, BANKS, FULLS = 4, 6, 6, 2
    PIECES = 2 * D // WCOLS
    QB = TC // P
    TT = S // P
    with ExitStack() as ctx:
        sb = lambda n, s, d: ctx.enter_context(nc.sbuf_tensor(n, s, d))
        sem = lambda n: ctx.enter_context(nc.semaphore(n))
        prm = sb("prm", [R_END, P], F32)
        taps_buf = sb("taps", [P, D], F32)
        taps = taps_buf[0:TAPS, :]
        sq = taps_buf[:, 0:D // 2].bitcast(BF16)
        wada = [sb(f"wada{i}", [P, KT, WCOLS], F32) for i in range(W_SLOTS)]
        xs = [sb(f"xs{i}", [P, D], F32) for i in range(X_SLOTS)]
        ss = sb("ss", [P, TT], F32)
        full = [sb(f"full{i}", [P, TC], F32) for i in range(FULLS)]
        acc = [sb(f"ada_acc{i}", [P, 2, WCOLS], F32) for i in range(2)]
        shift = sb("shift", [P, KT], F32)
        gain = sb("gain", [P, KT], F32)
        ps_par = ctx.enter_context(nc.psum_tensor("ps_par", [P, 512], F32))
        ps_ada = ctx.enter_context(nc.psum_tensor("ps_ada", [P, 2 * KT], F32))
        ps_x = ctx.enter_context(nc.psum_tensor("ps_x", [P, BANKS, TC], F32))

        by_last = [wada[n % W_SLOTS] for n in range(PIECES - W_SLOTS, PIECES)]
        halves = [w[:, h * KT // 2:(h + 1) * KT // 2, :].rearrange("p t n -> p (t n)") for w in by_last for h in range(2)]
        x_at = [x[:] for x in xs] + halves
        x_at += x_at[:TT - len(x_at)]
        ROOTS_AT = {(0, 1): 1, (0, 5): 2, (1, 3): 3}
        OWN, REUSED = X_SLOTS, X_SLOTS + len(halves)

        params_in = sem("params_in")
        wada_in = [sem(f"wada_in{i}") for i in range(W_SLOTS)]
        x_in = [sem(f"x_in{g}") for g in range(NC_)]
        first_in = sem("first_in")
        consts = sem("consts")
        params_t = sem("params_t")
        params_sb = sem("params_sb")
        cact_done = sem("cact_done")
        ada_mm = sem("ada_mm")
        ada_step = sem("ada_step")
        ada_vec = sem("ada_vec")
        sums_done = sem("sums_done")
        root_done = sem("root_done")
        rstd_done = sem("rstd_done")
        x_scaled = sem("x_scaled")
        x_turned = sem("x_turned")
        full_done = sem("full_done")
        hi_done = sem("hi_done")
        lo_done = sem("lo_done")

        rows = [(R_C, KT, k.c), (R_NORM, KT, k.norm_w), (R_BADA, 3 * KT, k.b_ada), (R_CONVB, KT, k.conv_b),
                (R_LNW, KT, k.conv_ln_w), (R_LNB, KT, k.conv_ln_b), (R_QN, LT, k.q_norm_w), (R_KVN, LT, k.kv_norm_w)]
        w_ada = k.w_ada.rearrange("o (t p) n -> p (o t) n", p=P)
        w_in = k.w_in.rearrange("o (t p) n -> p (o t) n", p=P)
        x_rows = k.x.rearrange("o (i p) d -> (o i) p d", p=P)

        with nc.Block() as block:
            @block.sync
            def _(sp):
                def ada(n):
                    if n >= W_SLOTS:
                        sp.wait_ge(ada_step, KT * (n - W_SLOTS + 1))
                    sp.dma_start(wada[n % W_SLOTS][:], w_ada[:, :, n * WCOLS:(n + 1) * WCOLS]).then_inc(
                        wada_in[n % W_SLOTS], 16)

                def load_x(i):
                    if i >= REUSED:
                        sp.wait_ge(x_turned, KT * ((i - REUSED) // QB + 1))
                    elif i >= OWN:
                        sp.wait_ge(ada_step, KT * (PIECES - W_SLOTS + 1 + (i - OWN) // 2))
                    sp.dma_start(x_at[i], x_rows[i]).then_inc(x_in[i // QB], 16)

                for r, n, src in rows:
                    sp.dma_start(prm[r:r + n, :], src.rearrange("o (t p) -> (o t) p", p=P)).then_inc(params_in, 16)
                sp.dma_start(taps, k.conv_w.rearrange("o t c -> (o t) c")).then_inc(params_in, 16)
                for n in range(W_SLOTS):
                    ada(n)
                for i in range(QB):
                    load_x(i)
                for n in range(W_SLOTS, PIECES):
                    ada(n)
                for i in range(QB, X_SLOTS):
                    load_x(i)
                for i in range(2):
                    sp.dma_start(k.raw[i][:], w_in[:, :, C_CQ + i * P:C_CQ + (i + 1) * P]).then_inc(first_in, 16)
                for i in range(X_SLOTS, TT):
                    load_x(i)
                sp.wait_ge(first_in, 32)

            @block.gpsimd
            def _(pool):
                pool.memset(k.ident[:], 0.0).then_inc(consts, 1)
                pool.memset(k.mask[:], 0.0).then_inc(consts, 1)
                pool.memset(k.mean_mat[:], 1.0 / D).then_inc(consts, 1)
                pool.memset(k.eps[:], EPS).then_inc(consts, 1)
                pool.wait_ge(consts, 4)
                pool.affine_select(out=k.ident[:], in_=k.ident[:], compare_op=ALU.not_equal, fill=1.0, base=0,
                                   pattern=[[-1, P]], channel_multiplier=1).then_inc(consts, 1)
                pool.affine_select(out=k.mask[:], in_=k.mask[:], compare_op=ALU.is_ge, fill=NEG, base=0,
                                   pattern=[[-1, P]], channel_multiplier=1).then_inc(consts, 1)
                pool.wait_ge(consts, 6)
                pool.tensor_copy(k.ident16[:], k.ident[:]).then_inc(consts, 1)
                for i in range(TT):
                    pool.wait_ge(rstd_done, i // QB + 1)
                    pool.tensor_scalar(x_at[i], x_at[i], ss[:, i:i + 1], 1.0,
                                       ALU.mult, ALU.mult).then_inc(x_scaled, 1)

            @block.scalar
            def _(act):
                act.wait_ge(params_sb, 1)
                act.activation(k.cact[:], k.prm_t[:, R_C:R_C + KT], ACT.Silu).then_inc(cact_done, 1)

                def roots(g):
                    act.wait_ge(x_in[g], 16 * QB)
                    for i in range(g * QB, (g + 1) * QB):
                        if i:
                            act.wait_ge(sums_done, i)
                        act.activation(sq, x_at[i], ACT.Square,
                                       accum_out=ss[:, i:i + 1]).then_inc(sums_done, 1)
                    s = ss[:, g * QB:(g + 1) * QB]
                    act.wait_ge(sums_done, (g + 1) * QB)
                    act.activation(s, s, ACT.Sqrt, scale=1.0 / D, bias=k.eps[:]).then_inc(root_done, 1)

                act.wait_ge(consts, 4)
                roots(0)
                act.wait_ge(ada_vec, 4)
                for g in range(NC_):
                    for t in range(KT):
                        n = g * KT + t
                        act.wait_ge(x_turned, n + 1)
                        if n >= FULLS:
                            act.wait_ge(lo_done, n - FULLS + 1)
                        act.activation(full[n % FULLS][:], ps_x[:, n % BANKS, :], ACT.Identity,
                                       scale=gain[:, t:t + 1], bias=shift[:, t:t + 1]).then_inc(full_done, 1)
                        if (g, t) in ROOTS_AT:
                            roots(ROOTS_AT[g, t])

            @block.vector
            def _(dve):
                dve.wait_ge(params_t, 2)
                dve.tensor_copy(k.prm_t[:], ps_par[:, 0:R_END]).then_inc(params_sb, 1)
                dve.tensor_copy(k.taps_t[:], ps_par[:, P:P + KT * TAPS]).then_inc(params_sb, 1)

                def invert(g):
                    s = ss[:, g * QB:(g + 1) * QB]
                    dve.wait_ge(root_done, g + 1)
                    dve.reciprocal(s, s).then_inc(rstd_done, 1)

                dve.wait_ge(cact_done, 1)
                for n in range(PIECES):
                    dve.wait_ge(wada_in[n % W_SLOTS], 16 * (n // W_SLOTS + 1))
                    if n >= 2:
                        dve.wait_ge(ada_mm, n - 1)
                    for t in range(KT):
                        a, w = acc[n % 2][:, t % 2, :], wada[n % W_SLOTS][:, t, :]
                        if t < 2:
                            ins = dve.tensor_scalar(a, w, k.cact[:, t:t + 1], None, ALU.mult)
                        else:
                            dve.wait_ge(ada_step, KT * n + t - 1)
                            ins = dve.scalar_tensor_tensor(a, w, k.cact[:, t:t + 1], a, ALU.mult, ALU.add)
                        ins.then_inc(ada_step, 1)
                    if n == PIECES - 3:
                        invert(0)
                dve.wait_ge(ada_mm, PIECES)
                dve.scalar_tensor_tensor(shift[:], ps_ada[:, 0:KT], float(D), k.prm_t[:, R_BADA:R_BADA + KT],
                                         ALU.mult, ALU.add).then_inc(ada_vec, 1)
                dve.scalar_tensor_tensor(gain[:], ps_ada[:, KT:2 * KT], float(D),
                                         k.prm_t[:, R_BADA + KT:R_BADA + 2 * KT], ALU.mult, ALU.add).then_inc(ada_vec, 1)
                dve.wait_ge(ada_vec, 2)
                dve.tensor_scalar_add(gain[:], gain[:], 1.0).then_inc(ada_vec, 1)
                dve.wait_ge(ada_vec, 3)
                dve.tensor_tensor(gain[:], gain[:], k.prm_t[:, R_NORM:R_NORM + KT], ALU.mult).then_inc(ada_vec, 1)
                for g in range(NC_):
                    for t in range(KT):
                        n = g * KT + t
                        hi, lo = (a[:, t, g * TC:(g + 1) * TC] for a in (k.h_hi, k.h_lo))
                        dve.wait_ge(full_done, n + 1)
                        dve.tensor_copy(hi, full[n % FULLS][:]).then_inc(hi_done, 1)
                        dve.wait_ge(hi_done, n + 1)
                        dve.tensor_tensor(lo, full[n % FULLS][:], hi.bitcast(F32), ALU.subtract).then_inc(lo_done, 1)
                        if (g, t) in ROOTS_AT:
                            invert(ROOTS_AT[g, t])

            @block.tensor
            def _(pe):
                pe.wait_ge(consts, 6)
                pe.wait_ge(params_in, 16 * (len(rows) + 1))
                pe.transpose(ps_par[:, 0:R_END], prm[:], k.ident[0:R_END, 0:R_END]).then_inc(params_t, 1)
                for t in range(KT):
                    mm = pe.transpose(ps_par[:, P + t * TAPS:P + (t + 1) * TAPS], taps[:, t * P:(t + 1) * P],
                                      k.ident[0:TAPS, 0:TAPS])
                mm.then_inc(params_t, 1)
                for n in range(PIECES):
                    pe.wait_ge(ada_step, KT * (n + 1))
                    for m in range(WCOLS // P):
                        j = n * (WCOLS // P) + m
                        for h in range(2):
                            mm = pe.matmul(ps_ada[:, j:j + 1], acc[n % 2][:, h, m * P:(m + 1) * P],
                                           k.mean_mat[:, 0:1], start=(h == 0), stop=(h == 1))
                    mm.then_inc(ada_mm, 1)
                for g in range(NC_):
                    pe.wait_ge(x_scaled, QB * (g + 1))
                    for t in range(KT):
                        n = g * KT + t
                        if n >= BANKS:
                            pe.wait_ge(full_done, n - BANKS + 1)
                        for j in range(QB):
                            mm = pe.transpose(ps_x[:, n % BANKS, j * P:(j + 1) * P],
                                              x_at[g * QB + j][:, t * P:(t + 1) * P], k.ident[:])
                        mm.then_inc(x_turned, 1)


def projection_phase(k):
    nc = k.nc
    PRE = 5
    PER = 6
    KINDS = ["glu", "val", "ga", "gb", "agate", "bgate"]
    COLS = {"glu": C_GLU, "val": C_VAL, "ga": C_GA, "gb": C_GB, "agate": C_AGATE, "bgate": C_BGATE}
    OUTS = {"ga": k.ga_dram, "gb": k.gb_dram, "agate": k.agate_dram, "bgate": k.bgate_dram}
    FUNC = {"glu": ACT.Sigmoid, "val": ACT.Copy, "ga": ACT.Sigmoid, "gb": ACT.Sigmoid,
            "agate": ACT.Silu, "bgate": ACT.Silu}
    PAD = TAPS - 1
    TWO_PI = 6.283185307179586
    C1 = 6.28125
    C2 = float(round((TWO_PI - C1) * 2.0 ** 20) / 2.0 ** 20)
    C3 = TWO_PI - C1 - C2
    MAGIC = 1.5 * 2.0 ** 23
    PI_BELOW = 3.1415925
    NORM = (R_QN, R_KVN)
    GCOLS = 128
    LAT_TILES = 2 * LT
    N_ANGLE = 9
    KPE_HALF = 2 * TC
    with ExitStack() as ctx:
        sb = lambda n, s, d: ctx.enter_context(nc.sbuf_tensor(n, s, d))
        sem = lambda n: ctx.enter_context(nc.semaphore(n))
        raw = k.raw
        wada0 = sb("wada_gate", [P, KT, GCOLS], F32)
        w_hi = [sb(f"w_hi{i}", [P, KT, P], F32R) for i in range(2)]
        w_lo = [sb(f"w_lo{i}", [P, KT, P], F32R) for i in range(2)]
        u = sb("u", [P, PAD + S], F32)
        acc = sb("acc", [P, S], F32)
        sg = sb("sg", [P, S], F32)
        lat = sb("lat", [P, LT, S], F32)
        stage = lat[:, LT - 1, :].rearrange("p (c n) -> p c n", c=NC_)
        part_hi = sb("part_hi", [P, LT, TC], F32R)
        part_lo = sb("part_lo", [P, LT, TC], F32R)
        freqs = sb("freqs", [P, 2], F32)
        halfpi = sb("halfpi", [P, 1], F32)
        ang, turns = u[:, PAD:], sg[:]
        kpe = lat[:, LT - 1, :]
        sq = acc[:].rearrange("p (i t n) -> p i t n", i=2, t=LT)
        wada = [wada0, ang[:, 0:KT * GCOLS].rearrange("p (t n) -> p t n", t=KT)]
        gate_row, ada_acc = sg[:, 0:D], [sg[:, D + i * P:D + (i + 1) * P] for i in range(2)]
        ps = ctx.enter_context(nc.psum_tensor("ps_proj", [P, 2 * NC_, TC], F32))

        raw_in = [sem(f"raw_in{i}") for i in range(2)]
        hi_made = sem("w_hi_made")
        lo_made = sem("w_lo_made")
        chunk_mm = sem("chunk_mm")
        chunk_out = sem("chunk_out")
        stored = sem("stored")
        glu_used = sem("glu_used")
        conv_tap = sem("conv_tap")
        conv_done = sem("conv_done")
        conv_out = sem("conv_out")
        pos_in = sem("pos_in")
        filled = sem("filled")
        angle_step = sem("angle_step")
        trig_done = sem("trig_done")
        trig_out = sem("trig_out")
        squared = sem("squared")
        summed = sem("summed")
        mean_mm = sem("mean_mm")
        rooted = sem("rooted")
        inverted = sem("inverted")
        scaled = sem("lat_scaled")
        part_hi_done, part_lo_done = sem("part_hi_done"), sem("part_lo_done")
        part_hi_out, part_lo_out = sem("part_hi_out"), sem("part_lo_out")
        kpe_step = sem("kpe_step")
        wada_in = [sem(f"wada_gate_in{i}") for i in range(2)]
        trig_back = sem("trig_back")
        gate_mm = sem("gate_mm")
        gate_read = sem("gate_read")
        gate_out = sem("gate_out")
        ada_step = sem("ada_gate_step")
        ada_begun = sem("ada_gate_begun")

        w_in = k.w_in.rearrange("o (t p) n -> p (o t) n", p=P)
        w_ada = k.w_ada.rearrange("o (t p) n -> p (o t) n", p=P)

        GATE_TILES = (1, 3)

        def tile_weights(sp, slot, col, step=0, swap=False):
            if swap:
                for to, at, n in ((0, 0, ROPE), (ROPE, ROPE // 2, ROPE // 2), (ROPE + ROPE // 2, 0, ROPE // 2)):
                    sp.dma_start(raw[slot][:, :, to:to + n], w_in[:, :, C_KPE + at:C_KPE + at + n]).then_inc(raw_in[slot], 16)
            else:
                sp.dma_start(raw[slot][:], w_in[:, :, col:min(col + D + P, k.w_in.shape[2])][:, :, bass.ds(step, P)]).then_inc(raw_in[slot], 16)

        PRE_RAW = [2 + 3, 2]

        def raw_count(i, q):
            return 16 * (PRE_RAW[(PRE + q) % 2] + q // 2 + 1) + i * (16 * PER // 2)

        with nc.Block() as block:
            @block.sync
            def _(sp):
                pre_cols = [C_CQ, C_CQ + P, C_CKV, C_CKV + P, None]
                sp.sem_inc(raw_in[0], 16)
                sp.sem_inc(raw_in[1], 16)
                sp.dma_start(kpe.bitcast(I32), k.positions.to_broadcast([P, S])).then_inc(pos_in, 16)
                sp.dma_start(freqs[:], k.freqs).then_inc(pos_in, 16)

                def store_tile(dst, q_chunks):
                    sp.wait_ge(chunk_out, q_chunks + NC_)
                    sp.dma_start(dst, lat[:, LT - 1, :]).then_inc(stored, 16)

                for t in range(PRE):
                    sp.wait_ge(lo_made, t + 1)
                    if t + 2 < PRE:
                        tile_weights(sp, t % 2, pre_cols[t + 2], swap=(t + 2 == PRE - 1))
                    else:
                        q = t + 2 - PRE
                        tile_weights(sp, t % 2, COLS[KINDS[q]])
                    if t == 0:
                        sp.wait_ge(trig_done, 2)
                        sp.dma_start(k.trig_dram, ang).then_inc(trig_out, 16)
                    if t == 2 * LT:
                        sp.wait_ge(gate_read, D // GCOLS)
                        sp.dma_start(k.gate_dram, gate_row).then_inc(gate_out, 16)
                        sp.dma_start(ang, k.trig_dram).then_inc(trig_back, 16)
                    if t in (LT, 2 * LT):
                        for c in range(NC_):
                            n = (t // LT - 1) * NC_ + c
                            dst = (k.qlat_dram[c].rearrange("p h t n -> h p t n") if t == LT else
                                   k.ckv_dram[:, :, :, c * TC:(c + 1) * TC])
                            sp.wait_ge(part_hi_done, n + 1)
                            sp.dma_start(dst[0], part_hi[:].bitcast(F32)).then_inc(part_hi_out, 16)
                            sp.wait_ge(part_lo_done, n + 1)
                            sp.dma_start(dst[1], part_lo[:].bitcast(F32)).then_inc(part_lo_out, 16)
                for c in range(2):
                    sp.wait_ge(part_lo_done, 2 * NC_ + c + 1)
                    for h, (part, out) in enumerate(((part_hi, part_hi_out), (part_lo, part_lo_out))):
                        sp.dma_start(k.kr_dram[h, :, c * KPE_HALF:(c + 1) * KPE_HALF],
                                     part[0:ROPE].rearrange("p t n -> p (t n)").bitcast(F32)).then_inc(out, 16)
                sp.sem_inc(stored, 16)
                with sp.Fori(0, H) as i:
                    here = sp.snap(i * P)
                    nxt = sp.snap(i * P + P)
                    for q, kind in enumerate(KINDS):
                        sp.wait_ge(lo_made, i * PER + (PRE + q + 1))
                        tile_weights(sp, (PRE + q) % 2, COLS[KINDS[(q + 2) % PER]], here if q + 2 < PER else nxt)
                        if kind in OUTS:
                            store_tile(OUTS[kind][bass.ds(here, P), :], i * (PER * NC_) + (PRE + q) * NC_)
                    sp.wait_ge(conv_done, i + 2)
                    sp.dma_start(k.conv_dram[bass.ds(here, P), :], acc[:]).then_inc(conv_out, 16)
                sp.wait_ge(conv_out, 16 * (H + 1))
                sp.wait_ge(stored, 16 * (1 + len(OUTS) * H))
                sp.wait_ge(part_hi_out, 16 * (2 * NC_ + 2))
                sp.wait_ge(part_lo_out, 16 * (2 * NC_ + 2))
                sp.wait_ge(trig_out, 16)
                for s in range(2):
                    sp.wait_ge(raw_in[s], 16 * (PRE_RAW[s] + 3 * H + 1))

            @block.scalar
            def _(act):
                def split_hi(t_count, slot, raw_need, used):
                    act.wait_ge(raw_in[slot], raw_need)
                    if used is not None:
                        act.wait_ge(chunk_mm, used)
                    act.activation(w_hi[slot][:], raw[slot][:], ACT.Copy).then_inc(hi_made, 1)

                split_hi(0, 0, 16, None)
                split_hi(1, 1, 16, None)
                pre_need = [16, 16, 32, 32, 80]
                act.wait_ge(filled, 1)
                act.wait_ge(angle_step, N_ANGLE)
                act.activation(ang[0:ROPE, :], ang[0:ROPE, :], ACT.Sin, bias=halfpi[0:ROPE, :]).then_inc(trig_done, 1)
                act.activation(ang[ROPE:P, :], ang[ROPE:P, :], ACT.Sin, scale=freqs[ROPE:P, 1:2]).then_inc(trig_done, 1)

                def square(n):
                    c = n % NC_
                    if n >= 2:
                        act.wait_ge(scaled, n - 1)
                    act.activation(sq[:, n % 2], lat[:, :, c * TC:(c + 1) * TC], ACT.Square).then_inc(squared, 1)

                def root(n):
                    act.wait_ge(mean_mm, n + 1)
                    act.activation(sq[:, n % 2, 1, :], ps[:, NC_ + n % NC_, :], ACT.Sqrt, scale=D / LAT,
                                   bias=k.eps[:]).then_inc(rooted, 1)

                for t in range(PRE):
                    for c in range(NC_):
                        if t in (LT, 2 * LT):
                            n = (t // LT - 1) * NC_ + c
                            if c == 0:
                                root(n)
                            if c + 1 < NC_:
                                root(n + 1)
                            act.wait_ge(scaled, n + 1)
                            if n:
                                act.wait_ge(part_hi_out, 16 * n)
                            act.activation(part_hi[:], lat[:, :, c * TC:(c + 1) * TC], ACT.Copy).then_inc(part_hi_done, 1)
                            if c + 2 < NC_:
                                square(n + 2)
                        act.wait_ge(chunk_mm, t * NC_ + c + 1)
                        if t >= LT:
                            act.wait_ge(part_lo_done, ((t - LT) // LT) * NC_ + c + 1)
                        if t < LAT_TILES:
                            dst = lat[:, t % LT, c * TC:(c + 1) * TC]
                        else:
                            dst = stage[:, c, :]
                        act.activation(dst, ps[:, t % 2 * NC_ + c, :], ACT.Copy).then_inc(chunk_out, 1)
                        if t in (LT - 1, 2 * LT - 1) and c < 2:
                            act.wait_ge(chunk_out, t * NC_ + c + 1)
                            square(t // LT * NC_ + c)
                    n = t + 2
                    need = pre_need[n] if n < PRE else raw_count(0, n - PRE)
                    split_hi(n, n % 2, need, (t + 1) * NC_)
                for c in range(2):
                    act.wait_ge(kpe_step, 3)
                    act.wait_ge(part_hi_out, 16 * (2 * NC_ + c))
                    act.activation(part_hi[0:ROPE].rearrange("p t n -> p (t n)"),
                                   kpe[0:ROPE, c * KPE_HALF:(c + 1) * KPE_HALF], ACT.Copy).then_inc(part_hi_done, 1)
                with act.Fori(0, H) as i:
                    n_stored = 0
                    for q, kind in enumerate(KINDS):
                        bank = (PRE + q) % 2 * NC_
                        for c in range(NC_):
                            act.wait_ge(chunk_mm, i * (PER * NC_) + ((PRE + q) * NC_ + c + 1))
                            if kind == "glu":
                                dst = sg[:, c * TC:(c + 1) * TC]
                                if c == 0:
                                    act.wait_ge(glu_used, i + 1)
                            elif kind == "val":
                                dst = u[:, PAD + c * TC:PAD + (c + 1) * TC]
                                if c == 0:
                                    act.wait_ge(conv_done, i + 1)
                            else:
                                dst = stage[:, c, :]
                                if c == 0:
                                    act.wait_ge(stored, i * (16 * len(OUTS)) + 16 * (1 + n_stored))
                            act.activation(dst, ps[:, bank + c, :], FUNC[kind]).then_inc(chunk_out, 1)
                        n_stored += kind in OUTS
                        j = i if q + 2 < PER else i + 1
                        split_hi(0, (PRE + q) % 2, raw_count(j, (q + 2) % PER),
                                 i * (PER * NC_) + (PRE + q + 1) * NC_)

            @block.gpsimd
            def _(pool):
                pool.memset(halfpi[:], TWO_PI / 4).then_inc(filled, 1)
                pool.memset(u[:, 0:PAD], 0.0).then_inc(filled, 1)
                pool.wait_ge(filled, 2)
                pool.sem_inc(glu_used, 1)

                def split_lo(n_made, slot):
                    pool.wait_ge(hi_made, n_made)
                    pool.tensor_tensor(w_lo[slot][:], raw[slot][:], w_hi[slot][:].bitcast(F32),
                                       ALU.subtract).then_inc(lo_made, 1)

                def gate_piece(n):
                    if n >= 2:
                        pool.wait_ge(ada_step, KT * (n - 1))
                    elif n == 1:
                        pool.wait_ge(trig_out, 16)
                    pool.dma_start(wada[n % 2][:], w_ada[:, :, 2 * D + n * GCOLS:2 * D + (n + 1) * GCOLS]).then_inc(
                        wada_in[n % 2], 16)

                def part_lo_of(a, c):
                    n = a * NC_ + c
                    pool.wait_ge(part_hi_done, n + 1)
                    if n:
                        pool.wait_ge(part_lo_out, 16 * n)
                    pool.tensor_tensor(part_lo[:], lat[:, :, c * TC:(c + 1) * TC], part_hi[:].bitcast(F32),
                                       ALU.subtract).then_inc(part_lo_done, 1)

                split_lo(1, 0)
                split_lo(2, 1)
                gate_piece(0)
                gate_piece(1)
                for t in range(PRE):
                    split_lo(t + 3, t % 2)
                    if t + 1 in (LT, 2 * LT):
                        for c in range(NC_):
                            part_lo_of((t + 1) // LT - 1, c)
                    if t + 1 in GATE_TILES:
                        n = 4 * GATE_TILES.index(t + 1)
                        for n in range(n + 2, min(n + 6, D // GCOLS)):
                            gate_piece(n)
                with pool.Fori(0, H) as i:
                    for q, kind in enumerate(KINDS):
                        if kind == "ga":
                            pool.wait_ge(chunk_out, i * (PER * NC_) + (PRE + 2) * NC_)
                            pool.tensor_tensor(u[:, PAD:], u[:, PAD:], sg[:], ALU.mult).then_inc(glu_used, 1)
                        split_lo(i * PER + (PRE + q + 3), (PRE + q) % 2)

            @block.vector
            def _(dve):
                dve.wait_ge(pos_in, 32)
                cs = ang[0:ROPE, :]
                for n, angle in enumerate([
                        lambda: dve.tensor_copy(ang, kpe.bitcast(I32)),
                        lambda: dve.tensor_scalar(ang, ang, freqs[:, 0:1], None, ALU.mult),
                        lambda: dve.tensor_scalar(turns, ang, 1.0 / TWO_PI, MAGIC, ALU.mult, ALU.add),
                        lambda: dve.tensor_scalar(turns, turns, MAGIC, None, ALU.subtract),
                        lambda: dve.scalar_tensor_tensor(ang, turns, -C1, ang, ALU.mult, ALU.add),
                        lambda: dve.scalar_tensor_tensor(ang, turns, -C2, ang, ALU.mult, ALU.add),
                        lambda: dve.scalar_tensor_tensor(ang, turns, -C3, ang, ALU.mult, ALU.add),
                        lambda: dve.tensor_scalar(ang, ang, PI_BELOW, -PI_BELOW, ALU.min, ALU.max),
                        lambda: dve.scalar_tensor_tensor(cs, cs, -1.0, cs, ALU.mult, ALU.min)]):
                    if n:
                        dve.wait_ge(angle_step, n)
                    angle().then_inc(angle_step, 1)

                def sum_squares(n):
                    dve.wait_ge(squared, n + 1)
                    dve.tensor_tensor(sq[:, n % 2, 0, :], sq[:, n % 2, 0, :], sq[:, n % 2, 1, :],
                                      ALU.add).then_inc(summed, 1)

                def normalise(n):
                    a, c = divmod(n, NC_)
                    root = sq[:, n % 2, 1, :]
                    x = lat[:, :, c * TC:(c + 1) * TC]
                    dve.wait_ge(rooted, n + 1)
                    dve.reciprocal(root, root).then_inc(inverted, 1)
                    dve.wait_ge(inverted, n + 1)
                    for t in range(LT):
                        ins = dve.scalar_tensor_tensor(x[:, t, :], x[:, t, :], k.prm_t[:, NORM[a] + t:NORM[a] + t + 1],
                                                       root, ALU.mult, ALU.mult)
                    ins.then_inc(scaled, 1)

                def gate_read_out(n):
                    dve.wait_ge(gate_mm, n + 1)
                    dve.tensor_scalar(gate_row[:, n * P:(n + 1) * P], ps[:, n % NC_, 0:GCOLS], float(D), None,
                                      ALU.mult).then_inc(gate_read, 1)

                def gate_pieces(ns):
                    for n in ns:
                        b = R_BADA + 2 * KT + n
                        if n >= 2:
                            dve.wait_ge(gate_mm, n - 1)
                        dve.tensor_scalar(ada_acc[n % 2], k.ident[:], k.prm_t[:, b:b + 1], None,
                                          ALU.mult).then_inc(ada_begun, 1)
                        dve.wait_ge(ada_begun, n + 1)
                        dve.wait_ge(wada_in[n % 2], 16 * (n // 2 + 1))
                        for t in range(KT):
                            if t or n:
                                dve.wait_ge(ada_step, KT * n + t)
                            dve.scalar_tensor_tensor(ada_acc[n % 2], wada[n % 2][:, t, :], k.cact[:, t:t + 1], ada_acc[n % 2],
                                                     ALU.mult, ALU.add).then_inc(ada_step, 1)
                        if n > ns[0]:
                            gate_read_out(n - 1)
                    gate_read_out(ns[-1])

                for a in range(2):
                    gate_pieces(range(4 * a, 4 * a + 4))
                    sum_squares(a * NC_)
                    sum_squares(a * NC_ + 1)
                    for c in range(NC_):
                        normalise(a * NC_ + c)
                        if c + 2 < NC_:
                            sum_squares(a * NC_ + c + 2)
                dve.wait_ge(gate_out, 16)
                dve.wait_ge(trig_back, 16)
                dve.wait_ge(chunk_out, PRE * NC_)
                dve.tensor_tensor(turns[0:ROPE, :], kpe[ROPE:P, :], ang[ROPE:P, :], ALU.mult).then_inc(kpe_step, 1)
                dve.tensor_tensor(kpe[0:ROPE, :], kpe[0:ROPE, :], ang[0:ROPE, :], ALU.mult).then_inc(kpe_step, 1)
                dve.wait_ge(kpe_step, 2)
                dve.tensor_tensor(kpe[0:ROPE, :], kpe[0:ROPE, :], turns[0:ROPE, :], ALU.add).then_inc(kpe_step, 1)
                for c in range(2):
                    dve.wait_ge(part_hi_done, 2 * NC_ + c + 1)
                    dve.wait_ge(part_lo_out, 16 * (2 * NC_ + c))
                    dve.tensor_tensor(part_lo[0:ROPE].rearrange("p t n -> p (t n)"),
                                      kpe[0:ROPE, c * KPE_HALF:(c + 1) * KPE_HALF],
                                      part_hi[0:ROPE].rearrange("p t n -> p (t n)").bitcast(F32),
                                      ALU.subtract).then_inc(part_lo_done, 1)

                dve.sem_inc(conv_done, 1)
                dve.sem_inc(conv_out, 16)
                with dve.Fori(0, H) as i:
                    dve.wait_ge(glu_used, i + 2)
                    dve.wait_ge(conv_out, i * 16 + 16)
                    tap = lambda n: k.taps_t[:, bass.ds(i * TAPS + n, 1)]
                    dve.tensor_scalar(acc[:], u[:, 0:S], tap(0), k.prm_t[:, bass.ds(i + R_CONVB, 1)],
                                      ALU.mult, ALU.add).then_inc(conv_tap, 1)
                    for n in range(1, TAPS):
                        dve.wait_ge(conv_tap, i * (TAPS - 1) + n)
                        ins = dve.scalar_tensor_tensor(acc[:], u[:, n:n + S], tap(n), acc[:],
                                                       ALU.mult, ALU.add)
                        ins.then_inc(conv_tap if n < TAPS - 1 else conv_done, 1)

            @block.tensor
            def _(pe):
                def tile(slot, lo_need, free_need, means=None, roots=None, gates_before=0, gates_from=None):
                    pe.wait_ge(lo_made, lo_need)
                    for c in range(NC_):
                        if means is not None:
                            for n in ((0, 1) if c == 0 else (c + 1,) if c + 1 < NC_ else ()):
                                pe.wait_ge(summed, means + n + 1)
                                pe.wait_ge(chunk_out, means // NC_ * LT * NC_ + LT * NC_)
                                pe.matmul(ps[:, NC_ + n, :], k.mean_mat[:], sq[:, (means + n) % 2, 0, :],
                                          start=True, stop=True).then_inc(mean_mm, 1)
                        if roots is not None:
                            pe.wait_ge(rooted, roots + c + 1)
                        if gates_before:
                            pe.wait_ge(gate_read, gates_before + c + 1 - 4)
                        if free_need is not None:
                            pe.wait_ge(chunk_out, free_need + c + 1)
                        out = ps[:, slot * NC_ + c, :]
                        for t in range(KT):
                            mm = split3(pe, out, w_hi[slot][:, t, :], w_lo[slot][:, t, :],
                                        k.h_hi[:, t, c * TC:(c + 1) * TC], k.h_lo[:, t, c * TC:(c + 1) * TC],
                                        t == 0, t == KT - 1)
                        mm.then_inc(chunk_mm, 1)
                        if gates_from is not None:
                            pe.wait_ge(ada_step, KT * (gates_from + c + 1))
                            pe.wait_ge(chunk_out, gates_from // 4 * LT * NC_ + c + 1)
                            pe.matmul(ps[:, (1 - slot) * NC_ + c, 0:GCOLS], k.mean_mat[:], ada_acc[(gates_from + c) % 2],
                                      start=True, stop=True).then_inc(gate_mm, 1)

                for t in range(PRE):
                    tile(t % 2, t + 1, (t - 2) * NC_ if t >= 2 else None,
                         (t // LT - 1) * NC_ if t in (LT, 2 * LT) else None, 0 if t == LT + 1 else None,
                         4 * (GATE_TILES.index(t - 1) + 1) if t - 1 in GATE_TILES else 0,
                         4 * GATE_TILES.index(t) if t in GATE_TILES else None)
                pe.wait_ge(rooted, 2 * NC_)
                with pe.Fori(0, H) as i:
                    for q in range(PER):
                        tile((PRE + q) % 2, i * PER + (PRE + q + 1), i * (PER * NC_) + (PRE + q - 2) * NC_)


def value_phase(k):
    nc = k.nc
    V_BANKS = 8
    SLOTS = 3
    QB = TC // P
    HALVES = H * VD // TC
    HH = TC // VD
    TT = S // P
    with ExitStack() as ctx:
        sb = lambda n, s, d: ctx.enter_context(nc.sbuf_tensor(n, s, d))
        sem = lambda n: ctx.enter_context(nc.semaphore(n))
        raw = [sb(f"wv_raw{i}", [P, LT, TC], F32) for i in range(HALVES)]
        w_hi = [sb(f"wv_hi{i}", [P, LT, TC], F32R) for i in range(HALVES)]
        w_lo = [sb(f"wv_lo{i}", [P, LT, TC], F32R) for i in range(HALVES)]
        v = [sb(f"v_st{i}", [P, H * VD], F32) for i in range(SLOTS)]
        ps = ctx.enter_context(nc.psum_tensor("ps_v", [P, V_BANKS, TC], F32))

        raw_in = [sem(f"wv_in{i}") for i in range(HALVES)]
        ckv_in = [sem(f"ckv_in{c}") for c in range(NC_)]
        next_in = sem("next_in")
        w_hi_made, w_lo_made = sem("wv_hi_made"), sem("wv_lo_made")
        v_mm = sem("v_mm")
        v_done = [sem(f"v_done{half}") for half in range(HALVES)]
        head_in = sem("head_w_first_in")
        head_hi_made = sem("head_w_first_hi")
        v_out = [sem(f"v_out{i}") for i in range(SLOTS)]

        w = k.w_ukv.rearrange("o (t p) (h n) -> p (o t) h n", p=P, n=KVH)[:, :, :, NOPE:]

        def copy_half(eng, copy, half):
            for j in range(TT):
                eng.wait_ge(v_mm, j * HALVES + half + 1)
                if j >= SLOTS:
                    eng.wait_ge(v_out[j % SLOTS], 16 * (j // SLOTS))
                copy(v[j % SLOTS][:, half * TC:(half + 1) * TC],
                     ps[:, (j * HALVES + half) % V_BANKS, :]).then_inc(v_done[half], 1)

        with nc.Block() as block:
            @block.sync
            def _(sp):
                def latents(c):
                    s = slice(c * TC, (c + 1) * TC)
                    for part, to in ((0, k.ckv_hi), (1, k.ckv_lo)):
                        sp.dma_start(to[:, :, s].bitcast(F32), k.ckv_dram[part, :, :, s]).then_inc(ckv_in[c], 16)

                for half in range(HALVES):
                    for t in range(LT):
                        sp.dma_start(raw[half][:, t, :].rearrange("p (h n) -> p h n", n=VD),
                                     w[:, t, half * HH:(half + 1) * HH]).then_inc(raw_in[half], 16)
                    latents(half)
                for c in range(HALVES, NC_):
                    latents(c)
                n_next = 0

                def load(to, src):
                    sp.dma_start(to, src).then_inc(next_in, 16)
                    return 1

                v_rows = k.v_dram.rearrange("(h p) j n -> j p h n", p=P)
                for j in range(TT):
                    for half in range(HALVES):
                        sp.wait_ge(v_done[half], j + 1)
                    sp.dma_start(v_rows[j], v[j % SLOTS][:].rearrange("p (h n) -> p h n",
                                                                      n=VD)).then_inc(v_out[j % SLOTS], 16)
                    if j == 0:
                        for to, src in first_weights(k):
                            sp.dma_start(to, src).then_inc(head_in, 16)
                    if j in (1, 2):
                        n_next += load(k.qlat[j - 1][:].bitcast(F32), k.qlat_dram[j - 1])
                    if j == 3:
                        n_next += load(k.trig[:], k.trig_dram)
                    if j == 4:
                        n_next += load(k.kr_hi2[0:ROPE].bitcast(F32), k.kr_dram[0])
                        n_next += load(k.kr_hi2[ROPE:P].bitcast(F32), k.kr_dram[0])
                        n_next += load(k.kr_lo[:].bitcast(F32), k.kr_dram[1])
                sp.wait_ge(next_in, 16 * n_next)
                for s in range(SLOTS):
                    sp.wait_ge(v_out[s], 16 * len(range(s, TT, SLOTS)))

            @block.tensor
            def _(pe):
                for j in range(TT):
                    if j % QB == 0:
                        pe.wait_ge(ckv_in[j // QB], 32)
                    for half in range(HALVES):
                        m = j * HALVES + half
                        if j == 0:
                            pe.wait_ge(w_lo_made, half + 1)
                        if m >= V_BANKS:
                            pe.wait_ge(v_done[half], j - V_BANKS // HALVES + 1)
                        q = slice(j * P, (j + 1) * P)
                        for t in range(LT):
                            mm = split3(pe, ps[:, m % V_BANKS, :], k.ckv_hi[:, t, q], k.ckv_lo[:, t, q],
                                        w_hi[half][:, t, :], w_lo[half][:, t, :], t == 0, t == LT - 1)
                        mm.then_inc(v_mm, 1)

            @block.scalar
            def _(act):
                for half in range(HALVES):
                    act.wait_ge(raw_in[half], 16 * LT)
                    act.activation(w_hi[half][:], raw[half][:], ACT.Copy).then_inc(w_hi_made, 1)
                copy_half(act, lambda to, src: act.activation(to, src, ACT.Copy), 0)
                act.wait_ge(head_in, 16 * 4)
                act.activation(k.wh[:], k.head_raw[:], ACT.Copy).then_inc(head_hi_made, 1)

            @block.vector
            def _(dve):
                for half in range(HALVES):
                    dve.wait_ge(w_hi_made, half + 1)
                    dve.tensor_tensor(w_lo[half][:], raw[half][:], w_hi[half][:].bitcast(F32),
                                      ALU.subtract).then_inc(w_lo_made, 1)
                copy_half(dve, lambda to, src: dve.tensor_copy(to, src), 1)
                dve.wait_ge(head_hi_made, 1)
                dve.tensor_tensor(k.wl[:], k.head_raw[:], k.wh[:].bitcast(F32), ALU.subtract)


def first_weights(k):
    w_uq = k.w_uq.rearrange("o (t p) n -> p (o t) n", p=P)
    w_ukv = k.w_ukv.rearrange("o (t p) n -> p (o t) n", p=P)
    half = ROPE // 2
    return [(k.head_raw[:, :, 0:QH], w_uq[:, :, 0:QH]),
            (k.head_raw[:, :, QH:QH + half], w_uq[:, :, NOPE + half:QH]),
            (k.head_raw[:, :, QH + half:QH + ROPE], w_uq[:, :, NOPE:NOPE + half]),
            (k.head_raw[:, :, 2 * P:3 * P], w_ukv[:, :, 0:NOPE])]


def attention_phase(k):
    nc = k.nc
    QB = TC // P
    ORDER = [0, 3, 1, 2]
    SCALE = float(NOPE + ROPE) ** -0.5
    RING = 5
    BLOCKS = [(g, b) for g in ORDER for b in range(QB)]
    TILES = [(g, j) for g in ORDER for j in range(QB * (g + 1))]
    N_CHUNK = sum(g + 1 for g, _ in BLOCKS)
    N_TILE = len(TILES)
    N_PROJ = 3 * NC_
    LAG = 2
    SLOTS = 3
    first_tile = {g: TILES.index((g, 0)) for g in ORDER}
    chunk_no = {}
    for s, (g, b) in enumerate(BLOCKS):
        for c in range(g + 1):
            chunk_no[s, c] = len(chunk_no)

    size = {g: sum(QB * g + b + 1 for b in range(QB)) for g in ORDER}
    base = {0: 0, 1: 0, 2: size[1], 3: size[1]}
    P_TILES = size[1] + size[3]
    assert size[0] <= size[1]

    def p_at(g, b):
        return base[g] + sum(QB * g + x + 1 for x in range(b))

    def plan():
        ev, waiting, pend = [], list(range(N_TILE)), []

        def tiles(n):
            for _ in range(n):
                t = waiting.pop(0)
                ev.append(("T", t))
                pend.append(t)
                if len(pend) > LAG:
                    ev.append(("PV", pend.pop(0)))

        share = {3: [0, 1, 1, 2], 1: [0, 2, 7, 7], 2: [0, 2, 3, 3]}
        for s, (g, b) in enumerate(BLOCKS):
            ev.append(("S", s))
            if s:
                ev.append(("E", s - 1))
            if s == 5:
                ev.append(("W", 0))
            if s in (6, 7):
                ev.append(("VS", s - 4))
            if g in share:
                tiles(share[g][b])
        ev.append(("E", len(BLOCKS) - 1))
        return ev, tiles, pend

    def with_tail(last):
        ev, tiles, pend = plan()
        if last:
            ev.remove(("W", 0))
            tiles(12)
        else:
            ev += [("QN", 0), ("QR", 0), ("RA", 0), ("K", 0), ("RH", 0), ("QN", 1), ("RL", 0)]
            for c in range(1, NC_):
                if c > 1:
                    ev.append(("QN", c))
                tiles(1)
                ev.append(("QR", c))
                tiles(1)
                if c == NC_ - 1:
                    tiles(2)
                    break
                ev += [("RA", c), ("K", c), ("RH", c)]
                tiles(1)
                ev.append(("RL", c))
                if c == 2:
                    ev.append(("VS", 0))
                tiles(1)
            ev += [("RA", c), ("K", c)]
        while pend:
            ev.append(("PV", pend.pop(0)))
        if not last:
            ev += [("RH", NC_ - 1), ("RL", NC_ - 1), ("VS", 1)]
        return ev

    prologue = []
    for c in range(NC_):
        prologue += [("QN", c), ("QR", c), ("RA", c), ("K", c), ("RH", c), ("RL", c)]
    prologue += [("VS", 0), ("VS", 1)]
    order_of = lambda ev: {e: n for n, e in enumerate(x for x in ev if x[0] in ("QN", "QR", "K"))}
    body, last_body = with_tail(False), with_tail(True)

    with ExitStack() as ctx:
        sb = lambda n, s, d: ctx.enter_context(nc.sbuf_tensor(n, s, d))
        sem = lambda n: ctx.enter_context(nc.semaphore(n))
        qlat, raw, wh, wl = k.qlat, k.head_raw, k.wh, k.wl
        qn_hi, qn_lo = sb("qn_hi", [P, S], F32R), sb("qn_lo", [P, S], F32R)
        kn_hi, kn_lo = sb("kn_hi", [P, S], F32R), sb("kn_lo", [P, S], F32R)
        qr = sb("qr", [P, S], F32R)
        v_hi, v_lo = sb("v_hi", [P, S // P, VD], F32R), sb("v_lo", [P, S // P, VD], F32R)
        ra = [sb(f"rope_a{i}", [ROPE, TC], F32) for i in range(2)]
        rb = sb("rope_b", [ROPE, TC], F32)
        v_raw = [sb(f"v_raw{i}", [P, QB, VD], F32) for i in range(2)]
        prob = sb("prob", [P, P_TILES * P], F32)
        pt_hi = [sb(f"pt_hi{i}", [P, TC], F32R) for i in range(SLOTS)]
        pt_lo = [sb(f"pt_lo{i}", [P, TC], F32R) for i in range(SLOTS)]
        bg = sb("bg", [P, TC], F32)
        nmax = sb("nmax", [P, 16, NC_], F32)
        nbias = sb("nbias", [P, 16], F32)
        rsum = sb("rsum", [P, 16, NC_], F32)
        rinv = sb("rinv", [P, 16], F32)
        ps = ctx.enter_context(nc.psum_tensor("ps_ring", [P, RING, TC], F32))
        ps_t = ctx.enter_context(nc.psum_tensor("ps_t", [P, 2, TC], F32))
        ps_o = ctx.enter_context(nc.psum_tensor("ps_o", [P, TC], F32))

        raw_in = sem("head_w_in")
        qlat_in = [sem(f"qlat_in{i}") for i in range(2)]
        bg_in = sem("bg_in")
        v_in = [sem(f"v_in{i}") for i in range(2)]
        v_hi_made, v_lo_made = sem("v_hi_made"), sem("v_lo_made")
        o_out = sem("o_out")
        w_hi_made, w_lo_made = sem("head_w_hi"), sem("head_w_lo")
        proj_mm = sem("proj_mm")
        proj_hi = sem("proj_hi")
        proj_free = sem("proj_free")
        rope_sum = sem("rope_sum")
        rope_hi = sem("rope_hi")
        rope_done = sem("rope_done")
        rope_step = sem("rope_step")
        scores_mm = sem("scores_mm")
        max_step = sem("max_step")
        max_done = sem("max_done")
        exp_done = sem("exp_done")
        sum_step = sem("sum_step")
        rinv_done = sem("rinv_done")
        normed = sem("normed")
        t_done = sem("t_done")
        t_hi, t_lo = sem("t_hi"), sem("t_lo")
        pv_done = sem("pv_done")
        passed = sem("passed")
        o_done = sem("o_done")

        class At:

            def __init__(self, i):
                self.i = i

            def scores(self, n):
                return self.i * N_CHUNK + n

            def block(self, n):
                return self.i * 16 + n

            def tile(self, n):
                return self.i * N_TILE + n

            def values(self, c):
                return self.i * NC_ + c

            def proj(self, n):
                return self.i * N_PROJ + (N_PROJ + n)

        T_CREDIT = 1
        LO_CREDIT = 2
        PV_CREDIT = SLOTS
        O_CREDIT = 1
        O_OUT_CREDIT = 16

        def release(use):
            before = use - RING
            if before < 0:
                total = N_CHUNK + N_PROJ
                before = max(x for x in range(total) if x % RING == use % RING) - total
            return before

        w_uq = k.w_uq.rearrange("o (t p) n -> p (o t) n", p=P)
        w_ukv = k.w_ukv.rearrange("o (t p) n -> p (o t) n", p=P)
        N_RAW = 4
        HALF = ROPE // 2

        with nc.Block() as block:
            @block.sync
            def _(sp):
                sp.sem_inc(o_out, O_OUT_CREDIT)

                def weights(q_cols, kv_cols):
                    sp.dma_start(raw[:, :, 0:QH], w_uq[:, :, bass.ds(q_cols, QH)]).then_inc(raw_in, 16)
                    sp.dma_start(raw[:, :, QH:QH + HALF],
                                 w_uq[:, :, NOPE + HALF:][:, :, bass.ds(q_cols, HALF)]).then_inc(raw_in, 16)
                    sp.dma_start(raw[:, :, QH + HALF:QH + ROPE],
                                 w_uq[:, :, NOPE:][:, :, bass.ds(q_cols, HALF)]).then_inc(raw_in, 16)
                    sp.dma_start(raw[:, :, 2 * P:3 * P], w_ukv[:, :, bass.ds(kv_cols, NOPE)]).then_inc(raw_in, 16)

                def values(rows, c):
                    sp.dma_start(v_raw[c % 2][:], k.v_dram[:, c * QB:(c + 1) * QB][bass.ds(rows, P)]).then_inc(
                        v_in[c % 2], 16)

                def q_chunk(c):
                    sp.dma_start(qlat[c % 2][:].bitcast(F32), k.qlat_dram[c]).then_inc(qlat_in[c % 2], 16)

                def gate(rows, g, n):
                    sp.wait_ge(o_out, n * 16 + O_OUT_CREDIT)
                    sp.sem_inc(passed, 1)
                    sp.dma_start(bg[:], k.bgate_dram[:, g * TC:(g + 1) * TC][bass.ds(rows, P), :]).then_inc(bg_in, 16)

                def store(rows, g, n):
                    sp.wait_ge(o_done, n + 1 + O_CREDIT)
                    sp.dma_start(k.attn_dram[:, g * TC:(g + 1) * TC][bass.ds(rows, P), :], bg[:]).then_inc(o_out, 16)

                sp.sem_inc(raw_in, 16 * N_RAW)
                sp.sem_inc(qlat_in[0], 16)
                sp.sem_inc(qlat_in[1], 16)
                values(0, 0)
                values(0, 1)
                for c in (2, 3):
                    sp.wait_ge(proj_mm, order_of(prologue)["QR", c - 2] + 1)
                    q_chunk(c)

                def head(i, last):
                    rows = sp.snap(i * P) if not last else i * P
                    for c in (2, 3):
                        sp.wait_ge(v_lo_made, At(i).values(c - 2) + 1)
                        sp.sem_inc(passed, 1)
                        values(rows, c)
                    if not last:
                        next_rows = sp.snap(i * P + P)
                        q_cols, kv_cols = sp.snap(i * QH + QH), sp.snap(i * KVH + KVH)
                        sp.wait_ge(w_lo_made, i + 1)
                        weights(q_cols, kv_cols)
                        sp.wait_ge(proj_mm, (i + 1) * N_PROJ)
                        q_chunk(0)
                        q_chunk(1)
                    for n, g in enumerate(ORDER):
                        gate(rows, g, i * QB + n)
                        if n >= QB - 2 and not last:
                            sp.wait_ge(proj_mm, At(i).proj(order_of(body)["QR", n - 2] + 1))
                            q_chunk(n)
                        if g == 1 and not last:
                            for c in (0, 1):
                                sp.wait_ge(v_lo_made, At(i).values(c + 2) + 1)
                                sp.sem_inc(passed, 1)
                                values(next_rows, c)
                        store(rows, g, i * QB + n)

                with sp.Fori(0, H - 1) as i:
                    head(i, False)
                head(H - 1, True)
                sp.wait_ge(o_out, H * QB * 16 + O_OUT_CREDIT)

            @block.tensor
            def _(pe):
                def ring_wait(at, use):
                    before = release(use)
                    if 0 <= before < N_CHUNK:
                        pe.wait_ge(exp_done, at.scores(before + 1))
                    else:
                        pe.wait_ge(proj_free, at.proj(before + 1 - (N_CHUNK if before >= 0 else 0)))

                def project(e, at, n, prol):
                    kind, c = e
                    use = N_CHUNK + n
                    bank = ps[:, use % RING, :]
                    if prol:
                        if n >= RING:
                            pe.wait_ge(proj_free, n - RING + 1)
                    else:
                        ring_wait(at, use)
                    cols = {"QN": 0, "QR": P, "K": 2 * P}[kind]
                    w = slice(cols, cols + P)
                    if kind in ("QN", "QR"):
                        if kind == "QN":
                            pe.wait_ge(qlat_in[c % 2], (c // 2 + 1) * 16 if prol else at.i * 32 + (32 + (c // 2 + 1) * 16))
                        for t in range(LT):
                            mm = split3(pe, bank, wh[:, t, w], wl[:, t, w], qlat[c % 2][:, 0, t, :],
                                        qlat[c % 2][:, 1, t, :], t == 0, t == LT - 1)
                    else:
                        s = slice(c * TC, (c + 1) * TC)
                        for t in range(LT):
                            mm = split3(pe, bank, wh[:, t, w], wl[:, t, w], k.ckv_hi[:, t, s], k.ckv_lo[:, t, s],
                                        t == 0, t == LT - 1)
                    mm.then_inc(proj_mm, 1)

                def scores(at, s):
                    g, b = BLOCKS[s]
                    q = slice((QB * g + b) * P, (QB * g + b + 1) * P)
                    if s == 0:
                        pe.wait_ge(proj_free, at.i * N_PROJ + N_PROJ - 2)
                        pe.wait_ge(rope_done, at.i * NC_ + NC_ - 1)
                    if s == QB:
                        pe.wait_ge(proj_free, at.i * N_PROJ + N_PROJ)
                        pe.wait_ge(rope_done, at.i * NC_ + NC_)
                    for c in range(g + 1):
                        n = chunk_no[s, c]
                        ring_wait(at, n)
                        width = TC if c < g else (b + 1) * P
                        out = ps[:, n % RING, 0:width]
                        ks = slice(c * TC, c * TC + width)
                        pe.matmul(out, qn_hi[:, q], kn_hi[:, ks], start=True, stop=False)
                        pe.matmul(out, qn_hi[:, q], kn_lo[:, ks], start=False, stop=False)
                        pe.matmul(out, qn_lo[:, q], kn_hi[:, ks], start=False, stop=False)
                        pe.matmul(out, qr[:, q], k.kr_hi2[:, ks], start=False, stop=False)
                        mm = pe.matmul(out, qr[0:ROPE, q], k.kr_lo[:, ks], start=False, stop=(c < g))
                        if c == g:
                            mm = pe.matmul(out[:, b * P:(b + 1) * P], k.ident16[:], k.mask[:], start=False, stop=True)
                        mm.then_inc(scores_mm, 1)

                def turn(at, n):
                    g, j = TILES[n]
                    r = max(0, j - QB * g)
                    last_block = BLOCKS.index((g, QB - 1))
                    if j % QB == 0:
                        pe.wait_ge(normed, at.scores(chunk_no[last_block, j // QB] + 1))
                    pe.wait_ge(t_lo, at.tile(n - 1 + LO_CREDIT))
                    for b in range(r, QB):
                        x = (p_at(g, b) + j) * P
                        mm = pe.transpose(ps_t[:, n % 2, b * P:(b + 1) * P], prob[:, x:x + P], k.ident[:])
                    mm.then_inc(t_done, 1)

                def times_v(at, n):
                    g, j = TILES[n]
                    r = max(0, j - QB * g)
                    if j == 0:
                        pe.wait_ge(o_done, at.i * QB + (ORDER.index(g) + O_CREDIT))
                    if j % QB == 0 and (g == 0 or (g == NC_ - 1 and j)):
                        pe.wait_ge(v_lo_made, at.values(j // QB) + 1)
                    pe.wait_ge(t_lo, at.tile(n + 1 + LO_CREDIT))
                    s = slice(r * P, TC)
                    out = ps_o[:, s]
                    mh, ml = pt_hi[n % SLOTS][:, s], pt_lo[n % SLOTS][:, s]
                    pe.matmul(out, v_hi[:, j, :], mh, start=(j == 0), stop=False)
                    pe.matmul(out, v_lo[:, j, :], mh, start=False, stop=False)
                    pe.matmul(out, v_hi[:, j, :], ml, start=False, stop=(j == QB * (g + 1) - 1)).then_inc(pv_done, 1)

                def run(ev, at, prol=False):
                    number = order_of(ev)
                    for e in ev:
                        if e[0] in ("QN", "QR", "K"):
                            if number[e] == 0 and not prol:
                                pe.wait_ge(w_lo_made, at.i + 2)
                            project(e, at, number[e], prol)
                        elif e[0] == "S":
                            scores(at, e[1])
                        elif e[0] == "T":
                            turn(at, e[1])
                        elif e[0] == "PV":
                            times_v(at, e[1])

                run(prologue, At(-1), prol=True)
                with pe.Fori(0, H - 1) as i:
                    run(body, At(i))
                run(last_body, At(H - 1))

            @block.scalar
            def _(act):
                def run(ev, at, prol=False):
                    number = order_of(ev)
                    for kind, n in ev:
                        if kind == "W":
                            act.wait_ge(raw_in, at.i * (16 * N_RAW) + 32 * N_RAW)
                            act.wait_ge(proj_mm, at.i * N_PROJ + N_PROJ)
                            act.activation(wh[:], raw[:], ACT.Copy).then_inc(w_hi_made, 1)
                        elif kind in ("QN", "K"):
                            m = number[kind, n]
                            bank = ps[:, (N_CHUNK + m) % RING, :]
                            s = slice(n * TC, (n + 1) * TC)
                            act.wait_ge(proj_mm, m + 1 if prol else at.proj(m + 1))
                            if kind == "QN":
                                ins = act.activation(qn_hi[:, s], bank, ACT.Copy, scale=SCALE)
                            else:
                                ins = act.activation(kn_hi[:, s], bank, ACT.Copy)
                            ins.then_inc(proj_hi, 1)
                        elif kind == "RH":
                            act.wait_ge(rope_sum, n + 1 if prol else at.i * NC_ + (NC_ + n + 1))
                            act.activation(qr[0:ROPE, n * TC:(n + 1) * TC], ra[n % 2][:], ACT.Copy).then_inc(rope_hi, 1)
                        elif kind == "VS":
                            i = at.i + 1 if n < 2 else at.i
                            act.wait_ge(v_in[n % 2], i * 32 + 16 * (n // 2 + 1))
                            if not prol:
                                act.wait_ge(pv_done, at.tile((TILES.index((2, n * QB + QB - 1)) + 1 if n < 2 else 0)
                                                             + PV_CREDIT))
                            act.activation(v_hi[:, n * QB:(n + 1) * QB, :], v_raw[n % 2][:],
                                           ACT.Copy).then_inc(v_hi_made, 1)
                        elif kind == "E":
                            g, b = BLOCKS[n]
                            act.wait_ge(max_done, at.block(n + 1))
                            if b == 0:
                                held = {0: 0, 3: 0, 1: first_tile[3], 2: first_tile[1]}[g]
                                act.wait_ge(t_done, at.tile(held + T_CREDIT))
                            for c in range(g + 1):
                                width = TC if c < g else (b + 1) * P
                                x = (p_at(g, b) + c * QB) * P
                                act.activation(prob[:, x:x + width], ps[:, chunk_no[n, c] % RING, 0:width], ACT.Exp,
                                               bias=nbias[:, n:n + 1],
                                               accum_out=rsum[:, n, c:c + 1]).then_inc(exp_done, 1)
                        elif kind == "T":
                            g, j = TILES[n]
                            s = slice(max(0, j - QB * g) * P, TC)
                            act.wait_ge(pv_done, at.tile(n + 1 - SLOTS + PV_CREDIT))
                            act.wait_ge(t_done, at.tile(n + 1 + T_CREDIT))
                            act.activation(pt_hi[n % SLOTS][:, s], ps_t[:, n % 2, s], ACT.Copy).then_inc(t_hi, 1)

                run(prologue, At(-1), prol=True)
                with act.Fori(0, H - 1) as i:
                    run(body, At(i))
                run(last_body, At(H - 1))

            @block.vector
            def _(dve):
                dve.sem_inc(t_lo, LO_CREDIT)
                dve.sem_inc(o_done, O_CREDIT)

                def run(ev, at, prol=False):
                    number = order_of(ev)
                    for kind, n in ev:
                        if kind in ("QN", "K"):
                            m = number[kind, n]
                            bank = ps[:, (N_CHUNK + m) % RING, :]
                            s = slice(n * TC, (n + 1) * TC)
                            hi_no = sum(1 for e, x in number.items() if e[0] != "QR" and x <= m)
                            per = N_PROJ - NC_
                            dve.wait_ge(proj_hi, hi_no if prol else at.i * per + (per + hi_no))
                            if kind == "QN":
                                ins = dve.scalar_tensor_tensor(qn_lo[:, s], bank, SCALE, qn_hi[:, s].bitcast(F32),
                                                               ALU.mult, ALU.subtract)
                            else:
                                ins = dve.tensor_tensor(kn_lo[:, s], bank, kn_hi[:, s].bitcast(F32), ALU.subtract)
                            ins.then_inc(proj_free, 1)
                        elif kind == "RA":
                            m = number["QR", n]
                            bank = ps[:, (N_CHUNK + m) % RING, :]
                            s = slice(n * TC, (n + 1) * TC)
                            a = ra[n % 2]
                            if n >= 2 or not prol:
                                dve.wait_ge(rope_done, n - 1 if prol else at.i * NC_ + (NC_ + n - 1))
                            dve.wait_ge(proj_mm, m + 1 if prol else at.proj(m + 1))
                            dve.scalar_tensor_tensor(a[:], bank[0:ROPE, :], SCALE, k.trig[0:ROPE, s],
                                                     ALU.mult, ALU.mult)
                            dve.scalar_tensor_tensor(rb[:], bank[ROPE:P, :], SCALE, k.trig[ROPE:P, s],
                                                     ALU.mult, ALU.mult).then_inc(proj_free, 1)
                            dve.wait_ge(proj_free, m + 1 if prol else at.proj(m + 1))
                            dve.tensor_tensor(a[:], a[:], rb[:], ALU.add).then_inc(rope_sum, 1)
                        elif kind == "RL":
                            s = slice(n * TC, (n + 1) * TC)
                            dve.wait_ge(rope_hi, n + 1 if prol else at.i * NC_ + (NC_ + n + 1))
                            dve.tensor_tensor(qr[ROPE:P, s], ra[n % 2][:], qr[0:ROPE, s].bitcast(F32),
                                              ALU.subtract).then_inc(rope_done, 1)
                        elif kind == "S":
                            g, b = BLOCKS[n]
                            for c in range(g + 1):
                                width = TC if c < g else (b + 1) * P
                                to = nmax[:, n, c:c + 1] if g else nbias[:, n:n + 1]
                                dve.wait_ge(scores_mm, at.scores(chunk_no[n, c] + 1))
                                ins = dve.tensor_reduce(to, ps[:, chunk_no[n, c] % RING, 0:width], AX.X, ALU.max,
                                                        negate=True)
                                ins.then_inc(max_step if g else max_done, 1)
                            if g:
                                n_max = chunk_no[n, g] + 1 - QB
                                dve.wait_ge(max_step, at.i * (N_CHUNK - QB) + n_max)
                                dve.tensor_reduce(nbias[:, n:n + 1], nmax[:, n, 0:g + 1], AX.X,
                                                  ALU.min).then_inc(max_done, 1)
                        elif kind == "E":
                            g, b = BLOCKS[n]
                            dve.wait_ge(exp_done, at.scores(chunk_no[n, g] + 1))
                            if g:
                                dve.tensor_reduce(rinv[:, n:n + 1], rsum[:, n, 0:g + 1], AX.X,
                                                  ALU.add).then_inc(sum_step, 1)
                                dve.wait_ge(sum_step, at.i * (16 - QB) + (n + 1 - QB))
                                src = rinv[:, n:n + 1]
                            else:
                                src = rsum[:, n, 0:1]
                            dve.reciprocal(rinv[:, n:n + 1], src).then_inc(rinv_done, 1)
                        elif kind == "T":
                            g, j = TILES[n]
                            s = slice(max(0, j - QB * g) * P, TC)
                            dve.wait_ge(t_hi, at.tile(n + 1))
                            dve.tensor_tensor(pt_lo[n % SLOTS][:, s], ps_t[:, n % 2, s],
                                              pt_hi[n % SLOTS][:, s].bitcast(F32), ALU.subtract).then_inc(t_lo, 1)
                        elif kind == "PV":
                            g, j = TILES[n]
                            if j == QB * (g + 1) - 1:
                                m = ORDER.index(g)
                                dve.wait_ge(pv_done, at.tile(n + 1 + PV_CREDIT))
                                dve.wait_ge(bg_in, at.i * (16 * QB) + 16 * (m + 1))
                                dve.tensor_tensor(bg[:], ps_o[:], bg[:], ALU.mult).then_inc(o_done, 1)

                run(prologue, At(-1), prol=True)
                with dve.Fori(0, H - 1) as i:
                    run(body, At(i))
                run(last_body, At(H - 1))

            @block.gpsimd
            def _(pool):
                pool.sem_inc(w_hi_made, 1)
                pool.sem_inc(w_lo_made, 1)
                pool.sem_inc(t_done, T_CREDIT)
                pool.sem_inc(pv_done, PV_CREDIT)

                def run(ev, at, prol=False):
                    for kind, n in ev:
                        if kind == "W":
                            pool.wait_ge(w_hi_made, at.i + 2)
                            pool.tensor_tensor(wl[:], raw[:], wh[:].bitcast(F32), ALU.subtract).then_inc(w_lo_made, 1)
                        elif kind == "VS":
                            i = at.i + 1 if n < 2 else at.i
                            pool.wait_ge(v_hi_made, i * NC_ + n + 1)
                            v = slice(n * QB, (n + 1) * QB)
                            pool.tensor_tensor(v_lo[:, v, :], v_raw[n % 2][:], v_hi[:, v, :].bitcast(F32),
                                               ALU.subtract).then_inc(v_lo_made, 1)
                        elif kind == "E":
                            g, b = BLOCKS[n]
                            pool.wait_ge(rinv_done, at.block(n + 1))
                            pool.sem_inc(passed, 1)
                            for c in range(g + 1):
                                width = TC if c < g else (b + 1) * P
                                x = (p_at(g, b) + c * QB) * P
                                pool.tensor_scalar(prob[:, x:x + width], prob[:, x:x + width], rinv[:, n:n + 1], 1.0,
                                                   ALU.mult, ALU.mult).then_inc(normed, 1)

                run(prologue, At(-1), prol=True)
                with pool.Fori(0, H - 1) as i:
                    run(body, At(i))
                run(last_body, At(H - 1))


def output_phase(k):
    nc = k.nc
    N = NC_
    BANKS = 6
    SL = 3
    U_CONV, U_END = N * KT, 2 * N * KT
    PER = TC // P
    TT = S // P
    XS = 4
    HALF = KT // 2
    FINAL = [(i, h) for h in range(2) for i in range(PER)] + [(i, h) for i in range(PER, TT) for h in range(2)]

    SOURCE_AT = {1: (0, 0), **{c: (c - 2, 4) for c in range(2, N + 1)},
                 N + 1: (N - 1, 4), **{c: (c - 2, 6) for c in range(N + 2, 2 * N + 2)}}
    STEPS = ["total", "centre", "squares", "scale", "lo_first", "lo_last"]
    STEP_AT = {(N - 2 + n, m): (N, s) for s, (n, m) in zip(STEPS, [(0, 6), (0, 7), (1, 0), (1, 2), (1, 4), (1, 5)])}
    MEAN_AT = {(N - 2, 7): (N, 0), (N - 1, 1): (N, 1)}
    for c in range(N + 1, 2 * N):
        STEP_AT.update({(c - 1, m): (c, s) for s, m in zip(STEPS, [0, 1, 2, 3, 5, 6])})
        MEAN_AT.update({(c - 1, 1): (c, 0), (c - 1, 3): (c, 1)})
    with ExitStack() as ctx:
        sb = lambda n, s, d: ctx.enter_context(nc.sbuf_tensor(n, s, d))
        sem = lambda n: ctx.enter_context(nc.semaphore(n))
        raw = [sb(f"o_raw{i}", [P, KT, P], F32) for i in range(2)]
        w_hi, w_lo = sb("o_w_hi", [P, KT, D], F32R), sb("o_w_lo", [P, KT, D], F32R)
        v = sb("o_v", [P, KT, TC], F32)
        z = sb("o_z", [P, KT, TC], F32)
        ag = sb("o_ag", [P, KT, TC], F32)
        a_hi = [sb(f"o_a_hi{i}", [P, KT, TC], F32R) for i in range(2)]
        a_lo = [sb(f"o_a_lo{i}", [P, KT, TC], F32R) for i in range(2)]
        tot = sb("o_tot", [P, TC], F32)
        g = [sb(f"o_g{i}", [P, TC], F32) for i in range(SL)]
        yb = [sb(f"o_yb{i}", [P, TC], F32) for i in range(SL)]
        y = [sb(f"o_y{i}", [P, TC], F32) for i in range(SL)]
        ss = sb("o_ss", [P, TT], F32)
        ps = ctx.enter_context(nc.psum_tensor("o_ps", [P, BANKS, TC], F32))
        ps_m = ctx.enter_context(nc.psum_tensor("o_ps_m", [P, 2, TC], F32))
        gate_row, norm_row = (r[:].rearrange("p t n -> p (t n)") for r in raw)
        x = [ag[:, 2 * i:2 * i + 2, :].rearrange("p t n -> p (t n)") for i in range(XS)]
        res = [z[:, 2 * i:2 * i + 2, :].rearrange("p t n -> p (t n)") for i in range(XS)]
        rstd, sq = tot, tot[:].bitcast(BF16)

        raw_in = [sem(f"o_raw_in{i}") for i in range(2)]
        hi_made, lo_made = sem("o_w_hi_made"), sem("o_w_lo_made")
        v_in = [sem(f"o_v_in{i}") for i in range(2)]
        ag_in = sem("o_ag_in")
        g_in = [sem(f"o_g_in{i}") for i in range(SL)]
        y_out = [sem(f"o_y_out{i}") for i in range(SL)]
        summed = sem("o_summed")
        mean_mm = sem("o_mean_mm")
        centred = sem("o_centred")
        squared = sem("o_squared")
        scaled = sem("o_scaled")
        rooted = sem("o_rooted")
        inverted = sem("o_inverted")
        silu_done = sem("o_silu_done")
        z_done = sem("o_z_done")
        hi_done, lo_done = sem("o_a_hi_done"), sem("o_a_lo_done")
        tile_mm = sem("o_tile_mm")
        bank_read = sem("o_bank_read")
        y_added = sem("o_y_added")
        rows_in = [sem(f"o_rows_in{i}") for i in range(2)]
        x_in = [sem(f"o_x_in{i}") for i in range(XS)]
        res_out = [sem(f"o_res_out{i}") for i in range(XS)]
        added = sem("o_added")
        row_squared = sem("o_row_squared")
        row_rooted = sem("o_row_rooted")
        row_inverted = sem("o_row_inverted")
        res_done = sem("o_res_done")

        by_tile = lambda ap: ap.rearrange("(t p) s -> p t s", p=P)
        weights = [ap.rearrange("o (t p) n -> p (o t) n", p=P) for ap in (k.w_attn_out, k.w_conv_out, k.w_out)]
        sources = [by_tile(ap) for ap in (k.attn_dram, k.conv_dram, k.merged_dram)]
        chunk = lambda n: slice(n * TC, (n + 1) * TC)
        cols = lambda m: slice(m * P, (m + 1) * P)
        x_rows = k.x.rearrange("o (n p) d -> (o n) p d", p=P)
        out_rows = k.out.rearrange("o (n p) d -> (o n) p d", p=P)
        is_conv = lambda c: N <= c < 2 * N

        def g_count(u):
            return sum(16 if t < U_CONV else 32 for t in range(u % SL, u + 1, SL))

        with nc.Block() as block:
            @block.sync
            def _(sp):
                def piece(w, m):
                    n = w * KT + m
                    if n >= 2:
                        sp.wait_ge(lo_made, n - 1)
                    sp.dma_start(raw[m % 2][:], weights[w][:, :, cols(m)]).then_inc(raw_in[m % 2], 16)

                def source(c):
                    for h in range(2):
                        t = slice(h * HALF, (h + 1) * HALF)
                        sp.dma_start(v[:, t, :], sources[c // N][:, t, chunk(c % N)]).then_inc(v_in[h], 16)

                def gate_source(c):
                    sp.dma_start(ag[:], by_tile(k.agate_dram)[:, :, chunk(c - N)]).then_inc(ag_in, 16)

                def gates(u):
                    if u >= SL:
                        sp.wait_ge(bank_read, u - SL + 1)
                    if u - SL >= U_CONV:
                        sp.wait_ge(y_added, u - SL - U_CONV + 1)
                    n, m = divmod(u, KT)
                    rows, s = slice(m * P, (m + 1) * P), chunk(n % N)
                    sp.dma_start(g[u % SL][:], (k.gb_dram if n < N else k.ga_dram)[rows, s]).then_inc(g_in[u % SL], 16)
                    if n >= N:
                        o = u - U_CONV
                        sp.wait_ge(y_out[o % SL], 16 * (o // SL + 1))
                        sp.dma_start(yb[u % SL][:], k.yb_dram[rows, s]).then_inc(g_in[u % SL], 16)

                def load_x(i):
                    sp.dma_start(x[i % XS], x_rows[i]).then_inc(x_in[i % XS], 16)

                piece(0, 0)
                source(0)
                piece(0, 1)
                gates(0)
                gates(1)
                for m in range(2, KT):
                    piece(0, m)
                for u in range(U_END):
                    n, m = divmod(u, KT)
                    for c in range(1, 2 * N + 2):
                        if SOURCE_AT[c] == (n, m):
                            if is_conv(c - 1):
                                sp.wait_ge(silu_done, KT * (c - N))
                            else:
                                sp.wait_ge(lo_done, KT * c)
                            if c >= 2 * N:
                                for s in range(SL):
                                    sp.wait_ge(y_out[s], 16 * len(range(s, (c - N + 1) * KT, SL)))
                            source(c)
                            if c == N:
                                gate_source(c)
                    if m == KT - 1 and is_conv(n + 1):
                        sp.wait_ge(z_done, KT * (n + 2 - N))
                        if is_conv(n + 2):
                            gate_source(n + 2)
                        else:
                            for i in range(XS):
                                load_x(i)
                    if n == N - 1 and 3 <= m < 3 + HALF:
                        piece(1, 2 * (m - 3))
                        piece(1, 2 * (m - 3) + 1)
                    if n == 2 * N - 1:
                        if m == 0:
                            piece(2, 0)
                        if m + 1 < KT:
                            piece(2, m + 1)
                    if u + 2 < U_END:
                        gates(u + 2)
                    if n < N:
                        sp.wait_ge(bank_read, u + 1)
                    else:
                        sp.wait_ge(y_added, u - U_CONV + 1)
                    sp.dma_start((k.yb_dram if n < N else k.merged_dram)[m * P:(m + 1) * P, chunk(n % N)],
                                 y[u % SL][:]).then_inc(y_out[u % SL], 16)

                sp.wait_ge(lo_made, 3 * KT - 1)
                sp.dma_start(gate_row, k.gate_dram).then_inc(rows_in[0], 16)
                sp.wait_ge(lo_made, 3 * KT)
                sp.dma_start(norm_row, k.final_norm_w.rearrange("(o d) -> o d", o=1).to_broadcast([P, D])).then_inc(
                    rows_in[1], 16)
                for s in range(SL):
                    sp.wait_ge(y_out[s], 16 * len(range(s, U_END, SL)))
                for i in range(TT):
                    c = 2 * N + i // PER
                    if i % PER == 1 and c + 2 < 3 * N:
                        sp.wait_ge(lo_done, KT * (c + 2))
                        source(c + 2)
                    if i >= 1 and i + XS - 1 < TT:
                        sp.wait_ge(added, i)
                        load_x(i + XS - 1)
                    sp.wait_ge(res_done, i + 1)
                    sp.dma_start(out_rows[i], res[i % XS]).then_inc(res_out[i % XS], 16)
                for s in range(XS):
                    sp.wait_ge(res_out[s], 16 * TT // XS)

            @block.tensor
            def _(pe):
                def mean(c, which):
                    j = c - N
                    pe.wait_ge(summed, 2 * j + which + 1)
                    if j:
                        pe.wait_ge(rooted if which else centred, j if which else 2 * j)
                    pe.matmul(ps_m[:, which, :], k.mean_mat[:], tot[:], start=True, stop=True).then_inc(mean_mm, 1)

                for u in range(U_END):
                    n, m = divmod(u, KT)
                    if n % N == 0:
                        pe.wait_ge(lo_made, n // N * KT + m + 1)
                    if u >= BANKS:
                        pe.wait_ge(bank_read, u - BANKS + 1)
                    for t in range(KT):
                        if m == 0:
                            pe.wait_ge(lo_done, n * KT + t + 1)
                        mm = split3(pe, ps[:, u % BANKS, :], w_hi[:, t, cols(m)], w_lo[:, t, cols(m)],
                                    a_hi[n % 2][:, t, :], a_lo[n % 2][:, t, :], t == 0, t == KT - 1)
                        if t == HALF - 1 and (n, m) in MEAN_AT:
                            mean(*MEAN_AT[n, m])
                    mm.then_inc(tile_mm, 1)
                for f, (i, half) in enumerate(FINAL):
                    u = U_END + f
                    n = 2 * N + i // PER
                    q, s = slice(i % PER * P, (i % PER + 1) * P), slice(half * TC, (half + 1) * TC)
                    if n == 2 * N and i == 0:
                        pe.wait_ge(lo_made, 2 * KT + (half + 1) * HALF)
                    pe.wait_ge(bank_read, u - BANKS + 1)
                    for t in range(KT):
                        if i % PER == 0 and half == 0:
                            pe.wait_ge(lo_done, n * KT + t + 1)
                        mm = split3(pe, ps[:, u % BANKS, :], a_hi[n % 2][:, t, q], a_lo[n % 2][:, t, q],
                                    w_hi[:, t, s], w_lo[:, t, s], t == 0, t == KT - 1)
                    mm.then_inc(tile_mm, 1)

            @block.scalar
            def _(act):
                def weight_hi(w, m):
                    n = w * KT + m
                    act.wait_ge(raw_in[m % 2], 16 * (n // 2 + 1))
                    if w:
                        act.wait_ge(tile_mm, (w * N - 1) * KT + m + 1)
                    act.activation(w_hi[:, :, cols(m)], raw[m % 2][:], ACT.Copy).then_inc(hi_made, 1)

                def operand_hi(c, t, src):
                    if c >= 2 and t == 0:
                        act.wait_ge(tile_mm, KT * (c - 1))
                    act.activation(a_hi[c % 2][:, t, :], src[:, t, :], ACT.Copy).then_inc(hi_done, 1)

                def split_hi(c, ts):
                    for t in ts:
                        act.wait_ge(v_in[t // HALF], 16 * (c + 1))
                        operand_hi(c, t, v)

                def conv_operand(c):
                    j = c - N
                    for h in range(2):
                        t = slice(h * HALF, (h + 1) * HALF)
                        act.wait_ge(centred, 2 * j + h + 1)
                        if j and h == 0:
                            act.wait_ge(lo_done, KT * c)
                        act.activation(z[:, t, :], v[:, t, :], ACT.Square).then_inc(squared, 1)
                    act.wait_ge(mean_mm, 2 * j + 2)
                    act.activation(rstd[:], ps_m[:, 1, :], ACT.Sqrt, bias=k.eps[:]).then_inc(rooted, 1)
                    for t in range(KT):
                        act.wait_ge(scaled, 2 * j + t // HALF + 1)
                        act.activation(z[:, t, :], v[:, t, :], ACT.Silu, scale=k.prm_t[:, R_LNW + t:R_LNW + t + 1],
                                       bias=k.prm_t[:, R_LNB + t:R_LNB + t + 1]).then_inc(silu_done, 1)
                    for t in range(KT):
                        act.wait_ge(z_done, j * KT + t + 1)
                        operand_hi(c, t, z)

                weight_hi(0, 0)
                split_hi(0, range(KT))
                for m in range(1, KT):
                    weight_hi(0, m)
                for c in range(1, 2 * N + 1):
                    if is_conv(c):
                        conv_operand(c)
                    else:
                        split_hi(c, range(KT))
                    if c % N == 0:
                        for m in range(KT):
                            weight_hi(c // N, m)
                for i in range(TT):
                    c = 2 * N + i // PER
                    if i % PER == 0 and c + 1 < 3 * N:
                        split_hi(c + 1, range(KT))
                    act.wait_ge(added, i + 1)
                    if i:
                        act.wait_ge(row_squared, i)
                    act.activation(sq, res[i % XS], ACT.Square, accum_out=ss[:, i:i + 1]).then_inc(row_squared, 1)
                    act.wait_ge(row_squared, i + 1)
                    act.activation(ss[:, i:i + 1], ss[:, i:i + 1], ACT.Sqrt, scale=1.0 / D,
                                   bias=k.eps[:]).then_inc(row_rooted, 1)

            @block.gpsimd
            def _(pool):
                def weight_lo(w, m):
                    pool.wait_ge(hi_made, w * KT + m + 1)
                    pool.tensor_tensor(w_lo[:, :, cols(m)], raw[m % 2][:], w_hi[:, :, cols(m)].bitcast(F32),
                                       ALU.subtract).then_inc(lo_made, 1)

                def gate_z(c, ts):
                    pool.wait_ge(ag_in, 16 * (c - N + 1))
                    for t in ts:
                        pool.wait_ge(silu_done, (c - N) * KT + t + 1)
                        pool.tensor_tensor(z[:, t, :], z[:, t, :], ag[:, t, :], ALU.mult).then_inc(z_done, 1)

                for m in range(KT):
                    weight_lo(0, m)
                gate_z(N, range(KT))
                for m in range(KT):
                    weight_lo(1, m)
                for u in range(U_CONV, U_END):
                    n, m = divmod(u, KT)
                    s = u % SL
                    pool.wait_ge(g_in[s], g_count(u))
                    pool.wait_ge(bank_read, u + 1)
                    pool.tensor_tensor(y[s][:], y[s][:], yb[s][:], ALU.add).then_inc(y_added, 1)
                    if is_conv(n + 1):
                        gate_z(n + 1, {2: (0, 1), 3: (2, 3, 4, 5), 4: (6, 7)}.get(m, ()))
                    else:
                        weight_lo(2, m)
                for i in range(TT):
                    pool.wait_ge(x_in[i % XS], 16 * (i // XS + 1))
                    pool.wait_ge(bank_read, U_END + FINAL.index((i, 1)) + 1)
                    pool.tensor_tensor(res[i % XS], res[i % XS], x[i % XS], ALU.add).then_inc(added, 1)

            @block.vector
            def _(dve):
                wide = lambda ap: ap.unsqueeze(1).to_broadcast([P, HALF, TC])

                def total(j, which, src):
                    if j or which:
                        dve.wait_ge(mean_mm, 2 * j + which)
                    if j and not which:
                        dve.wait_ge(scaled, 2 * j)
                    dve.tensor_reduce(tot[:], src[:].rearrange("p t s -> p s t"), AX.X, ALU.add).then_inc(summed, 1)

                def operand_lo(c, ts):
                    src = z if is_conv(c) else v
                    for t in ts:
                        dve.wait_ge(hi_done, c * KT + t + 1)
                        dve.tensor_tensor(a_lo[c % 2][:, t, :], src[:, t, :], a_hi[c % 2][:, t, :].bitcast(F32),
                                          ALU.subtract).then_inc(lo_done, 1)

                def conv_step(c, step):
                    j = c - N
                    if step == "total":
                        for h in range(2):
                            dve.wait_ge(v_in[h], 16 * (c + 1))
                        total(j, 0, v)
                    elif step == "centre":
                        dve.wait_ge(mean_mm, 2 * j + 1)
                        for h in range(2):
                            t = slice(h * HALF, (h + 1) * HALF)
                            dve.tensor_tensor(v[:, t, :], v[:, t, :], wide(ps_m[:, 0, :]),
                                              ALU.subtract).then_inc(centred, 1)
                    elif step == "squares":
                        dve.wait_ge(squared, 2 * j + 2)
                        total(j, 1, z)
                    elif step == "scale":
                        dve.wait_ge(rooted, j + 1)
                        dve.reciprocal(rstd[:], rstd[:]).then_inc(inverted, 1)
                        dve.wait_ge(inverted, j + 1)
                        for h in range(2):
                            t = slice(h * HALF, (h + 1) * HALF)
                            dve.tensor_tensor(v[:, t, :], v[:, t, :], wide(rstd[:]), ALU.mult).then_inc(scaled, 1)
                    else:
                        operand_lo(c, range(HALF) if step == "lo_first" else range(HALF, KT))

                operand_lo(0, range(KT))
                for u in range(U_END):
                    n, m = divmod(u, KT)
                    if (n, m) in STEP_AT:
                        conv_step(*STEP_AT[n, m])
                    if not is_conv(n + 1) and m == 3:
                        operand_lo(n + 1, range(KT))
                    dve.wait_ge(tile_mm, u + 1)
                    dve.wait_ge(g_in[u % SL], g_count(u))
                    if u >= SL:
                        dve.wait_ge(y_out[u % SL], 16 * (u // SL))
                    dve.tensor_tensor(y[u % SL][:], ps[:, u % BANKS, :], g[u % SL][:], ALU.mult).then_inc(bank_read, 1)

                def finish(i):
                    dve.wait_ge(row_rooted, i + 1)
                    dve.reciprocal(ss[:, i:i + 1], ss[:, i:i + 1]).then_inc(row_inverted, 1)
                    dve.wait_ge(row_inverted, i + 1)
                    dve.wait_ge(rows_in[1], 16)
                    dve.scalar_tensor_tensor(res[i % XS], res[i % XS], ss[:, i:i + 1], norm_row,
                                             ALU.mult, ALU.mult).then_inc(res_done, 1)

                finished = 0
                dve.wait_ge(rows_in[0], 16)
                for f, (i, half) in enumerate(FINAL):
                    u = U_END + f
                    dve.wait_ge(tile_mm, u + 1)
                    if i >= XS and half == 0:
                        dve.wait_ge(res_out[i % XS], 16 * (i // XS))
                    s = slice(half * TC, (half + 1) * TC)
                    dve.tensor_tensor(res[i % XS][:, s], ps[:, u % BANKS, :], gate_row[:, s],
                                      ALU.mult).then_inc(bank_read, 1)
                    if f >= 1 and FINAL[f - 1][1] == 1:
                        finish(finished)
                        finished += 1
                    if f % KT == 3 and f // KT + 1 < N:
                        operand_lo(2 * N + f // KT + 1, range(KT))
                finish(finished)


PHASES = ["setup", "proj", "value", "attn", "output"]


def build(nc, ins, out, phases=PHASES):
    with ExitStack() as ctx:
        k = Kernel(nc, ctx, ins, out)
        with ExitStack() as hctx:
            k.h_hi = hctx.enter_context(nc.sbuf_tensor("h_hi", [P, KT, S], F32R))
            k.h_lo = hctx.enter_context(nc.sbuf_tensor("h_lo", [P, KT, S], F32R))
            k.raw = [hctx.enter_context(nc.sbuf_tensor(f"raw{i}", [P, KT, P], F32)) for i in range(2)]
            if "setup" in phases:
                setup_phase(k)
            if "proj" in phases:
                projection_phase(k)
        with ExitStack() as actx:
            k.ckv_hi = actx.enter_context(nc.sbuf_tensor("ckv_hi", [P, LT, S], F32R))
            k.ckv_lo = actx.enter_context(nc.sbuf_tensor("ckv_lo", [P, LT, S], F32R))
            k.kr_hi2 = actx.enter_context(nc.sbuf_tensor("kr_hi2", [P, S], F32R))
            k.kr_lo = actx.enter_context(nc.sbuf_tensor("kr_lo", [ROPE, S], F32R))
            k.trig = actx.enter_context(nc.sbuf_tensor("trig", [P, S], F32))
            k.qlat = [actx.enter_context(nc.sbuf_tensor(f"qlat{i}", [P, 2, LT, TC], F32R)) for i in range(2)]
            k.head_raw = actx.enter_context(nc.sbuf_tensor("head_raw", [P, LT, 3 * P], F32))
            k.wh = actx.enter_context(nc.sbuf_tensor("head_w_h", [P, LT, 3 * P], F32R))
            k.wl = actx.enter_context(nc.sbuf_tensor("head_w_l", [P, LT, 3 * P], F32R))
            if "value" in phases:
                value_phase(k)
            if "attn" in phases:
                attention_phase(k)
        if "output" in phases:
            output_phase(k)


_INS = ["x", "c", "positions", "w_ada", "b_ada", "norm_w", "w_in", "conv_w", "conv_b", "conv_ln_w", "conv_ln_b",
        "w_conv_out", "q_norm_w", "w_uq", "kv_norm_w", "w_ukv", "w_attn_out", "w_out", "final_norm_w"]


def _freqs():
    import numpy as np

    f = np.float32(10000.0) ** (-np.arange(0, 64, 2, dtype=np.float32) / np.float32(64))
    sign = np.repeat(np.array([1, 1, -1, 1], np.float32), 32)
    return np.ascontiguousarray(np.stack([np.tile(f, 4), sign], axis=1).astype(np.float32))


def kernel(**inputs):
    import numpy as _np
    import concourse.bacc as _bacc
    from concourse import mybir as _mybir
    from concourse.bass_utils import run_bass_kernel_spmd as _run

    nc = _bacc.Bacc("TRN2", target_bir_lowering=False, num_devices=1)
    arrays, ins = {}, {}
    for name in _INS:
        arrays[f"in_{name}_dram"] = _np.ascontiguousarray(inputs[name])
    arrays["in_freqs_dram"] = _freqs()
    for name in _INS + ["freqs"]:
        a = arrays[f"in_{name}_dram"]
        ins[name] = nc.dram_tensor(f"in_{name}_dram", a.shape, _mybir.dt.from_np(a.dtype), kind="ExternalInput").ap()
    out = nc.dram_tensor("out_0_dram", (1, S, D), _mybir.dt.float32, kind="ExternalOutput").ap()
    build(nc, ins, out)
    r = _run(nc, [arrays], core_ids=[0])
    return r.results[0]["out_0_dram"]
```
